# Optimizing a Trainium2 kernel written in Bass

```python
import jax, jax.numpy as jnp
from jax import lax
import numpy as np
import math

D_MODEL = 1024
BATCH = 1
SEQ = 256
DEPTH = 1

MIX_WIDTH = D_MODEL
ATT_HEADS = 8
ATT_HEAD_DIM = 64
ATT_W = ATT_HEADS * ATT_HEAD_DIM
ROPE_DIM = ATT_HEAD_DIM // 4
ROPE_THETA = 500000.0
MOBA_BLOCK = 256
MOBA_TOPK = 3
Q_BLOCK = 64
MLSTM_HEADS = 4
MLSTM_QK_DIM = 64
MLSTM_V_DIM = 128
ML_QK_W = MLSTM_HEADS * MLSTM_QK_DIM
ML_V_W = MLSTM_HEADS * MLSTM_V_DIM
MLSTM_CHUNK = 64
D_FF = 4 * D_MODEL
EPS = 1e-6
IN_SPLITS = (ATT_W, ATT_W, ATT_W, ML_QK_W, ML_QK_W, ML_V_W, ML_V_W, MLSTM_HEADS, MLSTM_HEADS)
IN_WIDTH = 3 * ATT_W + 2 * ML_QK_W + 2 * ML_V_W + 2 * MLSTM_HEADS


def rms_norm(x, g):
    xf = x.astype(jnp.float32)
    y = xf * lax.rsqrt(jnp.mean(xf * xf, axis=-1, keepdims=True) + EPS) * g.astype(jnp.float32)
    return y.astype(x.dtype)

def partial_rope(x, positions):
    inv_freq = ROPE_THETA ** (-jnp.arange(0, ROPE_DIM, 2, dtype=jnp.float32) / ROPE_DIM)
    ang = positions.astype(jnp.float32)[:, None, :, None] * inv_freq
    cos = jnp.cos(jnp.concatenate([ang, ang], axis=-1))
    sin = jnp.sin(jnp.concatenate([ang, ang], axis=-1))
    xr, xp = x[..., :ROPE_DIM], x[..., ROPE_DIM:]
    x1, x2 = xr[..., :ROPE_DIM // 2], xr[..., ROPE_DIM // 2:]
    xr = xr * cos + jnp.concatenate([-x2, x1], axis=-1) * sin
    return jnp.concatenate([xr, xp], axis=-1)

def moba_attention(q, k, v):
    B, H, S, Dh = q.shape
    nb = -(-S // MOBA_BLOCK)
    pad = nb * MOBA_BLOCK - S
    kp = jnp.pad(k, ((0, 0), (0, 0), (0, pad), (0, 0)))
    vp = jnp.pad(v, ((0, 0), (0, 0), (0, pad), (0, 0)))
    kb = kp.reshape(B, H, nb, MOBA_BLOCK, Dh)
    vb = vp.reshape(B, H, nb, MOBA_BLOCK, Dh)
    k_mean = jnp.mean(kb, axis=3)
    n_sel = min(MOBA_TOPK, nb)
    scale = Dh ** -0.5
    blk_ids = jnp.arange(nb)
    gather = jax.vmap(jax.vmap(lambda blocks, ids: blocks[ids]))

    def one_block(c):
        q0 = c * Q_BLOCK
        own = q0 // MOBA_BLOCK
        qc = lax.dynamic_slice_in_dim(q, q0, Q_BLOCK, axis=2)
        qpos = q0 + jnp.arange(Q_BLOCK)
        gate = jnp.einsum('bhqd,bhnd->bhqn', qc, k_mean)
        gate = jnp.where(blk_ids < own, gate, -jnp.inf)
        _, sel = lax.top_k(gate, n_sel)
        valid = sel < own
        k_sel = gather(kb, sel)
        v_sel = gather(vb, sel)
        s_sel = jnp.einsum('bhqd,bhqnkd->bhqnk', qc, k_sel) * scale
        s_sel = jnp.where(valid[..., None], s_sel, -jnp.inf).reshape(B, H, Q_BLOCK, n_sel * MOBA_BLOCK)
        k_own = lax.dynamic_slice_in_dim(kp, own * MOBA_BLOCK, MOBA_BLOCK, axis=2)
        v_own = lax.dynamic_slice_in_dim(vp, own * MOBA_BLOCK, MOBA_BLOCK, axis=2)
        kpos = own * MOBA_BLOCK + jnp.arange(MOBA_BLOCK)
        s_own = jnp.einsum('bhqd,bhkd->bhqk', qc, k_own) * scale
        s_own = jnp.where(kpos[None, :] <= qpos[:, None], s_own, -jnp.inf)
        p = jax.nn.softmax(jnp.concatenate([s_sel, s_own], axis=-1).astype(jnp.float32), axis=-1)
        p_sel = p[..., :n_sel * MOBA_BLOCK].reshape(B, H, Q_BLOCK, n_sel, MOBA_BLOCK)
        p_own = p[..., n_sel * MOBA_BLOCK:]
        return (jnp.einsum('bhqnk,bhqnkd->bhqd', p_sel, v_sel)
                + jnp.einsum('bhqk,bhkd->bhqd', p_own, v_own))

    out = lax.map(one_block, jnp.arange(S // Q_BLOCK))
    return jnp.transpose(out, (1, 2, 0, 3, 4)).reshape(B, H, S, Dh)

def mlstm_chunkwise(q, k, v, ig, lf):
    B, H, S, dk = q.shape
    dv = v.shape[-1]
    L = MLSTM_CHUNK
    nc = S // L

    def chunks(a):
        return jnp.moveaxis(a.reshape((B, H, nc, L) + a.shape[3:]), 2, 0)

    causal = jnp.tril(jnp.ones((L, L), dtype=bool))

    def step(carry, xs):
        C, n, m = carry
        qc, kc, vc, ic, fc = xs
        b = jnp.cumsum(fc, axis=-1)
        d = b[..., :, None] - b[..., None, :] + ic[..., None, :]
        d = jnp.where(causal, d, -jnp.inf)
        m_inter = b + m[..., None]
        m_t = jnp.maximum(m_inter, jnp.max(d, axis=-1))
        s = jnp.einsum('bhtd,bhsd->bhts', qc, kc) * jnp.exp(d - m_t[..., None])
        decay = jnp.exp(m_inter - m_t)
        num = (jnp.einsum('bhts,bhsv->bhtv', s, vc)
               + decay[..., None] * jnp.einsum('bhtd,bhdv->bhtv', qc, C))
        den = jnp.sum(s, axis=-1) + decay * jnp.einsum('bhtd,bhd->bht', qc, n)
        h = num / jnp.maximum(jnp.abs(den), jnp.exp(-m_t))[..., None]
        b_last = b[..., -1]
        g = b_last[..., None] - b + ic
        m_new = jnp.maximum(b_last + m, jnp.max(g, axis=-1))
        carry_decay = jnp.exp(b_last + m - m_new)
        wg = jnp.exp(g - m_new[..., None])
        C_new = carry_decay[..., None, None] * C + jnp.einsum('bhs,bhsd,bhsv->bhdv', wg, kc, vc)
        n_new = carry_decay[..., None] * n + jnp.einsum('bhs,bhsd->bhd', wg, kc)
        return (C_new, n_new, m_new), h

    init = (jnp.zeros((B, H, dk, dv), jnp.float32),
            jnp.zeros((B, H, dk), jnp.float32),
            jnp.zeros((B, H), jnp.float32))
    _, h = lax.scan(step, init, (chunks(q), chunks(k), chunks(v), chunks(ig), chunks(lf)))
    return jnp.moveaxis(h, 0, 2).reshape(B, H, S, dv)

def hybrid_layer(x, positions, g_mix_pre, w_in, b_igate, b_fgate, g_mlstm_out, w_out,
                 g_mix_post, g_mlp_pre, w_up, w_down, g_mlp_post):
    B, S, _ = x.shape
    hdn = rms_norm(x, g_mix_pre)
    proj = hdn @ w_in
    aq, ak, av, mq, mk, mv, mo, mi, mf = jnp.split(proj, [int(c) for c in np.cumsum(IN_SPLITS)[:-1]], axis=-1)

    def to_heads(t, nh):
        return t.reshape(B, S, nh, -1).transpose(0, 2, 1, 3).astype(jnp.float32)

    q_a = partial_rope(to_heads(aq, ATT_HEADS), positions)
    k_a = partial_rope(to_heads(ak, ATT_HEADS), positions)
    v_a = to_heads(av, ATT_HEADS)
    att = moba_attention(q_a, k_a, v_a)
    att = att.transpose(0, 2, 1, 3).reshape(B, S, ATT_W)

    q_m = to_heads(mq, MLSTM_HEADS)
    k_m = to_heads(mk, MLSTM_HEADS) * (MLSTM_QK_DIM ** -0.5)
    v_m = to_heads(mv, MLSTM_HEADS)
    ig = (mi.astype(jnp.float32) + b_igate.astype(jnp.float32)).transpose(0, 2, 1)
    lf = jax.nn.log_sigmoid(mf.astype(jnp.float32) + b_fgate.astype(jnp.float32)).transpose(0, 2, 1)
    hm = mlstm_chunkwise(q_m, k_m, v_m, ig, lf)
    hm = hm * lax.rsqrt(jnp.mean(hm * hm, axis=-1, keepdims=True) + EPS)
    hm = hm.transpose(0, 2, 1, 3).reshape(B, S, ML_V_W) * g_mlstm_out.astype(jnp.float32)
    hm = hm * jax.nn.sigmoid(mo.astype(jnp.float32))

    mixed = jnp.concatenate([att, hm], axis=-1).astype(x.dtype)
    x = x + rms_norm(mixed @ w_out, g_mix_post)

    u = rms_norm(x, g_mlp_pre) @ w_up
    u = jnp.square(jax.nn.relu(u))
    x = x + rms_norm(u @ w_down, g_mlp_post)
    return x

def first_inputs(seed: int = 0) -> dict:
    key = jax.random.key(seed)
    ks = jax.random.split(key, 14)
    f32 = jnp.float32

    def gain(k, n):
        return 1.0 + 0.02 * jax.random.normal(k, (DEPTH, n), f32)

    x = jax.random.normal(ks[0], (BATCH, SEQ, D_MODEL), f32)
    positions = jnp.broadcast_to(jnp.arange(SEQ, dtype=jnp.int32), (BATCH, SEQ))
    g_mix_pre = gain(ks[1], D_MODEL)
    w_in = jax.random.normal(ks[2], (DEPTH, D_MODEL, IN_WIDTH), f32) * D_MODEL ** -0.5
    b_igate = 0.1 * jax.random.normal(ks[3], (DEPTH, MLSTM_HEADS), f32)
    b_fgate = (jnp.linspace(3.0, 6.0, MLSTM_HEADS, dtype=f32)[None, :]
               + 0.1 * jax.random.normal(ks[4], (DEPTH, MLSTM_HEADS), f32))
    g_mlstm_out = gain(ks[5], ML_V_W)
    w_out = jax.random.normal(ks[6], (DEPTH, MIX_WIDTH, D_MODEL), f32) * MIX_WIDTH ** -0.5
    g_mix_post = gain(ks[7], D_MODEL)
    g_mlp_pre = gain(ks[8], D_MODEL)
    w_up = jax.random.normal(ks[9], (DEPTH, D_MODEL, D_FF), f32) * D_MODEL ** -0.5
    w_down = jax.random.normal(ks[10], (DEPTH, D_FF, D_MODEL), f32) * D_FF ** -0.5
    g_mlp_post = gain(ks[11], D_MODEL)
    return {"x": x, "positions": positions, "g_mix_pre": g_mix_pre, "w_in": w_in,
            "b_igate": b_igate, "b_fgate": b_fgate, "g_mlstm_out": g_mlstm_out, "w_out": w_out,
            "g_mix_post": g_mix_post, "g_mlp_pre": g_mlp_pre, "w_up": w_up, "w_down": w_down,
            "g_mlp_post": g_mlp_post}

def first_block(x, positions, g_mix_pre, w_in, b_igate, b_fgate, g_mlstm_out, w_out,
              g_mix_post, g_mlp_pre, w_up, w_down, g_mlp_post):
    for layer in range(DEPTH):
        x = hybrid_layer(x, positions, g_mix_pre[layer], w_in[layer], b_igate[layer], b_fgate[layer],
                         g_mlstm_out[layer], w_out[layer], g_mix_post[layer], g_mlp_pre[layer],
                         w_up[layer], w_down[layer], g_mlp_post[layer])
    return x


DEPTH_2 = 2

ATTN_HEADS = 4
HEAD_DIM = 64
ATTN_W = ATTN_HEADS * 2 * HEAD_DIM
ROT_DIM = HEAD_DIM // 4
Q_BLOCK_2 = 128
CONV_W = 512
CONV_K = 31
D_FF_2 = ((int(math.ceil(8 * D_MODEL / 3)) + 255) // 256) * 256
N_BRANCH = 2
Q_OFF = 0
K_OFF = Q_OFF + ATTN_W
V_OFF = K_OFF + ATTN_W
C_OFF = V_OFF + ATTN_W
G_OFF = C_OFF + 2 * CONV_W
N_IN = G_OFF + N_BRANCH * D_MODEL
N_MOD = 6


def rms_norm_2(x, g, eps=1e-6):
    xf = x.astype(jnp.float32)
    y = xf * lax.rsqrt(jnp.mean(xf * xf, axis=-1, keepdims=True) + eps)
    return (y * g.astype(jnp.float32)).astype(x.dtype)

def layer_norm(x, g, b, eps=1e-5):
    xf = x.astype(jnp.float32)
    mu = jnp.mean(xf, axis=-1, keepdims=True)
    var = jnp.mean(jnp.square(xf - mu), axis=-1, keepdims=True)
    y = (xf - mu) * lax.rsqrt(var + eps)
    return (y * g.astype(jnp.float32) + b.astype(jnp.float32)).astype(x.dtype)

def partial_rope_2(t, cos, sin):
    half = ROT_DIM // 2
    x1 = t[..., :half]
    x2 = t[..., half:ROT_DIM]
    rot = jnp.concatenate([x1 * cos - x2 * sin, x2 * cos + x1 * sin], axis=-1)
    return jnp.concatenate([rot, t[..., ROT_DIM:]], axis=-1)

def diff_attention(q, k, v, lam):
    b, s, h, _, d = q.shape
    scale = 1.0 / math.sqrt(d)
    qt = q.transpose(0, 2, 3, 1, 4)
    kt = k.transpose(0, 2, 3, 1, 4)
    vt = v.transpose(0, 2, 1, 3)
    k_pos = jnp.arange(s)
    neg = jnp.finfo(jnp.float32).min

    def block(i):
        start = i * Q_BLOCK_2
        qb = lax.dynamic_slice_in_dim(qt, start, Q_BLOCK_2, axis=3)
        sc = jnp.einsum('bhcqd,bhckd->bhcqk', qb, kt).astype(jnp.float32) * scale
        q_pos = start + jnp.arange(Q_BLOCK_2)
        mask = q_pos[:, None] >= k_pos[None, :]
        sc = jnp.where(mask, sc, neg)
        p = jax.nn.softmax(sc, axis=-1)
        a = p[:, :, 0] - lam * p[:, :, 1]
        return jnp.einsum('bhqk,bhkv->bhqv', a.astype(vt.dtype), vt)

    out = lax.map(block, jnp.arange(s // Q_BLOCK_2))
    out = out.transpose(1, 0, 3, 2, 4)
    return out.reshape(b, s, h, 2 * d)

def causal_depthwise_conv(u, w, bias):
    y = lax.conv_general_dilated(
        u, w.astype(u.dtype), window_strides=(1,), padding=[(CONV_K - 1, 0)],
        dimension_numbers=('NWC', 'WIO', 'NWC'), feature_group_count=u.shape[-1])
    return y + bias

def second_inputs(seed: int = 0) -> dict:
    key = jax.random.key(seed)
    ks = jax.random.split(key, 24)
    f32 = jnp.float32

    def nrm(k, shape, s):
        return jax.random.normal(k, shape, f32) * s

    L = DEPTH_2
    return {
        "x": nrm(ks[0], (BATCH, SEQ, D_MODEL), 1.0),
        "c": nrm(ks[1], (BATCH, D_MODEL), 1.0),
        "positions": jnp.broadcast_to(jnp.arange(SEQ, dtype=jnp.int32)[None, :], (BATCH, SEQ)),
        "ada_w": nrm(ks[2], (L, D_MODEL, N_MOD * D_MODEL), 0.1 * D_MODEL ** -0.5),
        "ada_b": nrm(ks[3], (L, N_MOD * D_MODEL), 0.01),
        "norm1_g": 1.0 + nrm(ks[4], (L, D_MODEL), 0.01),
        "w_in": nrm(ks[5], (L, D_MODEL, N_IN), D_MODEL ** -0.5),
        "lambda_q1": nrm(ks[6], (L, HEAD_DIM), 0.1),
        "lambda_k1": nrm(ks[7], (L, HEAD_DIM), 0.1),
        "lambda_q2": nrm(ks[8], (L, HEAD_DIM), 0.1),
        "lambda_k2": nrm(ks[9], (L, HEAD_DIM), 0.1),
        "subln_g": 1.0 + nrm(ks[10], (L, 2 * HEAD_DIM), 0.01),
        "w_attn_o": nrm(ks[11], (L, ATTN_W, D_MODEL), ATTN_W ** -0.5),
        "dw_conv_w": nrm(ks[12], (L, CONV_K, 1, CONV_W), CONV_K ** -0.5),
        "dw_conv_b": nrm(ks[13], (L, CONV_W), 0.01),
        "conv_ln_g": 1.0 + nrm(ks[14], (L, CONV_W), 0.01),
        "conv_ln_b": nrm(ks[15], (L, CONV_W), 0.01),
        "w_conv_o": nrm(ks[16], (L, CONV_W, D_MODEL), CONV_W ** -0.5),
        "w_out": nrm(ks[17], (L, D_MODEL, D_MODEL), D_MODEL ** -0.5),
        "norm2_g": 1.0 + nrm(ks[18], (L, D_MODEL), 0.01),
        "w_ffn_in": nrm(ks[19], (L, D_MODEL, 2 * D_FF_2), D_MODEL ** -0.5),
        "w_ffn_out": nrm(ks[20], (L, D_FF_2, D_MODEL), D_FF_2 ** -0.5),
        "final_g": 1.0 + nrm(ks[21], (D_MODEL,), 0.01),
    }

def second_block(x, c, positions, ada_w, ada_b, norm1_g, w_in, lambda_q1, lambda_k1,
              lambda_q2, lambda_k2, subln_g, w_attn_o, dw_conv_w, dw_conv_b,
              conv_ln_g, conv_ln_b, w_conv_o, w_out, norm2_g, w_ffn_in, w_ffn_out,
              final_g):
    b, s, _ = x.shape
    inv_freq = 1.0 / (ROPE_THETA ** (jnp.arange(0, ROT_DIM, 2, dtype=jnp.float32) / ROT_DIM))
    ang = positions.astype(jnp.float32)[..., None] * inv_freq
    cos = jnp.cos(ang)[:, :, None, None, :].astype(x.dtype)
    sin = jnp.sin(ang)[:, :, None, None, :].astype(x.dtype)
    c_act = jax.nn.silu(c)

    for l in range(DEPTH_2):
        mod = c_act @ ada_w[l] + ada_b[l]
        shift1, scale1, gate1, shift2, scale2, gate2 = [
            m[:, None, :] for m in jnp.split(mod, N_MOD, axis=-1)]

        h = rms_norm_2(x, norm1_g[l]) * (1.0 + scale1) + shift1
        z = h @ w_in[l]

        q = z[..., Q_OFF:K_OFF].reshape(b, s, ATTN_HEADS, 2, HEAD_DIM)
        k = z[..., K_OFF:V_OFF].reshape(b, s, ATTN_HEADS, 2, HEAD_DIM)
        v = z[..., V_OFF:C_OFF].reshape(b, s, ATTN_HEADS, 2 * HEAD_DIM)
        q = partial_rope_2(q, cos, sin)
        k = partial_rope_2(k, cos, sin)
        lambda_init = 0.8 - 0.6 * math.exp(-0.3 * l)
        lam = (jnp.exp(jnp.sum(lambda_q1[l].astype(jnp.float32) * lambda_k1[l].astype(jnp.float32)))
               - jnp.exp(jnp.sum(lambda_q2[l].astype(jnp.float32) * lambda_k2[l].astype(jnp.float32)))
               + lambda_init)
        o = diff_attention(q, k, v, lam)
        o = rms_norm_2(o, subln_g[l], eps=1e-5) * (1.0 - lambda_init)
        y_attn = o.reshape(b, s, ATTN_W) @ w_attn_o[l]

        ga, gb = jnp.split(z[..., C_OFF:G_OFF], 2, axis=-1)
        u = ga * jax.nn.sigmoid(gb)
        u = causal_depthwise_conv(u, dw_conv_w[l], dw_conv_b[l])
        u = jax.nn.silu(layer_norm(u, conv_ln_g[l], conv_ln_b[l]))
        y_conv = u @ w_conv_o[l]

        g_attn, g_conv = jnp.split(jax.nn.sigmoid(z[..., G_OFF:]), N_BRANCH, axis=-1)
        mixed = (g_attn * y_attn + g_conv * y_conv) @ w_out[l]
        x = x + (1.0 + gate1) * mixed

        h2 = rms_norm_2(x, norm2_g[l]) * (1.0 + scale2) + shift2
        f_gate, f_up = jnp.split(h2 @ w_ffn_in[l], 2, axis=-1)
        x = x + (1.0 + gate2) * ((jax.nn.silu(f_gate) * f_up) @ w_ffn_out[l])

    return rms_norm_2(x, final_g)


def setup_inputs(seed=0):
    out = dict(first_inputs(seed))
    for name, value in second_inputs(seed + 1).items():
        if name != "x":
            out[name + "_2"] = value
    return out


def reference(
    x, positions, g_mix_pre, w_in, b_igate, b_fgate, g_mlstm_out, w_out, g_mix_post, g_mlp_pre,
    w_up, w_down, g_mlp_post, c_2, positions_2, ada_w_2, ada_b_2, norm1_g_2, w_in_2,
    lambda_q1_2, lambda_k1_2, lambda_q2_2, lambda_k2_2, subln_g_2, w_attn_o_2, dw_conv_w_2,
    dw_conv_b_2, conv_ln_g_2, conv_ln_b_2, w_conv_o_2, w_out_2, norm2_g_2, w_ffn_in_2,
    w_ffn_out_2, final_g_2,
):
    x = first_block(
        x, positions, g_mix_pre, w_in, b_igate, b_fgate, g_mlstm_out, w_out, g_mix_post,
        g_mlp_pre, w_up, w_down, g_mlp_post,
    )
    return second_block(
        x, c_2, positions_2, ada_w_2, ada_b_2, norm1_g_2, w_in_2, lambda_q1_2, lambda_k1_2,
        lambda_q2_2, lambda_k2_2, subln_g_2, w_attn_o_2, dw_conv_w_2, dw_conv_b_2, conv_ln_g_2,
        conv_ln_b_2, w_conv_o_2, w_out_2, norm2_g_2, w_ffn_in_2, w_ffn_out_2, final_g_2,
    )


_drawn_inputs = setup_inputs


def setup_inputs(seed=0):
    import zlib

    import numpy as np

    out = dict(_drawn_inputs(seed))
    spreads = {}
    factors = {'b_igate': 28.357,
     'g_mlstm_out': 3.505,
     'g_mix_post': 3.405,
     'g_mlp_pre': 4.018,
     'g_mlp_post': 4.231,
     'ada_b_2': 3.423,
     'norm1_g_2': 8.0,
     'lambda_q1_2': 6.925,
     'lambda_k1_2': 5.012,
     'subln_g_2': 38.71,
     'dw_conv_b_2': 25.402,
     'conv_ln_g_2': 45.947,
     'conv_ln_b_2': 43.769,
     'norm2_g_2': 8.0,
     'final_g_2': 32.152,
     'lambda_q2_2': 2.698}
    for name, (base, spread) in spreads.items():
        noise = np.random.default_rng([zlib.crc32(name.encode()), seed]).standard_normal(out[name].shape)
        drawn = base * np.exp(spread * noise) if base else spread * noise
        out[name] = __import__('jax').numpy.asarray(drawn.astype(out[name].dtype))
    for name, factor in factors.items():
        out[name] = (out[name] * factor).astype(out[name].dtype)
    return out
```

```python
from contextlib import ExitStack

import numpy as np

import concourse.bass as bass
from concourse import mybir

F32 = mybir.dt.float32
F32R = mybir.dt.float32r
I32 = mybir.dt.int32
ALU = mybir.AluOpType
ACT = mybir.ActivationFunctionType
AX = mybir.AxisListType

P = 128
S = 256
TT = S // P
D = 1024
KD = D // P
GF = 512
GT = GF // P
CK = 4
RING = 3
LEAD = 2
EPS = 1e-6
EPS_SUB = 1e-5
QK = 64
SCALE = QK ** -0.5
UNITS = 8
TAPS = 31
MH = 4
LAYERS = 2
MODS = 48
ADA_GROUPS = MODS // GT
ADA_K = 2
ADA_RING = 3
LAMBDA_INIT = [0.8 - 0.6 * float(np.exp(-0.3 * l)) for l in range(LAYERS)]
MAGIC = 1.5 * 2.0 ** 23
TWO_PI = (6.28125, 0.0019350051879882812, 3.0199157663446332e-07)
PI = float(np.float32(np.pi))
BEFORE_PI = 3.1415925

C_ID, C_ROT, C_ONE = 0, P, 2 * P
C_ADD, C_MUL, C_FREQ = 3 * P, 6 * P, 9 * P
C_ALL = 9 * P + 1


def constants():
    c = np.zeros((P, C_ALL), np.float32)
    i = np.arange(P)
    c[:, C_ID:C_ID + P] = np.eye(P)
    half = QK // 8
    freq = 500000.0 ** (-np.arange(0, 2 * half, 2, dtype=np.float32) / np.float32(2 * half))
    for p in range(P):
        d = p % QK
        if d < half:
            c[p + half, C_ROT + p] = -1.0
        elif d < 2 * half:
            c[p - half, C_ROT + p] = 1.0
        if d < 2 * half:
            c[p, C_FREQ] = freq[d % half]
    c[:, C_ONE:C_ONE + P] = 1.0
    tri = np.where(i[None, :] <= i[:, None], 0.0, -1e30)
    c[:, C_ADD:C_ADD + P] = tri
    c[:, C_ADD + 2 * P:C_ADD + 3 * P] = tri
    up = (i[:, None] <= i[None, :]).astype(np.float32)
    c[:, C_MUL:C_MUL + P] = up
    c[:, C_MUL + P:C_MUL + 2 * P] = 1.0
    c[:, C_MUL + 2 * P:C_MUL + 3 * P] = up
    return c


class Tally:

    def __init__(self):
        self.n = {}

    def __call__(self, name, by=1):
        self.n[name] = self.n.get(name, 0) + by
        return self.n[name]

    def seen(self, name):
        return self.n.get(name, 0)


class Own:

    def __init__(self, eng, sem, steps):
        self.eng, self.sem, self.steps, self.n, self.last = eng, sem, steps, Tally(), None

    def __call__(self, ins, name=None, value=None):
        name = name or self.steps
        ins.then_inc(self.sem(name), 1)
        self.last = name, value or self.n(name)
        return self.last[1]

    def settle(self):
        self.eng.wait_ge(self.sem(self.last[0]), self.last[1])


def plan(t):
    chunks, groups = [], {}

    def group(name, w, cols, tiles, first=0):
        ids = []
        for k in range(0, tiles, CK):
            nk = min(CK, tiles - k)
            rows = w[k * P:(k + nk) * P, :]
            parts, at = [], 0
            for lo, n in cols:
                parts.append((at, n, rows[:, lo:lo + n].rearrange("(k p) f -> p k f", p=P)))
                at += n
            ids.append(len(chunks))
            chunks.append((nk, parts))
        groups[name] = (len(groups), ids)

    w = t["w_in"][0]
    for n in range(6):
        group(("in", n), w, [(n * GF, GF)], KD)
    for n in range(2):
        group(("out", n), t["w_out"][0], [(n * GF, GF)], KD)
    for n in range(8):
        group(("up", n), t["w_up"][0], [(n * GF, GF)], KD)
    for n in range(2):
        group(("down", n), t["w_down"][0], [(n * GF, GF)], 32)
    for l in range(LAYERS):
        w = t["w_in_2"][l]
        for n in (3, 4, 0, 1, 2, 5, 6, 7, 8):
            group((l, "in", n), w, [(n * GF, GF)], KD)
        for n in range(2):
            group((l, "attn", n), t["w_attn_o_2"][l], [(n * GF, GF)], 4)
            group((l, "conv", n), t["w_conv_o_2"][l], [(n * GF, GF)], 4)
        for n in range(2):
            group((l, "out", n), t["w_out_2"][l], [(n * GF, GF)], KD)
        for n in range(11):
            group((l, "ffn", n), t["w_ffn_in_2"][l], [(n * 256, 256), (2816 + n * 256, 256)], KD)
        for n in range(2):
            group((l, "down", n), t["w_ffn_out_2"][l], [(n * GF, GF)], 22)
    return chunks, groups


def two_blocks(nc, t, consts, out):
    chunks, groups = plan(t)
    NCH = len(chunks)

    first = {name: ids[0] for name, (_, ids) in groups.items()}
    at0 = [first[("in", 2)] + 1, first[("out", 0)] + 1, first[("out", 1)] + 1] + [first[("up", 1)] + 1 + 3 * i for i in range(5)]
    at0 += [first[("down", 0)] + i for i in (2, 5, 9, 13)]
    b = first[(0, "attn", 0)]
    at1 = [b + i for i in (3, 6, 9, 12, 16, 19, 22, 26, 29, 33, 36, 39)]
    ada_at = {c: (l, q) for l, at in enumerate((at0, at1)) for q, c in enumerate(at)}
    ada_work = {}
    for c, (l, q) in ada_at.items():
        for k in range(KD):
            ada_work.setdefault(c - 3 + 3 * k // KD, []).append((l * ADA_GROUPS + q, k))

    by_pool = set()
    for l in range(LAYERS):
        by_pool |= set(range(first[(l, "in", 0)], first[(l, "attn", 0)]))
    by_pool |= set(range(first[(1, "ffn", 0)], NCH, 2))
    low_done, made = [], {"lo_done_v": 0, "lo_done_p": 0}
    for c in range(NCH):
        name = "lo_done_p" if c in by_pool else "lo_done_v"
        made[name] += 1
        low_done.append((name, made[name]))

    pack, srcs = {}, [
        ("g_mix_pre", t["g_mix_pre"][0], KD), ("g_mlstm", t["g_mlstm_out"][0], MH), ("g_mix_post", t["g_mix_post"][0], KD),
        ("g_mlp_pre", t["g_mlp_pre"][0], KD), ("g_mlp_post", t["g_mlp_post"][0], KD), ("c", t["c_2"][0], KD),
        ("final", t["final_g_2"], KD)]
    for l in range(LAYERS):
        srcs += [(("norm1", l), t["norm1_g_2"][l], KD), (("norm2", l), t["norm2_g_2"][l], KD), (("subln", l), t["subln_g_2"][l], 1),
                 (("convb", l), t["dw_conv_b_2"][l], GT), (("lng", l), t["conv_ln_g_2"][l], GT), (("lnb", l), t["conv_ln_b_2"][l], GT)]
    NROW = 0
    for name, ap, tiles in srcs:
        pack[name] = (NROW, ap, tiles)
        NROW += tiles
    PARAM_DMAS = len(srcs) + 2
    NMOD = LAYERS * MODS

    landed, count = [], [0] * RING
    for c, (nk, parts) in enumerate(chunks):
        count[c % RING] += 16 * len(parts)
        landed.append(count[c % RING])

    with ExitStack() as ctx:
        def sb(name, shape, dt=F32, on=ctx):
            return on.enter_context(nc.sbuf_tensor(name, shape, dt))

        def ps(name, shape):
            return ctx.enter_context(nc.psum_tensor(name, shape, F32))

        sems = {}

        def sem(name):
            if name not in sems:
                sems[name] = nc.alloc_semaphore(name)
            return sems[name]

        mm = ps("mm", [P, 4, GF])
        pa = ps("pa", [P, GF])
        pv = [ps(f"pv{i}", [P, GF]) for i in range(3)]

        raw = sb("raw", [P, RING, CK, GF])
        hi = sb("hi", [P, RING, CK, GF], F32R)
        lo = sb("lo", [P, RING, CK, GF], F32R)
        ada_raw = sb("ada_raw", [P, ADA_RING, ADA_K, GF])
        ada_acc = sb("ada_acc", [P, 2, GF])
        cst = sb("cst", [P, C_ALL])
        x = sb("x", [P, KD, S])
        act_hi = sb("act_hi", [P, KD, S], F32R)
        act_lo = sb("act_lo", [P, KD, S], F32R)
        hf = sb("hf", [P, 4, S])
        sq = sb("sq", [P, KD, S])
        rstd = sb("rstd", [P, 2, S])
        tabs = sb("tabs", [P, 2, 2 * S])
        parT = sb("parT", [P, NROW])
        adabT = sb("adabT", [P, NMOD])
        modT = sb("modT", [P, NMOD])
        convw = sb("convw", [P, LAYERS * GT, TAPS])
        ca = sb("ca", [P, 2, KD])
        cols = sb("cols", [P, 40])
        small = sb("small", [P, 24])
        nlam = sb("nlam", [P, LAYERS])

        mixA = ExitStack()
        qk1 = sb("qk1", [P, KD, S], on=mixA)
        v1 = sb("v1", [P, TT, GF], on=mixA)
        mqk = sb("mqk", [P, 4, S], on=mixA)
        mv = sb("mv", [P, TT, GF], on=mixA)
        mo = sb("mo", [P, 4, S], on=mixA)
        wg = sb("wg", [P, KD, 8], on=mixA)
        att = ExitStack()
        att_hi = sb("att_hi", [P, 4, S], F32R, on=att)
        att_lo = sb("att_lo", [P, 4, S], F32R, on=att)
        att.close()
        hng = sb("hng", [P, KD, S], on=mixA)
        gbias = sb("gbias", [4, 2], on=mixA)
        gate = sb("gate", [4, 8, S], on=mixA)
        acol = sb("acol", [P, TT, 4], on=mixA)
        sA = sb("sA", [P, 2, 3 * P], on=mixA)
        pA = sb("pA", [P, 2, 3 * P], on=mixA)
        ptA = sb("ptA", [P, 2, 3 * P], on=mixA)
        bcA = sb("bcA", [P, 2, 2 * S], on=mixA)
        emA = sb("emA", [P, 2, S], on=mixA)
        hmA = sb("hmA", [P, 2, S], on=mixA)
        rows = sb("rows", [P, P], on=mixA)
        adab = sb("adab", [P, P], on=mixA)
        cwr = sb("cwr", [P, LAYERS, GF], on=mixA)
        lamr = sb("lamr", [1, LAYERS * 2, 2, QK], on=mixA)
        lamp = sb("lamp", [1, LAYERS * 2, QK], on=mixA)
        lams = sb("lams", [1, 16], on=mixA)
        posi = sb("posi", [1, 2 * S], I32, on=mixA)
        posf = sb("posf", [1, 2 * S], on=mixA)
        mixA.close()
        mixB = ExitStack()
        qk2 = sb("qk2", [P, KD, S], on=mixB)
        v2 = sb("v2", [P, TT, GF], on=mixB)
        gates = sb("gates", [P, 16, S], on=mixB)
        cu = sb("cu", [P, GT, S + TAPS - 1], on=mixB)
        cacc = sb("cacc", [P, GT, S], on=mixB)
        csq = sb("csq", [P, GT, S], on=mixB)
        o_hi = sb("o_hi", [P, GT, S], F32R, on=mixB)
        o_lo = sb("o_lo", [P, GT, S], F32R, on=mixB)
        uc_hi = sb("uc_hi", [P, GT, S], F32R, on=mixB)
        uc_lo = sb("uc_lo", [P, GT, S], F32R, on=mixB)
        sB = sb("sB", [P, 2, 3 * P], on=mixB)
        pB = sb("pB", [P, 2, 3 * P], on=mixB)
        ptB = sb("ptB", [P, 3 * P], on=mixB)
        oB = sb("oB", [P, S], on=mixB)
        mixB.close()
        last = ExitStack()
        outf = sb("outf", [P, KD, S], on=last)
        outt = sb("outt", [P, TT, D], on=last)
        last.close()
        u_hi = sb("u_hi", [P, 32, S], F32R)
        u_lo = sb("u_lo", [P, 32, S], F32R)

        ident = cst[:, C_ID:C_ID + P]
        rot = cst[:, C_ROT:C_ROT + P]
        ones = cst[:, C_ONE:C_ONE + P]

        def pcols(name):
            at, _, tiles = pack[name]
            return parT[:, at:at + tiles]

        def banks(name):
            g = groups[name][0]
            return mm[:, 2 * (g % 2):2 * (g % 2) + 2, :]

        def tile_of(src, f):
            return src[:, f // 2, (f % 2) * S:(f % 2) * S + S]

        def freed(name):
            g = groups[name][0]
            return f"group_free{g % 2}", g // 2 + 1

        todoA = [(("in", g), j) for g in (3, 4, 5) for j in range(2)]

        def todoB(l):
            return [((l, "in", g), j) for g in (5, 6, 7, 8) for j in range(2)]

        block = ctx.enter_context(nc.Block())

        @block.sync
        def _(sp):
            xin = sq[:].rearrange("p k s -> p (k s)").rearrange("p (t d) -> p t d", t=TT)
            for tt in range(TT):
                sp.dma_start(xin[:, tt, :], t["x"][0, tt * P:tt * P + P, :]).then_inc(sem("x_loaded"), 16)
            sp.dma_start(cst[:], consts).then_inc(sem("const_loaded"), 16)
            for c, (nk, parts) in enumerate(chunks):
                if c >= RING:
                    name, value = low_done[c - RING]
                    sp.wait_ge(sem(name), value)
                for at, w, src in parts:
                    sp.dma_start(raw[:, c % RING, 0:nk, at:at + w], src).then_inc(sem(f"raw_loaded{c % RING}"), 16)
            for i in range(4):
                sp.wait_ge(sem("out_ready"), i + 1)
                kh, tt = i // TT, i % TT
                f = slice(kh * GF, kh * GF + GF)
                sp.dma_start(out[0, tt * P:tt * P + P, f], outt[:, tt, f]).then_inc(sem("stored"), 16)
            sp.wait_ge(sem("stored"), 64)

        @block.tensor
        def _(pe):
            n = Tally()

            def bank(i):
                used = n.seen(f"bank{i}")
                n(f"bank{i}")
                if used:
                    pe.wait_ge(sem(f"bank{i}_free"), used)
                return pa if i == "a" else pv[i]

            def full(ins, i):
                ins.then_inc(sem(f"bank{i}_full"), 1)

            def wait(name, by=1):
                pe.wait_ge(sem(name), n(name, by))

            def chunk(name, j, a_hi, a_lo, token_major=False, ready=None, per=1):
                g, ids = groups[name]
                c = ids[j]
                nk = chunks[c][0]
                if j == 0 and g >= 2:
                    pe.wait_ge(sem(f"group_free{g % 2}"), g // 2)
                pe.wait_ge(sem(low_done[c][0]), low_done[c][1])
                w_hi, w_lo = hi[:, c % RING], lo[:, c % RING]
                b0 = 2 * (g % 2)
                for kk in range(nk):
                    k = CK * j + kk
                    if ready and k % per == 0:
                        wait(ready)
                    ends = j == len(ids) - 1 and kk == nk - 1
                    if token_major:
                        for tt in range(TT):
                            tok = slice(tt * P, tt * P + P)
                            for i, (a, w) in enumerate(((a_hi, w_hi), (a_lo, w_hi), (a_hi, w_lo))):
                                ins = pe.matmul(mm[:, b0 + tt, :], a[:, k, tok], w[:, kk, :], start=(k == 0 and i == 0),
                                                stop=(ends and i == 2), skip_group_check=True)
                    else:
                        for f in range(GT):
                            o = mm[:, b0 + f // 2, (f % 2) * S:(f % 2) * S + S]
                            fs = slice(f * P, f * P + P)
                            for i, (w, a) in enumerate(((w_hi, a_hi), (w_hi, a_lo), (w_lo, a_hi))):
                                ins = pe.matmul(o, w[:, kk, fs], a[:, k, :], start=(k == 0 and i == 0 and f % 2 == 0),
                                                stop=(ends and i == 2), skip_group_check=True)
                ins.then_inc(sem("mm_done"), 1)
                if c in ada_at:
                    wait("ada_ready")
                    i = n.seen("ada_ready") - 1
                    full(pe.matmul(bank(2)[:], ones, ada_acc[:, i % 2, :], start=True, stop=True), 2)

            def product(name, a_hi, a_lo, **kw):
                for j in range(len(groups[name][1])):
                    chunk(name, j, a_hi, a_lo, **kw)

            def sum_squares(half):
                if half == 0:
                    bank("a")
                wait("sq_ready")
                for k in range(4 * half, 4 * half + 4):
                    ins = pe.matmul(pa[:, 0:S], ones, sq[:, k, :], start=(k == 0), stop=(k == KD - 1))
                if half:
                    full(ins, "a")

            def rope(qk):
                for name in ("q", "k"):
                    for j in range(2):
                        i = 2 * j
                        k = (0 if name == "q" else 4) + 2 * j
                        full(pe.matmul(bank(i)[:], rot, qk[:, k:k + 2, :], start=True, stop=True), i)

            def scores(qk, u):
                b = bank(0)
                r = slice(QK * (u % 2), QK * (u % 2) + QK)
                q, k = qk[r, u // 2, :], qk[r, 4 + u // 2, :]
                pe.matmul(b[:, 0:P], q[:, 0:P], k[:, 0:P], start=True, stop=True)
                full(pe.matmul(b[:, P:3 * P], q[:, P:S], k, start=True, stop=True), 0)

            turned = []

            def turn(p):
                wait("probs_ready")
                b = bank(1)
                turned.append(n.seen("bank1"))
                for i in range(3):
                    ins = pe.transpose(b[:, i * P:(i + 1) * P], p[:, i * P:(i + 1) * P], ident)
                full(ins, 1)

            def apply_v(pt, v, f0, width, r0, last):
                pe.wait_ge(sem("bank1_free"), turned.pop(0))
                b = bank(2) if r0 == 0 else pv[2]
                o = b[r0:r0 + width, :]
                pe.matmul(o[:, 0:S], v[:, 0, f0:f0 + width], pt[:, 0:S], start=True, stop=False, skip_group_check=True)
                ins = pe.matmul(o[:, P:S], v[:, 1, f0:f0 + width], pt[:, S:3 * P], start=False, stop=True, skip_group_check=True)
                if last:
                    full(ins, 2)

            def head_squares():
                wait("hsq_ready")
                full(pe.matmul(bank("a")[:, 0:S], ones, sq[:, 0, :], start=True, stop=True), "a")

            pe.wait_ge(sem("const_loaded"), 16)
            pe.wait_ge(sem("x_loaded"), 16 * TT)
            xin = sq[:].rearrange("p k s -> p (k s)").rearrange("p (t d) -> p t d", t=TT)
            for j in range(4):
                i = 2 * (j % 2)
                b = bank(i)
                for a, k in enumerate((2 * j, 2 * j + 1)):
                    for tt in range(TT):
                        ins = pe.transpose(b[:, a * S + tt * P:a * S + tt * P + P], xin[:, tt, k * P:(k + 1) * P], ident)
                full(ins, i)
            pe.wait_ge(sem("params_loaded"), 16 * PARAM_DMAS)
            b = bank(0)
            pe.transpose(b[:, 0:NROW], rows[0:NROW, :], ident[0:NROW, 0:NROW])
            full(pe.transpose(b[:, P:P + NMOD], adab[0:NMOD, :], ident[0:NMOD, 0:NMOD]), 0)
            b = bank(2)
            for i in range(LAYERS * GT):
                ins = pe.transpose(b[:, 32 * i:32 * i + TAPS], cwr[0:TAPS, i // GT, (i % GT) * P:(i % GT + 1) * P], ident[0:TAPS, 0:TAPS])
            full(ins, 2)
            sum_squares(0)
            sum_squares(1)
            wait("positions_ready")
            full(pe.matmul(bank(0)[:], ones[0:1, :], posf[0:1, :], start=True, stop=True), 0)
            wait("lam_ready")
            full(pe.matmul(bank(2)[:, 0:LAYERS], ones[0:1, :], lams[0:1, 8:8 + LAYERS], start=True, stop=True), 2)

            product(("in", 0), act_hi, act_lo, ready="act_ready")
            product(("in", 1), act_hi, act_lo)
            product(("in", 2), act_hi, act_lo, token_major=True)
            pe.wait_ge(sem(freed(("in", 0))[0]), freed(("in", 0))[1])
            pe.wait_ge(sem(freed(("in", 1))[0]), freed(("in", 1))[1])
            rope(qk1)
            pe.wait_ge(sem("gate_weights_loaded"), 48)
            b = bank(2)
            for half in range(2):
                for k in range(KD):
                    ins = pe.matmul(b[0:4, half * S:half * S + S], wg[:, k, 4 * half:4 * half + 4], hng[:, k, :],
                                    start=(k == 0 and half == 0), stop=(k == KD - 1), skip_group_check=True)
            full(ins, 2)
            wait("rope_done", 4)
            pe.wait_ge(sem(freed(("in", 2))[0]), freed(("in", 2))[1])
            scores(qk1, 0)
            for i in range(UNITS + 1):
                if i < len(todoA):
                    name, j = todoA[i]
                    chunk(name, j, act_hi, act_lo, token_major=(name == ("in", 4)))
                if i + 1 < UNITS:
                    scores(qk1, i + 1)
                if i < UNITS:
                    turn(pA[:, i % 2, :])
                u = i - 1
                if u >= 0:
                    apply_v(ptA[:, u % 2, :], v1, u * QK, QK, QK * (u % 2), u % 2 == 1)

            wait("gate_rows_ready")
            b = bank(0)
            for tt in range(TT):
                ins = pe.transpose(b[:, 4 * tt:4 * tt + 4], gate[:, 5, tt * P:tt * P + P], ident[0:4, 0:4])
            full(ins, 0)
            for g in (3, 4, 5):
                pe.wait_ge(sem(freed(("in", g))[0]), freed(("in", g))[1])

            def m_scores(h):
                full(pe.matmul(bank(1)[:], ident[0:4, h:h + 1].to_broadcast([4, P]), gate[:, 2:4, :], start=True, stop=True), 1)
                b = bank(0)
                r = slice(QK * (h % 2), QK * (h % 2) + QK)
                q, k = mqk[r, h // 2, :], mqk[r, 2 + h // 2, :]
                pe.matmul(b[:, 0:S], k[:, 0:P], q, start=True, stop=True)
                full(pe.matmul(b[:, S:3 * P], k[:, P:S], q[:, P:S], start=True, stop=True), 0)

            def m_sums(h):
                wait("mweights_ready")
                b = bank(2)
                w = pA[:, h % 2, :]
                f = slice(h * P, (h + 1) * P)
                pe.matmul(b[:, 0:S], mv[:, 0, f], w[:, 0:S], start=True, stop=False, skip_group_check=True)
                pe.matmul(b[:, P:S], mv[:, 1, f], w[:, S:3 * P], start=False, stop=True, skip_group_check=True)
                pe.matmul(b[:, S:2 * S], ones, w[:, 0:S], start=False, stop=False, skip_group_check=True)
                full(pe.matmul(b[:, S + P:2 * S], ones, w[:, S:3 * P], start=False, stop=True, skip_group_check=True), 2)

            m_scores(0)
            for h in range(MH + 1):
                if h + 1 < MH:
                    m_scores(h + 1)
                if h < MH:
                    m_sums(h)
                if h:
                    head_squares()

            for half in range(2):
                ready = None if half else "act_ready"
                chunk(("out", half), 0, att_hi, att_lo, ready=ready)
                chunk(("out", half), 1, act_hi, act_lo, ready=ready)
            for _ in range(2):
                sum_squares(0)
                sum_squares(1)
            for g in range(8):
                product(("up", g), act_hi, act_lo, ready="act_ready" if g == 0 else None)
            product(("down", 0), u_hi, u_lo, ready="u_ready", per=4)
            product(("down", 1), u_hi, u_lo)
            for _ in range(2):
                sum_squares(0)
                sum_squares(1)

            for l in range(LAYERS):
                product((l, "in", 3), act_hi, act_lo, ready="act_ready")
                for g in (4, 0, 1):
                    product((l, "in", g), act_hi, act_lo)
                product((l, "in", 2), act_hi, act_lo, token_major=True)
                for g in (0, 1):
                    pe.wait_ge(sem(freed((l, "in", g))[0]), freed((l, "in", g))[1])
                rope(qk2)
                wait("rope_done", 4)
                pe.wait_ge(sem(freed((l, "in", 2))[0]), freed((l, "in", 2))[1])
                scores(qk2, 0)
                for i in range(UNITS + 2):
                    if i < UNITS:
                        chunk(*todoB(l)[i], act_hi, act_lo)
                    if i + 1 < UNITS:
                        scores(qk2, i + 1)
                    if i % 2 == 0 and i >= 2:
                        apply_v(ptB, v2, (i // 2 - 1) * P, P, 0, True)
                    if i % 2 == 1 and i < UNITS:
                        turn(pB[:, 1, :])
                    if i % 2 == 1 and i >= 3:
                        head_squares()
                wait("conv_done", GT)
                b = bank(2)
                for k in range(GT):
                    ins = pe.matmul(b[:, 0:S], ones, cacc[:, k, :], start=(k == 0), stop=(k == GT - 1))
                full(ins, 2)
                wait("csq_ready")
                b = bank("a")
                for k in range(GT):
                    ins = pe.matmul(b[:, 0:S], ones, csq[:, k, :], start=(k == 0), stop=(k == GT - 1))
                full(ins, "a")
                product((l, "attn", 0), o_hi, o_lo, ready="o_ready")
                product((l, "conv", 0), uc_hi, uc_lo, ready="uc_ready", per=4)
                product((l, "attn", 1), o_hi, o_lo)
                product((l, "conv", 1), uc_hi, uc_lo)
                product((l, "out", 0), act_hi, act_lo, ready="mixed_split", per=4)
                product((l, "out", 1), act_hi, act_lo)
                sum_squares(0)
                sum_squares(1)
                for g in range(11):
                    product((l, "ffn", g), act_hi, act_lo, ready="act_ready" if g == 0 else None)
                product((l, "down", 0), u_hi, u_lo, ready="u_ready", per=2)
                product((l, "down", 1), u_hi, u_lo)
                sum_squares(0)
                sum_squares(1)

            for kh in range(2):
                wait("outf_ready", 4)
                for tt in range(TT):
                    i = 2 * tt
                    b = bank(i)
                    for k in range(4):
                        ins = pe.transpose(b[:, k * P:(k + 1) * P], outf[:, 4 * kh + k, tt * P:tt * P + P], ident)
                    full(ins, i)

        @block.scalar
        def _(act):
            a = Own(act, sem, "act_step")
            n = Tally()

            def wait(name, by=1):
                act.wait_ge(sem(name), n(name, by))

            def full(i):
                wait(f"bank{i}_full")
                return pa if i == "a" else pv[i]

            def split(c):
                if c >= NCH:
                    return
                act.wait_ge(sem(f"raw_loaded{c % RING}"), landed[c])
                if c >= RING:
                    act.wait_ge(sem("mm_done"), c - RING + 1)
                nk = chunks[c][0]
                a(act.activation(hi[:, c % RING, 0:nk, :], raw[:, c % RING, 0:nk, :], ACT.Copy), "hi_done")

            def steps(name):
                for c in groups[name][1]:
                    split(c + LEAD)

            def complete(name):
                act.wait_ge(sem("mm_done"), groups[name][1][-1] + 1)
                return banks(name)

            def evacuate(name, dst, func=ACT.Copy, scale=1.0):
                a(act.activation(dst, complete(name), func, scale=scale), *freed(name))

            def rstd_from(width, eps, slot):
                b = full("a")
                a(act.activation(rstd[:, slot, :], b[:, 0:S], ACT.Ln, scale=1.0 / width, bias=small[:, eps:eps + 1]), "banka_free")
                a.settle()
                a(act.activation(rstd[:, slot, :], rstd[:, slot, :], ACT.Exp, scale=-0.5), "rstd_ready")

            def squares_of_x(ready="x_ready"):
                for half in range(2):
                    wait(ready)
                    k = slice(4 * half, 4 * half + 4)
                    a(act.activation(sq[:, k, :], x[:, k, :], ACT.Square), "sq_ready")

            def high_of_norm(src, shift=None):
                for k in range(KD):
                    wait("hf_ready")
                    bias = shift[:, k:k + 1] if shift is not None else 0.0
                    a(act.activation(act_hi[:, k, :], src(k), ACT.Identity, bias=bias), "act_hi_ready")

            def high(src, dst, ready, done, scale=1.0):
                wait(ready)
                a(act.activation(dst, src, ACT.Copy, scale=scale), done)

            def exps(u, s, p):
                wait("max_ready")
                i = u % 2
                for q, (lo_, hi_) in enumerate(((0, P), (P, 3 * P))):
                    a(act.activation(p[:, i, lo_:hi_], s[:, i, lo_:hi_], ACT.Exp, bias=small[:, 2 + 2 * i + q:3 + 2 * i + q],
                                     accum_out=small[:, 6 + 2 * i + q:7 + 2 * i + q]), "exp_done")

            def take_turned(pt):
                a(act.activation(pt, full(1)[:, 0:3 * P], ACT.Copy), "bank1_free")

            for name, (r, ap, tiles) in pack.items():
                act.dma_start(rows[r:r + tiles, :], ap.rearrange("(r p) -> r p", p=P)).then_inc(sem("params_loaded"), 16)
            act.dma_start(adab[0:NMOD, :], t["ada_b_2"].rearrange("l (r p) -> (l r) p", p=P)).then_inc(sem("params_loaded"), 16)
            act.dma_start(cwr[0:TAPS, :, :], t["dw_conv_w_2"].rearrange("l j o c -> j (l o) c")).then_inc(sem("params_loaded"), 16)
            act.dma_start(posi[0:1, 0:S], t["positions"]).then_inc(sem("pos_loaded"), 16)
            act.dma_start(posi[0:1, S:2 * S], t["positions_2"]).then_inc(sem("pos_loaded"), 16)
            pairs = lamr[:].rearrange("o (l c) i d -> o l c i d", c=2)
            for i, name in enumerate(("lambda_q1_2", "lambda_k1_2", "lambda_q2_2", "lambda_k2_2")):
                for l in range(LAYERS):
                    act.dma_start(pairs[0:1, l, i // 2, i % 2, :], t[name][l:l + 1, :]).then_inc(sem("lam_loaded"), 16)
            act.dma_start(wg[:, :, :], t["w_in"][0, :, 3072:3080].rearrange("(k p) f -> p k f", p=P)).then_inc(sem("gate_weights_loaded"), 16)
            act.dma_start(gbias[:, 0:1], t["b_igate"].rearrange("o h -> h o")).then_inc(sem("gate_weights_loaded"), 16)
            act.dma_start(gbias[:, 1:2], t["b_fgate"].rearrange("o h -> h o")).then_inc(sem("gate_weights_loaded"), 16)

            squares_of_x("x_tiles_ready")
            split(0)
            wait("angles_ready")
            a(act.activation(tabs[:, :, :], tabs[:, :, :], ACT.Sin), "tables_ready")
            wait("lam_dots_ready")
            a(act.activation(lams[0:1, 4:8], lams[0:1, 0:4], ACT.Exp), "lam_exps_ready")
            wait("c_loaded")
            a(act.activation(ca[:, 0, :], pcols("c"), ACT.Exp, scale=-1.0), "c_exp_ready")
            wait("eps_ready")
            rstd_from(D, 0, 0)
            split(1)
            high_of_norm(lambda k: hng[:, k, :])
            steps(("in", 0))
            evacuate(("in", 0), qk1[:, 0:4, :])
            steps(("in", 1))
            evacuate(("in", 1), qk1[:, 4:8, :])
            steps(("in", 2))
            evacuate(("in", 2), v1[:, :, :])

            wait("gates_biased")
            a(act.activation(gate[:, 2, :], gate[:, 1, :], ACT.Abs))
            a.settle()
            a(act.activation(gate[:, 2, :], gate[:, 2, :], ACT.Exp, scale=-1.0))
            a.settle()
            a(act.activation(gate[:, 2, :], gate[:, 2, :], ACT.Ln, bias=1.0), "softplus_ready")

            exps(0, sA, pA)
            for i in range(UNITS + 1):
                if i < len(todoA):
                    name, j = todoA[i]
                    split(groups[name][1][j] + LEAD)
                if i + 1 < UNITS:
                    exps(i + 1, sA, pA)
                if i < UNITS:
                    take_turned(ptA[:, i % 2, :])
                if i < len(todoA) and j == 1:
                    if name[1] == 3:
                        evacuate(name, mqk[:, :, :])
                    elif name[1] == 4:
                        evacuate(name, mv[:, :, :])
                    else:
                        evacuate(name, mo[:, :, :], ACT.Tanh, 0.5)
                if i >= 2 and i % 2 == 0:
                    h = i // 2 - 1
                    high(hf[:, h % 2, :], att_hi[:, h, :], "of_ready", "act_hi_ready")

            def m_exps(h):
                a(act.activation(bcA[:, h % 2, :], full(1)[:], ACT.Copy), "bank1_free")
                wait("mexp_arg_ready")
                a(act.activation(sA[:, h % 2, :], sA[:, h % 2, :], ACT.Exp), "mexp_done")
                if h >= 2:
                    act.wait_ge(sem("hm_ready"), h - 1)
                a(act.activation(emA[:, h % 2, :], bcA[:, h % 2, S:2 * S], ACT.Exp), "mexp_done")

            def m_norm(h):
                wait("hm_ready")
                a(act.activation(sq[:, 0, :], hmA[:, h % 2, :], ACT.Square), "hsq_ready")
                rstd_from(P, 0, h % 2)
                high(hf[:, h % 2, :], act_hi[:, 4 + h, :], "of_ready", "act_hi_ready")

            m_exps(0)
            for h in range(MH + 1):
                if h + 1 < MH:
                    m_exps(h + 1)
                if h:
                    m_norm(h - 1)

            def post_norm(stage):
                for half in range(2):
                    steps((stage, half))
                    a(act.activation(sq[:, 4 * half:4 * half + 4, :], complete((stage, half)), ACT.Square), "sq_ready")
                rstd_from(D, 0, 0)

            post_norm("out")
            squares_of_x()
            rstd_from(D, 0, 1)
            high_of_norm(lambda k: hf[:, k % 4, :])
            for g in range(8):
                steps(("up", g))
                if g:
                    act.wait_ge(sem("u_hi_ready"), g)
                a(act.activation(sq[:, 0:4, :], complete(("up", g)), ACT.Relu), *freed(("up", g)))
                high(sq[:, 4:8, :], u_hi[:, 4 * g:4 * g + 4, :], "u_f32_ready", "u_hi_ready")
            post_norm("down")

            for l in range(LAYERS):
                squares_of_x()
                rstd_from(D, 0, 1)
                high_of_norm(lambda k: hf[:, k % 4, :], shift=modT[:, l * MODS:l * MODS + KD])
                steps((l, "in", 3))
                steps((l, "in", 4))
                evacuate((l, "in", 4), csq[:, :, :], ACT.Tanh, 0.5)
                for g in (0, 1):
                    steps((l, "in", g))
                    evacuate((l, "in", g), qk2[:, 4 * g:4 * g + 4, :])
                steps((l, "in", 2))
                evacuate((l, "in", 2), v2[:, :, :])
                exps(0, sB, pB)
                for i in range(UNITS + 2):
                    if i < UNITS:
                        name, j = todoB(l)[i]
                        split(groups[name][1][j] + LEAD)
                    if i + 1 < UNITS:
                        exps(i + 1, sB, pB)
                    if i % 2 == 0 and i >= 2:
                        wait("o_f32_ready")
                        a(act.activation(sq[:, 0, :], oB[:], ACT.Square), "hsq_ready")
                    if i % 2 == 1 and i < UNITS:
                        take_turned(ptB[:])
                    if i < UNITS and j == 1:
                        g = name[2] - 5
                        evacuate(name, gates[:, 4 * g:4 * g + 4, :], ACT.Tanh, 0.5)
                    if i % 2 == 1 and i >= 3:
                        h = (i - 3) // 2
                        rstd_from(P, 1, h % 2)
                        high(hf[:, h % 2, :], o_hi[:, h, :], "on_ready", "o_hi_ready")
                wait("centred")
                a(act.activation(csq[:, :, :], cacc[:, :, :], ACT.Square), "csq_ready")
                rstd_from(GF, 1, 0)
                wait("ln_ready")
                a(act.activation(csq[:, :, :], cacc[:, :, :], ACT.Tanh, scale=0.5), "ln_tanh_ready")
                high(csq[:, :, :], uc_hi[:, :, :], "uc_f32_ready", "uc_hi_ready", scale=0.5)
                for half in range(2):
                    steps((l, "attn", half))
                    steps((l, "conv", half))
                    k = slice(4 * half, 4 * half + 4)
                    high(gates[:, k, :], act_hi[:, k, :], "mixed_ready", "mixed_hi_ready", scale=0.5)
                for half in range(2):
                    steps((l, "out", half))
                squares_of_x()
                rstd_from(D, 0, 0)
                high_of_norm(lambda k: hf[:, k % 4, :], shift=modT[:, l * MODS + 3 * KD:l * MODS + 4 * KD])
                for g in range(11):
                    steps((l, "ffn", g))
                    a(act.activation(sq[:, 0:2, :], complete((l, "ffn", g))[:, 0, :], ACT.Tanh, scale=0.5), "silu_gate_ready")
                    high(sq[:, 4:6, :], u_hi[:, 2 * g:2 * g + 2, :], "u_f32_ready", "u_hi_ready")
                for half in range(2):
                    steps((l, "down", half))
            squares_of_x()
            rstd_from(D, 0, 1)

        @block.gpsimd
        def _(pool):
            p = Own(pool, sem, "pool_step")

            loads = LAYERS * ADA_GROUPS * KD // ADA_K

            def load(j):
                if j >= loads:
                    return
                i, k = j * ADA_K // KD, j * ADA_K % KD
                src = t["ada_w_2"][i // ADA_GROUPS, k * P:(k + ADA_K) * P, i % ADA_GROUPS * GF:(i % ADA_GROUPS + 1) * GF]
                pool.dma_start(ada_raw[:, j % ADA_RING], src.rearrange("(k p) f -> p k f", p=P)).then_inc(sem(f"ada_loaded{j % ADA_RING}"), 16)

            def ada(i, k):
                acc = ada_acc[:, i % 2, :]
                if k == 0 and i >= 2:
                    pool.wait_ge(sem("ada_reduced"), i - 1)
                j, kk = (i * KD + k) // ADA_K, k % ADA_K
                w = ada_raw[:, j % ADA_RING, kk, :]
                if kk == 0:
                    pool.wait_ge(sem(f"ada_loaded{j % ADA_RING}"), 16 * (j // ADA_RING + 1))
                p(pool.tensor_scalar(w if k else acc, w, ca[:, 1, k:k + 1], None, ALU.mult))
                if k:
                    p.settle()
                    p(pool.tensor_tensor(acc, acc, w, ALU.add), "ada_ready" if k == KD - 1 else None)
                if kk == ADA_K - 1:
                    p.settle()
                    load(j + ADA_RING)

            def split(c):
                if c not in by_pool:
                    return
                pool.wait_ge(sem("hi_done"), c + 1)
                nk = chunks[c][0]
                p(pool.tensor_tensor(lo[:, c % RING, 0:nk, :], raw[:, c % RING, 0:nk, :], hi[:, c % RING, 0:nk, :].bitcast(F32),
                                     ALU.subtract), "lo_done_p")

            for j in range(ADA_RING):
                load(j)
            pool.wait_ge(sem("c_ready"), 1)
            for c in range(NCH):
                split(c + LEAD)
                for i, k in ada_work.get(c, ()):
                    ada(i, k)

        @block.vector
        def _(dve):
            v = Own(dve, sem, "dve_step")
            n = Tally()

            def wait(name, by=1):
                dve.wait_ge(sem(name), n(name, by))

            def full(i):
                wait(f"bank{i}_full")
                return pv[i]

            def link(ins, name=None, value=None):
                v(ins, name, value)
                v.settle()

            def split(c):
                if c >= NCH or c in by_pool:
                    return
                dve.wait_ge(sem("hi_done"), c + 1)
                nk = chunks[c][0]
                v(dve.tensor_tensor(lo[:, c % RING, 0:nk, :], raw[:, c % RING, 0:nk, :], hi[:, c % RING, 0:nk, :].bitcast(F32),
                                    ALU.subtract), "lo_done_v")

            def ada_columns(c):
                if c not in ada_at:
                    return
                l, q = ada_at[c]
                b = full(2)
                m = hf[:, 0:2, :].rearrange("p a (b c) -> p (a b) c", b=2)
                link(dve.tensor_tensor(m, b[:].rearrange("p (f j) -> p f j", f=GT), ident.unsqueeze(1).to_broadcast([P, GT, P]), ALU.mult), "bank2_free")
                dve.sem_inc(sem("ada_reduced"), 1)
                link(dve.tensor_reduce(small[:, 10:14], m, AX.X, ALU.add))
                mc = slice(l * MODS + q * GT, l * MODS + q * GT + GT)
                link(dve.tensor_tensor(modT[:, mc], small[:, 10:14], adabT[:, mc], ALU.add))

            def steps(name):
                for c in groups[name][1]:
                    split(c + LEAD)
                    ada_columns(c)

            def complete(name):
                dve.wait_ge(sem("mm_done"), groups[name][1][-1] + 1)
                return banks(name)

            def low(src, d_hi, d_lo, hi_done, done, scale=None, shift=None):
                wait(hi_done)
                h = d_hi.bitcast(F32)
                if scale is not None:
                    ins = dve.scalar_tensor_tensor(out=d_lo, in0=src, scalar=scale, in1=h, op0=ALU.mult, op1=ALU.subtract)
                elif shift is not None:
                    ins = dve.scalar_tensor_tensor(out=d_lo, in0=src, scalar=shift, in1=h, op0=ALU.add, op1=ALU.subtract)
                else:
                    ins = dve.tensor_tensor(d_lo, src, h, ALU.subtract)
                v(ins, done)

            def normalise(gain, slot, dst, shift=None):
                wait("rstd_ready")

                def low_part(k):
                    low(dst(k), act_hi[:, k, :], act_lo[:, k, :], "act_hi_ready", "act_ready",
                        shift=shift[:, k:k + 1] if shift is not None else None)

                for k in range(KD):
                    if k >= 4:
                        v.settle()
                    v(dve.scalar_tensor_tensor(out=dst(k), in0=x[:, k, :], scalar=gain[:, k:k + 1], in1=rstd[:, slot, :],
                                               op0=ALU.mult, op1=ALU.mult), "hf_ready")
                    if k >= 2:
                        low_part(k - 2)
                low_part(KD - 2)
                low_part(KD - 1)
                v.settle()

            def conv_work(l):
                for j in range(TAPS):
                    for k in range(GT):
                        w = convw[:, GT * l + k, j:j + 1]
                        src = cu[:, k, j:j + S]
                        name = "conv_done" if j == TAPS - 1 else f"conv_step{k}"
                        if j == 0:
                            v(dve.tensor_scalar(cacc[:, k, :], src, w, pcols(("convb", l))[:, k:k + 1], ALU.mult, ALU.add), name)
                        else:
                            dve.wait_ge(sem(f"conv_step{k}"), v.n.seen(f"conv_step{k}"))
                            v(dve.scalar_tensor_tensor(out=cacc[:, k, :], in0=src, scalar=w, in1=cacc[:, k, :], op0=ALU.mult, op1=ALU.add), name)
                        yield

            def softmax_max(u, s):
                b = full(0)
                i = u % 2
                link(dve.scalar_tensor_tensor(out=s[:, i, :], in0=b[:, 0:3 * P], scalar=SCALE, in1=cst[:, C_ADD:C_ADD + 3 * P],
                                              op0=ALU.mult, op1=ALU.add), "bank0_free")
                v(dve.tensor_reduce(small[:, 2 + 2 * i:3 + 2 * i], s[:, i, 0:P], AX.X, ALU.max, negate=True))
                v(dve.tensor_reduce(small[:, 3 + 2 * i:4 + 2 * i], s[:, i, P:3 * P], AX.X, ALU.max, negate=True), "max_ready")

            def rope(qk, blk):
                for j in range(4):
                    i = 2 * (j % 2)
                    b = full(i)
                    z = hf[:, 0:2, :]
                    k = slice(2 * j, 2 * j + 2)
                    sn = tabs[:, blk, 0:S].unsqueeze(1).to_broadcast([P, 2, S])
                    cs = tabs[:, blk, S:2 * S].unsqueeze(1).to_broadcast([P, 2, S])
                    v(dve.tensor_tensor(z, b[:].rearrange("p (a s) -> p a s", a=2), sn, ALU.mult), f"bank{i}_free")
                    link(dve.tensor_tensor(qk[:, k, :], qk[:, k, :], cs, ALU.mult))
                    link(dve.tensor_tensor(qk[:, k, :], qk[:, k, :], z, ALU.add), "rope_done")

            def reduce_angles(i, ang):
                tmp, r = hf[:, 0, :], hf[:, 1, :]
                link(dve.tensor_scalar(tmp, ang, 1.0 / (2.0 * np.pi), MAGIC, ALU.mult, ALU.add))
                link(dve.tensor_scalar(tmp, tmp, MAGIC, None, ALU.subtract))
                link(dve.scalar_tensor_tensor(out=r, in0=tmp, scalar=-TWO_PI[0], in1=ang, op0=ALU.mult, op1=ALU.add))
                link(dve.scalar_tensor_tensor(out=r, in0=tmp, scalar=-TWO_PI[1], in1=r, op0=ALU.mult, op1=ALU.add))
                link(dve.scalar_tensor_tensor(out=r, in0=tmp, scalar=-TWO_PI[2], in1=r, op0=ALU.mult, op1=ALU.add))
                link(dve.tensor_scalar(tabs[:, i, 0:S], r, BEFORE_PI, -BEFORE_PI, ALU.min, ALU.max))
                link(dve.scalar_tensor_tensor(out=r, in0=tabs[:, i, 0:S], scalar=-1.0, in1=tabs[:, i, 0:S], op0=ALU.mult, op1=ALU.max))
                link(dve.tensor_scalar(tabs[:, i, S:2 * S], r, -1.0, PI / 2, ALU.mult, ALU.add), "angles_ready" if i else None)

            v(dve.memset(small[:, 0:1], EPS))
            v(dve.memset(small[:, 1:2], EPS_SUB), "eps_ready")
            wait("pos_loaded", 32)
            v(dve.tensor_copy(posf[0:1, :], posi[0:1, :]), "positions_ready")
            for j in range(4):
                i = 2 * (j % 2)
                b = full(i)
                v(dve.tensor_copy(x[:, 2 * j:2 * j + 2, :], b[:].rearrange("p (a s) -> p a s", a=2)), f"bank{i}_free")
            v.settle()
            dve.sem_inc(sem("x_tiles_ready"), 2)
            b = full(0)
            v(dve.tensor_copy(parT[:], b[:, 0:NROW]))
            link(dve.tensor_copy(adabT[:], b[:, P:P + NMOD]), "bank0_free")
            dve.sem_inc(sem("c_loaded"), 1)
            v(dve.tensor_scalar(convw[:], full(2)[:, 0:32 * LAYERS * GT].rearrange("p (i j) -> p i j", j=32)[:, :, 0:TAPS], 0.5, None, ALU.mult), "bank2_free")
            wait("lam_loaded", 16 * 4 * LAYERS)
            link(dve.tensor_tensor(lamp[0:1, :, :], lamr[0:1, :, 0, :], lamr[0:1, :, 1, :], ALU.mult))
            v(dve.tensor_reduce(lams[0:1, 0:4], lamp[0:1, :, :], AX.X, ALU.add), "lam_dots_ready")
            b = full(0)
            dve.wait_ge(sem("const_loaded"), 16)
            link(dve.tensor_scalar(hf[:, 2:4, :], b[:].rearrange("p (a s) -> p a s", a=2), cst[:, C_FREQ:C_FREQ + 1], None, ALU.mult), "bank0_free")
            reduce_angles(0, hf[:, 2, :])
            reduce_angles(1, hf[:, 3, :])
            wait("lam_exps_ready")
            e = lams[0:1, 4:8].rearrange("o (l c) -> o l c", c=2)
            link(dve.tensor_tensor(lams[0:1, 8:10], e[:, :, 1], e[:, :, 0], ALU.subtract))
            link(dve.tensor_scalar(lams[0:1, 8:9], lams[0:1, 8:9], -LAMBDA_INIT[0], None, ALU.add))
            v(dve.tensor_scalar(lams[0:1, 9:10], lams[0:1, 9:10], -LAMBDA_INIT[1], None, ALU.add), "lam_ready")
            wait("c_exp_ready")
            link(dve.tensor_scalar(ca[:, 0, :], ca[:, 0, :], 1.0, None, ALU.add))
            link(dve.reciprocal(ca[:, 0, :], ca[:, 0, :]))
            link(dve.tensor_tensor(ca[:, 1, :], ca[:, 0, :], pcols("c"), ALU.mult), "c_ready")
            v(dve.tensor_scalar(cols[:, 32:36], pcols("g_mlstm"), 0.5, None, ALU.mult))
            for l in range(LAYERS):
                v(dve.tensor_scalar(cols[:, 36 + l:37 + l], pcols(("subln", l)), 1.0 - LAMBDA_INIT[l], None, ALU.mult))
            link(dve.tensor_copy(nlam[:], full(2)[:, 0:LAYERS]), "bank2_free")
            split(0)
            normalise(pcols("g_mix_pre"), 0, lambda k: hng[:, k, :])
            split(1)
            for g in range(3):
                steps(("in", g))
            wait("tables_ready")
            rope(qk1, 0)

            b = full(2)
            wait("gate_weights_loaded", 48)
            v(dve.tensor_scalar(gate[:, 0, :], b[0:4, 0:S], gbias[:, 0:1], None, ALU.add))
            v(dve.tensor_scalar(gate[:, 1, :], b[0:4, S:2 * S], gbias[:, 1:2], None, ALU.add), "bank2_free")
            v.settle()
            dve.sem_inc(sem("gates_biased"), 1)
            link(dve.memset(gate[:, 7, :], 0.0))

            def gate_rows():
                wait("softplus_ready")
                link(dve.scalar_tensor_tensor(out=gate[:, 3, :], in0=gate[:, 1, :], scalar=0.0, in1=gate[:, 2, :], op0=ALU.min, op1=ALU.subtract))
                link(dve.tensor_tensor_scan(gate[:, 4, :], gate[:, 3, :], gate[:, 7, :], 0.0, ALU.add, ALU.add))
                link(dve.tensor_tensor(gate[:, 5, :], gate[:, 0, :], gate[:, 4, :], ALU.subtract))
                link(dve.tensor_tensor_scan(gate[:, 6, :], gate[:, 5, :], gate[:, 5, :], 0.0, ALU.max, ALU.max))
                link(dve.tensor_scalar(gate[:, 2, :], gate[:, 6, :], -1.0, None, ALU.mult))
                link(dve.tensor_tensor(gate[:, 3, :], gate[:, 2, :], gate[:, 4, :], ALU.subtract), "gate_rows_ready")

            def probs(u, p):
                i = u % 2
                wait("exp_done", 2)
                r = small[:, 14 + 2 * i:16 + 2 * i]
                link(dve.reciprocal(r, small[:, 6 + 2 * i:8 + 2 * i]))
                v(dve.tensor_scalar(p[:, i, 0:P], p[:, i, 0:P], r[:, 0:1], None, ALU.mult))
                v(dve.tensor_scalar(p[:, i, P:3 * P], p[:, i, P:3 * P], r[:, 1:2], None, ALU.mult), "probs_ready")

            softmax_max(0, sA)
            gate_rows()
            for i in range(UNITS + 1):
                if i < len(todoA):
                    name, j = todoA[i]
                    split(groups[name][1][j] + LEAD)
                if i < UNITS:
                    probs(i, pA)
                if i + 1 < UNITS:
                    softmax_max(i + 1, sA)
                if i >= 2 and i % 2 == 0:
                    h = i // 2 - 1
                    v(dve.tensor_copy(hf[:, h % 2, :], full(2)[:, 0:S]), "bank2_free")
                    v.settle()
                    dve.sem_inc(sem("of_ready"), 1)
                    low(hf[:, h % 2, :], att_hi[:, h, :], att_lo[:, h, :], "act_hi_ready", "act_ready")
            link(dve.tensor_copy(acol[:].rearrange("p t h -> p (t h)"), full(0)[:, 0:8]), "bank0_free")

            def m_args(h):
                dve.wait_ge(sem("bank1_free"), UNITS + h + 1)
                i = h % 2
                v(dve.tensor_scalar(sA[:, i, 0:S], bcA[:, i, 0:S], acol[:, 0, h:h + 1], 0.0, ALU.add, ALU.min))
                v(dve.tensor_scalar(sA[:, i, S:3 * P], bcA[:, i, P:S], acol[:, 1, h:h + 1], 0.0, ALU.add, ALU.min), "mexp_arg_ready")

            def m_weights(h):
                i = h % 2
                wait("mexp_done", 2)
                link(dve.tensor_tensor(sA[:, i, :], sA[:, i, :], cst[:, C_MUL:C_MUL + 3 * P], ALU.mult))
                link(dve.scalar_tensor_tensor(out=pA[:, i, :], in0=full(0)[:, 0:3 * P], scalar=SCALE, in1=sA[:, i, :],
                                              op0=ALU.mult, op1=ALU.mult), "bank0_free")
                dve.sem_inc(sem("mweights_ready"), 1)

            def m_out(h):
                i = h % 2
                b = full(2)
                d = hf[:, 2 + i, :]
                link(dve.tensor_tensor(d, b[:, S:2 * S], emA[:, i, :], ALU.max))
                link(dve.scalar_tensor_tensor(out=d, in0=b[:, S:2 * S], scalar=-1.0, in1=d, op0=ALU.mult, op1=ALU.max))
                link(dve.reciprocal(d, d))
                link(dve.tensor_tensor(hmA[:, i, :], b[:, 0:S], d, ALU.mult), "bank2_free")
                dve.sem_inc(sem("hm_ready"), 1)

            def m_final(h):
                i = h % 2
                wait("rstd_ready")
                link(dve.scalar_tensor_tensor(out=hf[:, 2 + i, :], in0=hmA[:, i, :], scalar=cols[:, 32 + h:33 + h], in1=rstd[:, i, :],
                                              op0=ALU.mult, op1=ALU.mult))
                v(dve.scalar_tensor_tensor(out=hf[:, i, :], in0=mo[:, h, :], scalar=1.0, in1=hf[:, 2 + i, :], op0=ALU.add, op1=ALU.mult), "of_ready", MH + h + 1)
                low(hf[:, i, :], act_hi[:, 4 + h, :], act_lo[:, 4 + h, :], "act_hi_ready", "act_ready")
                v.settle()

            m_args(0)
            m_weights(0)
            for h in range(MH + 1):
                if h + 1 < MH:
                    m_args(h + 1)
                if h < MH:
                    m_out(h)
                if h + 1 < MH:
                    m_weights(h + 1)
                if h:
                    m_final(h - 1)

            def post_norm(stage, gain):
                for half in range(2):
                    steps((stage, half))
                wait("rstd_ready")
                for half in range(2):
                    src = complete((stage, half))
                    for f in range(GT):
                        k = GT * half + f
                        ins = dve.scalar_tensor_tensor(out=hf[:, f, :], in0=tile_of(src, f), scalar=gain[:, k:k + 1], in1=rstd[:, 0, :],
                                                       op0=ALU.mult, op1=ALU.mult)
                        v(ins, *(freed((stage, half)) if f == GT - 1 else ()))
                    v.settle()
                    k = slice(GT * half, GT * half + GT)
                    link(dve.tensor_tensor(x[:, k, :], x[:, k, :], hf[:], ALU.add), "x_ready")

            post_norm("out", pcols("g_mix_post"))
            normalise(pcols("g_mlp_pre"), 1, lambda k: hf[:, k % 4, :])
            for g in range(8):
                steps(("up", g))
                name, value = freed(("up", g))
                dve.wait_ge(sem(name), value)
                v(dve.tensor_tensor(sq[:, 4:8, :], sq[:, 0:4, :], sq[:, 0:4, :], ALU.mult), "u_f32_ready")
                k = slice(4 * g, 4 * g + 4)
                low(sq[:, 4:8, :], u_hi[:, k, :], u_lo[:, k, :], "u_hi_ready", "u_ready")
                v.settle()
            post_norm("down", pcols("g_mlp_post"))

            def update(name, half, gain):
                src = complete(name)
                for f in range(GT):
                    k = GT * half + f
                    ins = dve.scalar_tensor_tensor(out=x[:, k, :], in0=tile_of(src, f), scalar=gain[:, k:k + 1], in1=x[:, k, :],
                                                   op0=ALU.mult, op1=ALU.add)
                    v(ins, *(freed(name) if f == GT - 1 else ()))
                v.settle()
                dve.sem_inc(sem("x_ready"), 1)

            for l in range(LAYERS):
                mod = [modT[:, l * MODS + i * KD:l * MODS + (i + 1) * KD] for i in range(6)]
                gain1, gate1, gain2, gate2 = (cols[:, 8 * i:8 * i + 8] for i in range(4))
                v(dve.scalar_tensor_tensor(out=gain1, in0=mod[1], scalar=1.0, in1=pcols(("norm1", l)), op0=ALU.add, op1=ALU.mult))
                v(dve.tensor_scalar(gate1, mod[2], 1.0, None, ALU.add))
                v(dve.scalar_tensor_tensor(out=gain2, in0=mod[4], scalar=1.0, in1=pcols(("norm2", l)), op0=ALU.add, op1=ALU.mult))
                link(dve.tensor_scalar(gate2, mod[5], 1.0, None, ALU.add))
                normalise(gain1, 1, lambda k: hf[:, k % 4, :], shift=mod[0])
                steps((l, "in", 3))
                steps((l, "in", 4))
                link(dve.memset(cu[:, :, 0:TAPS - 1], 0.0))
                name, value = freed((l, "in", 4))
                dve.wait_ge(sem(name), value)
                src = complete((l, "in", 3)).rearrange("p b (a s) -> p (b a) s", a=2)
                link(dve.scalar_tensor_tensor(out=cu[:, :, TAPS - 1:], in0=csq[:], scalar=1.0, in1=src, op0=ALU.add, op1=ALU.mult), *freed((l, "in", 3)))
                conv = conv_work(l)
                for g in (0, 1, 2):
                    for c in groups[(l, "in", g)][1]:
                        split(c + LEAD)
                        for _ in range(10):
                            next(conv)
                rope(qk2, 1)
                softmax_max(0, sB)
                for i in range(UNITS + 2):
                    if i < UNITS:
                        name, j = todoB(l)[i]
                        split(groups[name][1][j] + LEAD)
                        for _ in range(8):
                            next(conv)
                        c = i % 2
                        wait("exp_done", 2)
                        r = small[:, 14 + 2 * c:16 + 2 * c]
                        link(dve.reciprocal(r, small[:, 6 + 2 * c:8 + 2 * c]))
                        if c:
                            link(dve.tensor_scalar(r, r, nlam[:, l:l + 1], None, ALU.mult))
                        for q, (lo_, hi_) in enumerate(((0, P), (P, 3 * P))):
                            pc = pB[:, c, lo_:hi_]
                            if c == 0:
                                v(dve.tensor_scalar(pc, pc, r[:, q:q + 1], None, ALU.mult))
                            else:
                                v(dve.scalar_tensor_tensor(out=pc, in0=pc, scalar=r[:, q:q + 1], in1=pB[:, 0, lo_:hi_], op0=ALU.mult, op1=ALU.add),
                                  "probs_ready" if q else None)
                        v.settle()
                    if i + 1 < UNITS:
                        softmax_max(i + 1, sB)
                    if i % 2 == 0 and i >= 2:
                        link(dve.tensor_copy(oB[:], full(2)[:, 0:S]), "bank2_free")
                        dve.sem_inc(sem("o_f32_ready"), 1)
                    if i % 2 == 1 and i >= 3:
                        h = (i - 3) // 2
                        wait("rstd_ready")
                        v(dve.scalar_tensor_tensor(out=hf[:, h % 2, :], in0=oB[:], scalar=cols[:, 36 + l:37 + l], in1=rstd[:, h % 2, :],
                                                   op0=ALU.mult, op1=ALU.mult), "on_ready")
                        low(hf[:, h % 2, :], o_hi[:, h, :], o_lo[:, h, :], "o_hi_ready", "o_ready")
                        v.settle()
                link(dve.tensor_scalar(hf[:, 0, :], full(2)[:, 0:S], 1.0 / GF, None, ALU.mult), "bank2_free")
                link(dve.tensor_tensor(cacc[:], cacc[:], hf[:, 0:1, :].to_broadcast([P, GT, S]), ALU.subtract), "centred")
                wait("rstd_ready")
                link(dve.tensor_tensor(cacc[:], cacc[:], rstd[:, 0:1, :].to_broadcast([P, GT, S]), ALU.mult))
                for k in range(GT):
                    v(dve.tensor_scalar(cacc[:, k, :], cacc[:, k, :], pcols(("lng", l))[:, k:k + 1], pcols(("lnb", l))[:, k:k + 1], ALU.mult, ALU.add),
                      "ln_ready" if k == GT - 1 else None)
                wait("ln_tanh_ready")
                v(dve.scalar_tensor_tensor(out=csq[:], in0=csq[:], scalar=1.0, in1=cacc[:], op0=ALU.add, op1=ALU.mult), "uc_f32_ready")
                low(csq[:], uc_hi[:], uc_lo[:], "uc_hi_ready", "uc_ready", scale=0.5)
                for half in range(2):
                    for branch, first in (("attn", 4 * half), ("conv", 8 + 4 * half)):
                        name = (l, branch, half)
                        steps(name)
                        g = gates[:, first:first + 4, :]
                        link(dve.scalar_tensor_tensor(out=g, in0=g, scalar=1.0, in1=complete(name).rearrange("p b (a s) -> p (b a) s", a=2),
                                                      op0=ALU.add, op1=ALU.mult), *freed(name))
                    k = slice(4 * half, 4 * half + 4)
                    v(dve.tensor_tensor(gates[:, k, :], gates[:, k, :], gates[:, 8 + 4 * half:12 + 4 * half, :], ALU.add), "mixed_ready")
                    low(gates[:, k, :], act_hi[:, k, :], act_lo[:, k, :], "mixed_hi_ready", "mixed_split", scale=0.5)
                for half in range(2):
                    steps((l, "out", half))
                    update((l, "out", half), half, gate1)
                normalise(gain2, 0, lambda k: hf[:, k % 4, :], shift=mod[3])
                for g in range(11):
                    steps((l, "ffn", g))
                    src = complete((l, "ffn", g))
                    wait("silu_gate_ready")
                    link(dve.scalar_tensor_tensor(out=sq[:, 2:4, :], in0=sq[:, 0:2, :], scalar=1.0, in1=src[:, 0, :].rearrange("p (a s) -> p a s", a=2),
                                                  op0=ALU.add, op1=ALU.mult))
                    link(dve.scalar_tensor_tensor(out=sq[:, 4:6, :], in0=sq[:, 2:4, :], scalar=0.5, in1=src[:, 1, :].rearrange("p (a s) -> p a s", a=2),
                                                  op0=ALU.mult, op1=ALU.mult), *freed((l, "ffn", g)))
                    dve.sem_inc(sem("u_f32_ready"), 1)
                    k = slice(2 * g, 2 * g + 2)
                    low(sq[:, 4:6, :], u_hi[:, k, :], u_lo[:, k, :], "u_hi_ready", "u_ready")
                    v.settle()
                for half in range(2):
                    steps((l, "down", half))
                    update((l, "down", half), half, gate2)
            wait("rstd_ready")
            gain = pcols("final")
            for k in range(KD):
                v(dve.scalar_tensor_tensor(out=outf[:, k, :], in0=x[:, k, :], scalar=gain[:, k:k + 1], in1=rstd[:, 1, :],
                                           op0=ALU.mult, op1=ALU.mult), "outf_ready")
            for kh in range(2):
                for tt in range(TT):
                    link(dve.tensor_copy(outt[:, tt, kh * GF:kh * GF + GF], full(2 * tt)[:]), f"bank{2 * tt}_free")
                    dve.sem_inc(sem("out_ready"), 1)


_INS = ["x", "positions", "g_mix_pre", "w_in", "b_igate", "b_fgate", "g_mlstm_out", "w_out", "g_mix_post", "g_mlp_pre",
        "w_up", "w_down", "g_mlp_post", "c_2", "positions_2", "ada_w_2", "ada_b_2", "norm1_g_2", "w_in_2",
        "lambda_q1_2", "lambda_k1_2", "lambda_q2_2", "lambda_k2_2", "subln_g_2", "w_attn_o_2", "dw_conv_w_2",
        "dw_conv_b_2", "conv_ln_g_2", "conv_ln_b_2", "w_conv_o_2", "w_out_2", "norm2_g_2", "w_ffn_in_2",
        "w_ffn_out_2", "final_g_2"]


def kernel(**inputs):
    import numpy as _np
    import concourse.bacc as _bacc
    from concourse import mybir as _mybir
    from concourse.bass_utils import run_bass_kernel_spmd as _run

    nc = _bacc.Bacc("TRN2", target_bir_lowering=False, num_devices=1)
    arrays, aps = {}, {}
    for name in _INS:
        a = _np.ascontiguousarray(inputs[name])
        arrays[f"in_{name}_dram"] = a
        aps[name] = nc.dram_tensor(f"in_{name}_dram", a.shape, _mybir.dt.from_np(a.dtype), kind="ExternalInput").ap()
    c = constants()
    arrays["constants_dram"] = c
    consts = nc.dram_tensor("constants_dram", c.shape, _mybir.dt.float32, kind="ExternalInput").ap()
    out = nc.dram_tensor("out_0_dram", (1, S, D), _mybir.dt.float32, kind="ExternalOutput").ap()
    two_blocks(nc, aps, consts, out)
    r = _run(nc, [arrays], core_ids=[0])
    return r.results[0]["out_0_dram"]
```

```python
from contextlib import ExitStack

import numpy as np

import concourse.bass as bass
from concourse import mybir

F32 = mybir.dt.float32
F32R = mybir.dt.float32r
I32 = mybir.dt.int32
ALU = mybir.AluOpType
ACT = mybir.ActivationFunctionType
AX = mybir.AxisListType

P = 128
S = 256
TT = S // P
D = 1024
KD = D // P
GF = 512
GT = GF // P
CK = 4
RING = 3
LEAD = 2
EPS = 1e-6
EPS_SUB = 1e-5
QK = 64
SCALE = QK ** -0.5
ATTN_HEADS = 4
FAR = 3e38
TAPS_PER_UNIT = 10
CONV_END = 5
UNITS = 8
TAPS = 31
MH = 4
LAYERS = 2
MODS = 48
ADA_GROUPS = MODS // GT
ADA_K = 2
ADA_RING = 3
LAMBDA_INIT = [0.8 - 0.6 * float(np.exp(-0.3 * l)) for l in range(LAYERS)]
MAGIC = 1.5 * 2.0 ** 23
TWO_PI = (6.28125, 0.0019350051879882812, 3.0199157663446332e-07)
PI = float(np.float32(np.pi))
BEFORE_PI = 3.1415925

C_ID, C_ROT, C_ONE = 0, P, 2 * P
C_ADD, C_MUL, C_FREQ = 3 * P, 6 * P, 9 * P
C_ALL = 9 * P + 1


def constants():
    c = np.zeros((P, C_ALL), np.float32)
    i = np.arange(P)
    c[:, C_ID:C_ID + P] = np.eye(P)
    half = QK // 8
    freq = 500000.0 ** (-np.arange(0, 2 * half, 2, dtype=np.float32) / np.float32(2 * half))
    for p in range(P):
        d = p % QK
        if d < half:
            c[p + half, C_ROT + p] = -1.0
        elif d < 2 * half:
            c[p - half, C_ROT + p] = 1.0
        if d < 2 * half:
            c[p, C_FREQ] = freq[d % half]
    c[:, C_ONE:C_ONE + P] = 1.0
    tri = np.where(i[None, :] <= i[:, None], 0.0, -1e30)
    c[:, C_ADD:C_ADD + P] = tri
    c[:, C_ADD + 2 * P:C_ADD + 3 * P] = tri
    up = (i[:, None] <= i[None, :]).astype(np.float32)
    c[:, C_MUL:C_MUL + P] = up
    c[:, C_MUL + P:C_MUL + 2 * P] = 1.0
    c[:, C_MUL + 2 * P:C_MUL + 3 * P] = up
    return c


class Tally:

    def __init__(self):
        self.n = {}

    def __call__(self, name, by=1):
        self.n[name] = self.n.get(name, 0) + by
        return self.n[name]

    def seen(self, name):
        return self.n.get(name, 0)


class Own:

    def __init__(self, eng, sem, steps):
        self.eng, self.sem, self.steps, self.n, self.last = eng, sem, steps, Tally(), None

    def __call__(self, ins, name=None, value=None):
        name = name or self.steps
        ins.then_inc(self.sem(name), 1)
        self.last = name, value or self.n(name)
        return self.last[1]

    def settle(self):
        self.eng.wait_ge(self.sem(self.last[0]), self.last[1])


def plan(t):
    chunks, groups = [], {}

    def group(name, w, cols, tiles, start=0):
        _, ids = groups.setdefault(name, (len(groups), []))
        for k in range(start, tiles, CK):
            nk = min(CK, tiles - k)
            rows = w[k * P:(k + nk) * P, :]
            parts, at = [], 0
            for lo, n in cols:
                parts.append((at, n, rows[:, lo:lo + n].rearrange("(k p) f -> p k f", p=P)))
                at += n
            ids.append(len(chunks))
            chunks.append((nk, parts))

    w = t["w_in"][0]
    for n in range(6):
        group(("in", n), w, [(n * GF, GF)], KD)
    for start in (0, CK):
        for n in range(2):
            group(("out", n), t["w_out"][0], [(n * GF, GF)], start + CK, start)
    for n in range(8):
        group(("up", n), t["w_up"][0], [(n * GF, GF)], KD)
    for n in range(2):
        group(("down", n), t["w_down"][0], [(n * GF, GF)], 32)
    for l in range(LAYERS):
        w = t["w_in_2"][l]
        for n in (3, 4, 0, 1, 2, 5, 6, 7, 8):
            group((l, "in", n), w, [(n * GF, GF)], KD)
        for branch, w_o in (("conv", t["w_conv_o_2"][l]), ("attn", t["w_attn_o_2"][l])):
            for n in range(2):
                group((l, branch, n), w_o, [(n * GF, GF)], GT)
        for start in (0, CK):
            for n in range(2):
                group((l, "out", n), t["w_out_2"][l], [(n * GF, GF)], start + CK, start)
        for n in range(11):
            group((l, "ffn", n), t["w_ffn_in_2"][l], [(n * 256, 256), (2816 + n * 256, 256)], KD)
        for n in range(2):
            group((l, "down", n), t["w_ffn_out_2"][l], [(n * GF, GF)], 22)
    return chunks, groups


def two_blocks(nc, t, consts, out):
    chunks, groups = plan(t)
    NCH = len(chunks)

    first = {name: ids[0] for name, (_, ids) in groups.items()}
    at0 = [first[("in", 2)] + 1, groups[("out", 0)][1][1], groups[("out", 1)][1][1]] + [first[("up", 1)] + 1 + 3 * i for i in range(5)]
    at0 += [first[("down", 0)] + i for i in (2, 5, 9, 13)]
    b = first[(0, "conv", 0)]
    at1 = [b + i for i in (3, 6, 9, 12, 16, 19, 22, 26, 29, 33, 36, 39)]
    ada_at = {c: (l, q) for l, at in enumerate((at0, at1)) for q, c in enumerate(at)}
    ada_work = {}
    for c, (l, q) in ada_at.items():
        for k in range(KD):
            ada_work.setdefault(c - 3 + 3 * k // KD, []).append((l * ADA_GROUPS + q, k))

    by_pool = set()
    for l in range(LAYERS):
        by_pool |= set(range(first[(l, "in", 0)], first[(l, "conv", 0)]))
    by_pool |= set(range(first[(1, "ffn", 0)], NCH, 2))
    low_done, made = [], {"lo_done_v": 0, "lo_done_p": 0}
    for c in range(NCH):
        name = "lo_done_p" if c in by_pool else "lo_done_v"
        made[name] += 1
        low_done.append((name, made[name]))

    pack, srcs = {}, [
        ("g_mix_pre", t["g_mix_pre"][0], KD), ("g_mlstm", t["g_mlstm_out"][0], MH), ("g_mix_post", t["g_mix_post"][0], KD),
        ("g_mlp_pre", t["g_mlp_pre"][0], KD), ("g_mlp_post", t["g_mlp_post"][0], KD), ("c", t["c_2"][0], KD),
        ("final", t["final_g_2"], KD)]
    for l in range(LAYERS):
        srcs += [(("norm1", l), t["norm1_g_2"][l], KD), (("norm2", l), t["norm2_g_2"][l], KD), (("subln", l), t["subln_g_2"][l], 1),
                 (("convb", l), t["dw_conv_b_2"][l], GT), (("lng", l), t["conv_ln_g_2"][l], GT), (("lnb", l), t["conv_ln_b_2"][l], GT)]
    NROW = 0
    for name, ap, tiles in srcs:
        pack[name] = (NROW, ap, tiles)
        NROW += tiles
    PARAM_DMAS = len(srcs) + 2
    NMOD = LAYERS * MODS

    landed, count = [], [0] * RING
    for c, (nk, parts) in enumerate(chunks):
        count[c % RING] += 16 * len(parts)
        landed.append(count[c % RING])

    with ExitStack() as ctx:
        def sb(name, shape, dt=F32, on=ctx):
            return on.enter_context(nc.sbuf_tensor(name, shape, dt))

        def ps(name, shape):
            return ctx.enter_context(nc.psum_tensor(name, shape, F32))

        sems = {}

        def sem(name):
            if name not in sems:
                sems[name] = nc.alloc_semaphore(name)
            return sems[name]

        mm = ps("mm", [P, 4, GF])
        pa = ps("pa", [P, GF])
        pv = [ps(f"pv{i}", [P, GF]) for i in range(3)]

        raw = sb("raw", [P, RING, CK, GF])
        hi = sb("hi", [P, RING, CK, GF], F32R)
        lo = sb("lo", [P, RING, CK, GF], F32R)
        ada_raw = sb("ada_raw", [P, ADA_RING, ADA_K, GF])
        ada_acc = sb("ada_acc", [P, 2, GF])
        cst = sb("cst", [P, C_ALL])
        x = sb("x", [P, KD, S])
        act_hi = sb("act_hi", [P, KD, S], F32R)
        act_lo = sb("act_lo", [P, KD, S], F32R)
        hf = sb("hf", [P, 4, S])
        sq = sb("sq", [P, KD, S])
        rstd = sb("rstd", [P, 2, S])
        tabs = sb("tabs", [P, 2, 2 * S])
        parT = sb("parT", [P, NROW])
        adabT = sb("adabT", [P, NMOD])
        modT = sb("modT", [P, NMOD])
        convw = sb("convw", [P, LAYERS * GT, TAPS])
        ca = sb("ca", [P, 2, KD])
        cols = sb("cols", [P, 44])
        small = sb("small", [P, 24])
        nlam = sb("nlam", [P, LAYERS])

        mixA = ExitStack()
        qk1 = sb("qk1", [P, KD, S], on=mixA)
        v1 = sb("v1", [P, TT, GF], on=mixA)
        early = ExitStack()
        xin = sb("xin", [P, TT, D], on=early)
        early.close()
        mqk = sb("mqk", [P, 4, S], on=mixA)
        mv = sb("mv", [P, TT, GF], on=mixA)
        mo = sb("mo", [P, 4, S], on=mixA)
        wg = sb("wg", [P, KD, 8], on=mixA)
        att = ExitStack()
        att_hi = sb("att_hi", [P, 4, S], F32R, on=att)
        att_lo = sb("att_lo", [P, 4, S], F32R, on=att)
        att.close()
        hng = sb("hng", [P, KD, S], on=mixA)
        gbias = sb("gbias", [4, 2], on=mixA)
        gate = sb("gate", [4, 8, S], on=mixA)
        acol = sb("acol", [P, TT, 4], on=mixA)
        sA = sb("sA", [P, 2, 3 * P], on=mixA)
        pA = sb("pA", [P, 2, 3 * P], on=mixA)
        ptA = sb("ptA", [P, 2, 3 * P], on=mixA)
        bcA = sb("bcA", [P, 2, 2 * S], on=mixA)
        emA = sb("emA", [P, 2, S], on=mixA)
        hmA = sb("hmA", [P, 2, S], on=mixA)
        rows = sb("rows", [P, P], on=mixA)
        adab = sb("adab", [P, P], on=mixA)
        cwr = sb("cwr", [P, LAYERS, GF], on=mixA)
        lamr = sb("lamr", [1, LAYERS * 2, 2, QK], on=mixA)
        lamp = sb("lamp", [1, LAYERS * 2, QK], on=mixA)
        lams = sb("lams", [1, 16], on=mixA)
        posi = sb("posi", [1, 2 * S], I32, on=mixA)
        posf = sb("posf", [1, 2 * S], on=mixA)
        mixA.close()
        mixB = ExitStack()
        qk2 = sb("qk2", [P, KD, S], on=mixB)
        v2 = sb("v2", [P, TT, GF], on=mixB)
        gates = sb("gates", [P, 16, S], on=mixB)
        cu = sb("cu", [P, GT, S + TAPS - 1], on=mixB)
        cacc = sb("cacc", [P, GT, S], on=mixB)
        csq = sb("csq", [P, GT, S], on=mixB)
        o_hi = sb("o_hi", [P, GT, S], F32R, on=mixB)
        o_lo = sb("o_lo", [P, GT, S], F32R, on=mixB)
        uc_hi = sb("uc_hi", [P, GT, S], F32R, on=mixB)
        uc_lo = sb("uc_lo", [P, GT, S], F32R, on=mixB)
        sB = sb("sB", [P, 2, 3 * P], on=mixB)
        pB = sb("pB", [P, 2, 3 * P], on=mixB)
        ptB = sb("ptB", [P, 3 * P], on=mixB)
        oB = sb("oB", [P, S], on=mixB)
        mixB.close()
        last = ExitStack()
        outf = sb("outf", [P, KD, S], on=last)
        outt = sb("outt", [P, TT, D], on=last)
        last.close()
        u_hi = sb("u_hi", [P, 32, S], F32R)
        u_lo = sb("u_lo", [P, 32, S], F32R)

        ident = cst[:, C_ID:C_ID + P]
        rot = cst[:, C_ROT:C_ROT + P]
        ones = cst[:, C_ONE:C_ONE + P]

        def pcols(name):
            at, _, tiles = pack[name]
            return parT[:, at:at + tiles]

        def banks(name):
            g = groups[name][0]
            return mm[:, 2 * (g % 2):2 * (g % 2) + 2, :]

        def tile_of(src, f):
            return src[:, f // 2, (f % 2) * S:(f % 2) * S + S]

        def freed(name):
            g = groups[name][0]
            return f"group_free{g % 2}", g // 2 + 1

        fill_at = {0: 0, 2: 1}
        ahead_of_norm = [("out", 1), ("down", 1)] + [(l, stage, 1) for l in range(LAYERS) for stage in ("out", "down")]

        todoA = [(("in", g), j) for g in (3, 4, 5) for j in range(2)]

        def todoB(l):
            return [((l, "in", g), j) for g in (5, 6, 7, 8) for j in range(2)]

        def out_chunks(l):
            return sorted(groups[(l, "out", 0)][1] + groups[(l, "out", 1)][1])

        block = ctx.enter_context(nc.Block())

        @block.sync
        def _(sp):
            for tt in range(TT):
                sp.dma_start(xin[:, tt, :], t["x"][0, tt * P:tt * P + P, :]).then_inc(sem("x_loaded"), 16)
            sp.dma_start(cst[:], consts).then_inc(sem("const_loaded"), 16)
            sp.dma_start(posi[0:1, 0:S], t["positions"]).then_inc(sem("pos_loaded"), 16)
            sp.dma_start(posi[0:1, S:2 * S], t["positions_2"]).then_inc(sem("pos_loaded"), 16)
            for c, (nk, parts) in enumerate(chunks):
                if c >= RING:
                    name, value = low_done[c - RING]
                    sp.wait_ge(sem(name), value)
                for at, w, src in parts:
                    sp.dma_start(raw[:, c % RING, 0:nk, at:at + w], src).then_inc(sem(f"raw_loaded{c % RING}"), 16)
            for i in range(4):
                sp.wait_ge(sem("out_ready"), i + 1)
                kh, tt = i // TT, i % TT
                f = slice(kh * GF, kh * GF + GF)
                sp.dma_start(out[0, tt * P:tt * P + P, f], outt[:, tt, f]).then_inc(sem("stored"), 16)
            sp.wait_ge(sem("stored"), 64)

        @block.tensor
        def _(pe):
            n = Tally()

            def bank(i):
                used = n.seen(f"bank{i}")
                n(f"bank{i}")
                if used:
                    pe.wait_ge(sem(f"bank{i}_free"), used)
                return pa if i == "a" else pv[i]

            def full(ins, i):
                ins.then_inc(sem(f"bank{i}_full"), 1)

            def wait(name, by=1):
                pe.wait_ge(sem(name), n(name, by))

            def tile_products(b0, slot, kk, k, tiles, a_hi, a_lo, ends):
                w_hi, w_lo = hi[:, slot], lo[:, slot]
                for f in tiles:
                    o = mm[:, b0 + f // 2, (f % 2) * S:(f % 2) * S + S]
                    fs = slice(f * P, f * P + P)
                    for i, (w, a) in enumerate(((w_hi, a_hi), (w_hi, a_lo), (w_lo, a_hi))):
                        ins = pe.matmul(o, w[:, kk, fs], a[:, k, :], start=(k == 0 and i == 0 and f % 2 == 0),
                                        stop=(ends and i == 2), skip_group_check=True)
                return ins

            def chunk(name, j, a_hi, a_lo, token_major=False, ready=None, per=1):
                g, ids = groups[name]
                c = ids[j]
                nk = chunks[c][0]
                if j == 0 and g >= 2:
                    pe.wait_ge(sem(f"group_free{g % 2}"), g // 2)
                pe.wait_ge(sem(low_done[c][0]), low_done[c][1])
                w_hi, w_lo = hi[:, c % RING], lo[:, c % RING]
                b0 = 2 * (g % 2)
                for kk in range(nk):
                    k = CK * j + kk
                    if ready and k % per == 0:
                        wait(ready)
                    ends = j == len(ids) - 1 and kk == nk - 1
                    if token_major:
                        for tt in range(TT):
                            tok = slice(tt * P, tt * P + P)
                            for i, (a, w) in enumerate(((a_hi, w_hi), (a_lo, w_hi), (a_hi, w_lo))):
                                ins = pe.matmul(mm[:, b0 + tt, :], a[:, k, tok], w[:, kk, :], start=(k == 0 and i == 0),
                                                stop=(ends and i == 2), skip_group_check=True)
                    elif not (name in ahead_of_norm and j == len(ids) - 1):
                        ins = tile_products(b0, c % RING, kk, k, range(GT), a_hi, a_lo, ends)
                if name in ahead_of_norm and j == len(ids) - 1:
                    for pair in range(2):
                        for kk in range(nk):
                            ins = tile_products(b0, c % RING, kk, CK * j + kk, (2 * pair, 2 * pair + 1), a_hi, a_lo, kk == nk - 1)
                        if pair == 0:
                            ins.then_inc(sem("half_done"), 1)
                ins.then_inc(sem("mm_done"), 1)
                if c in ada_at:
                    wait("ada_ready")
                    i = n.seen("ada_ready") - 1
                    full(pe.matmul(bank(2)[:], ones, ada_acc[:, i % 2, :], start=True, stop=True), 2)

            def product(name, a_hi, a_lo, **kw):
                for j in range(len(groups[name][1])):
                    chunk(name, j, a_hi, a_lo, **kw)

            def sum_squares():
                bank("a")
                for pair in range(KD // 2):
                    wait("sq_ready")
                    for k in (2 * pair, 2 * pair + 1):
                        ins = pe.matmul(pa[:, 0:S], ones, sq[:, k, :], start=(k == 0), stop=(k == KD - 1))
                full(ins, "a")

            def rope(qk):
                for name in ("q", "k"):
                    for j in range(2):
                        i = 2 * j
                        k = (0 if name == "q" else 4) + 2 * j
                        full(pe.matmul(bank(i)[:], rot, qk[:, k:k + 2, :], start=True, stop=True), i)

            def scores(qk, u):
                b = bank(0)
                r = slice(QK * (u % 2), QK * (u % 2) + QK)
                q, k = qk[r, u // 2, :], qk[r, 4 + u // 2, :]
                pe.matmul(b[:, 0:P], q[:, 0:P], k[:, 0:P], start=True, stop=True)
                full(pe.matmul(b[:, P:3 * P], q[:, P:S], k, start=True, stop=True), 0)

            turned = []

            def turn(p):
                wait("probs_ready")
                b = bank(1)
                turned.append(n.seen("bank1"))
                for i in range(3):
                    ins = pe.transpose(b[:, i * P:(i + 1) * P], p[:, i * P:(i + 1) * P], ident)
                full(ins, 1)

            def apply_v(pt, v, f0, width, r0, last):
                pe.wait_ge(sem("bank1_free"), turned.pop(0))
                b = bank(2) if r0 == 0 else pv[2]
                o = b[r0:r0 + width, :]
                pe.matmul(o[:, 0:S], v[:, 0, f0:f0 + width], pt[:, 0:S], start=True, stop=False, skip_group_check=True)
                ins = pe.matmul(o[:, P:S], v[:, 1, f0:f0 + width], pt[:, S:3 * P], start=False, stop=True, skip_group_check=True)
                if last:
                    full(ins, 2)

            def head_squares():
                wait("hsq_ready")
                full(pe.matmul(bank("a")[:, 0:S], ones, sq[:, 0, :], start=True, stop=True), "a")

            pe.wait_ge(sem("const_loaded"), 16)
            pe.wait_ge(sem("x_loaded"), 16 * TT)
            for j in range(4):
                i = 2 * (j % 2)
                b = bank(i)
                for a, k in enumerate((2 * j, 2 * j + 1)):
                    for tt in range(TT):
                        ins = pe.transpose(b[:, a * S + tt * P:a * S + tt * P + P], xin[:, tt, k * P:(k + 1) * P], ident)
                full(ins, i)
            pe.wait_ge(sem("params_loaded"), 16 * PARAM_DMAS)
            b = bank(0)
            pe.transpose(b[:, 0:NROW], rows[0:NROW, :], ident[0:NROW, 0:NROW])
            full(pe.transpose(b[:, P:P + NMOD], adab[0:NMOD, :], ident[0:NMOD, 0:NMOD]), 0)
            b = bank(2)
            for i in range(LAYERS * GT):
                ins = pe.transpose(b[:, 32 * i:32 * i + TAPS], cwr[0:TAPS, i // GT, (i % GT) * P:(i % GT + 1) * P], ident[0:TAPS, 0:TAPS])
            full(ins, 2)
            sum_squares()
            wait("positions_ready")
            full(pe.matmul(bank(0)[:], ones[0:1, :], posf[0:1, :], start=True, stop=True), 0)

            product(("in", 0), act_hi, act_lo, ready="act_ready")
            wait("lam_ready")
            full(pe.matmul(bank(2)[:, 0:LAYERS], ones[0:1, :], lams[0:1, 8:8 + LAYERS], start=True, stop=True), 2)
            product(("in", 1), act_hi, act_lo)
            chunk(("in", 2), 0, act_hi, act_lo, token_major=True)
            pe.wait_ge(sem(freed(("in", 0))[0]), freed(("in", 0))[1])
            pe.wait_ge(sem(freed(("in", 1))[0]), freed(("in", 1))[1])
            rope(qk1)
            chunk(("in", 2), 1, act_hi, act_lo, token_major=True)
            pe.wait_ge(sem("gate_weights_loaded"), 48)
            b = bank(2)
            for half in range(2):
                for k in range(KD):
                    ins = pe.matmul(b[0:4, half * S:half * S + S], wg[:, k, 4 * half:4 * half + 4], hng[:, k, :],
                                    start=(k == 0 and half == 0), stop=(k == KD - 1), skip_group_check=True)
            full(ins, 2)
            wait("rope_done", 4)
            pe.wait_ge(sem(freed(("in", 2))[0]), freed(("in", 2))[1])
            scores(qk1, 0)
            for i in range(UNITS + 1):
                if i < len(todoA):
                    name, j = todoA[i]
                    chunk(name, j, act_hi, act_lo, token_major=(name == ("in", 4)))
                if i + 1 < UNITS:
                    scores(qk1, i + 1)
                if i < UNITS:
                    turn(pA[:, i % 2, :])
                u = i - 1
                if u >= 0:
                    apply_v(ptA[:, u % 2, :], v1, u * QK, QK, QK * (u % 2), u % 2 == 1)

            wait("gate_rows_ready")
            b = bank(0)
            for tt in range(TT):
                ins = pe.transpose(b[:, 4 * tt:4 * tt + 4], gate[:, 5, tt * P:tt * P + P], ident[0:4, 0:4])
            full(ins, 0)
            for g in (3, 4, 5):
                pe.wait_ge(sem(freed(("in", g))[0]), freed(("in", g))[1])

            def m_scores(h):
                full(pe.matmul(bank(1)[:], ident[0:4, h:h + 1].to_broadcast([4, P]), gate[:, 2:4, :], start=True, stop=True), 1)
                b = bank(0)
                r = slice(QK * (h % 2), QK * (h % 2) + QK)
                q, k = mqk[r, h // 2, :], mqk[r, 2 + h // 2, :]
                pe.matmul(b[:, 0:S], k[:, 0:P], q, start=True, stop=True)
                full(pe.matmul(b[:, S:3 * P], k[:, P:S], q[:, P:S], start=True, stop=True), 0)

            def m_sums(h):
                wait("mweights_ready")
                b = bank(2)
                w = pA[:, h % 2, :]
                f = slice(h * P, (h + 1) * P)
                pe.matmul(b[:, 0:S], mv[:, 0, f], w[:, 0:S], start=True, stop=False, skip_group_check=True)
                pe.matmul(b[:, P:S], mv[:, 1, f], w[:, S:3 * P], start=False, stop=True, skip_group_check=True)
                pe.matmul(b[:, S:2 * S], ones, w[:, 0:S], start=False, stop=False, skip_group_check=True)
                full(pe.matmul(b[:, S + P:2 * S], ones, w[:, S:3 * P], start=False, stop=True, skip_group_check=True), 2)

            m_scores(0)
            for h in range(MH + 1):
                if h in fill_at:
                    chunk(("out", fill_at[h]), 0, att_hi, att_lo, ready=None if h else "act_ready")
                if h + 1 < MH:
                    m_scores(h + 1)
                if h < MH:
                    m_sums(h)
                if h:
                    head_squares()

            for half in range(2):
                chunk(("out", half), 1, act_hi, act_lo, ready=None if half else "act_ready")
            for _ in range(2):
                sum_squares()
            for g in range(8):
                product(("up", g), act_hi, act_lo, ready="act_ready" if g == 0 else None)
            product(("down", 0), u_hi, u_lo, ready="u_ready", per=4)
            product(("down", 1), u_hi, u_lo)
            for _ in range(2):
                sum_squares()

            for l in range(LAYERS):
                product((l, "in", 3), act_hi, act_lo, ready="act_ready")
                for g in (4, 0, 1):
                    product((l, "in", g), act_hi, act_lo)
                chunk((l, "in", 2), 0, act_hi, act_lo, token_major=True)
                for g in (0, 1):
                    pe.wait_ge(sem(freed((l, "in", g))[0]), freed((l, "in", g))[1])
                rope(qk2)
                chunk((l, "in", 2), 1, act_hi, act_lo, token_major=True)
                wait("rope_done", 4)
                scores(qk2, 0)
                for i in range(UNITS + 2):
                    if i < UNITS:
                        chunk(*todoB(l)[i], act_hi, act_lo)
                    else:
                        chunk((l, "conv", i - UNITS), 0, uc_hi, uc_lo, ready="uc_ready" if i == UNITS else None)
                    if i == CONV_END + 2:
                        wait("csq_ready")
                        b = bank("a")
                        for k in range(GT):
                            ins = pe.matmul(b[:, 0:S], ones, csq[:, k, :], start=(k == 0), stop=(k == GT - 1))
                        full(ins, "a")
                    if i + 1 < UNITS:
                        scores(qk2, i + 1)
                    if i == CONV_END + 1:
                        wait("conv_done", GT)
                        b = bank(2)
                        for k in range(GT):
                            ins = pe.matmul(b[:, 0:S], ones, cacc[:, k, :], start=(k == 0), stop=(k == GT - 1))
                        full(ins, 2)
                    if i % 2 == 0 and i >= 2:
                        if i == 2:
                            pe.wait_ge(sem(freed((l, "in", 2))[0]), freed((l, "in", 2))[1])
                        apply_v(ptB, v2, (i // 2 - 1) * P, P, 0, True)
                    if i % 2 == 1 and i < UNITS:
                        turn(pB[:, 1, :])
                    if i % 2 == 1 and i >= 3:
                        head_squares()
                product((l, "attn", 0), o_hi, o_lo, ready="o_ready")
                product((l, "attn", 1), o_hi, o_lo)
                for j in range(2):
                    for half in range(2):
                        chunk((l, "out", half), j, act_hi, act_lo, ready=None if half else "mixed_split", per=2)
                sum_squares()
                for g in range(11):
                    product((l, "ffn", g), act_hi, act_lo, ready="act_ready" if g == 0 else None)
                product((l, "down", 0), u_hi, u_lo, ready="u_ready", per=2)
                product((l, "down", 1), u_hi, u_lo)
                sum_squares()

            for kh in range(2):
                wait("outf_ready", 4)
                for tt in range(TT):
                    i = 2 * tt
                    b = bank(i)
                    for k in range(4):
                        ins = pe.transpose(b[:, k * P:(k + 1) * P], outf[:, 4 * kh + k, tt * P:tt * P + P], ident)
                    full(ins, i)

        @block.scalar
        def _(act):
            a = Own(act, sem, "act_step")
            n = Tally()

            def wait(name, by=1):
                act.wait_ge(sem(name), n(name, by))

            def full(i):
                wait(f"bank{i}_full")
                return pa if i == "a" else pv[i]

            def split(c):
                if c >= NCH:
                    return
                act.wait_ge(sem(f"raw_loaded{c % RING}"), landed[c])
                if c >= RING:
                    act.wait_ge(sem("mm_done"), c - RING + 1)
                nk = chunks[c][0]
                a(act.activation(hi[:, c % RING, 0:nk, :], raw[:, c % RING, 0:nk, :], ACT.Copy), "hi_done")

            def steps(name):
                for c in groups[name][1]:
                    split(c + LEAD)

            def complete(name):
                act.wait_ge(sem("mm_done"), groups[name][1][-1] + 1)
                return banks(name)

            def evacuate(name, dst, func=ACT.Copy, scale=1.0):
                a(act.activation(dst, complete(name), func, scale=scale), *freed(name))

            loaded = [None]

            def log_tables():
                if loaded[0] != "log":
                    act.preload_act_table_set("natural_log_exp_and_others")
                loaded[0] = "log"

            def other(func):
                loaded[0] = None
                return func

            def rstd_from(width, eps, slot):
                log_tables()
                b = full("a")
                a(act.activation(rstd[:, slot, :], b[:, 0:S], ACT.Ln, scale=1.0 / width, bias=small[:, eps:eps + 1]), "banka_free")
                a.settle()
                a(act.activation(rstd[:, slot, :], rstd[:, slot, :], ACT.Exp, scale=-0.5), "rstd_ready")

            def squares_of_x(ready="x_ready"):
                log_tables()
                for pair in range(KD // 2):
                    wait(ready)
                    k = slice(2 * pair, 2 * pair + 2)
                    a(act.activation(sq[:, k, :], x[:, k, :], ACT.Square), "sq_ready")

            def high_of_norm(src, shift=None):
                for k in range(KD):
                    wait("hf_ready")
                    bias = shift[:, k:k + 1] if shift is not None else 0.0
                    a(act.activation(act_hi[:, k, :], src(k), ACT.Identity, bias=bias), "act_hi_ready")

            def high(src, dst, ready, done, scale=1.0):
                wait(ready)
                a(act.activation(dst, src, ACT.Copy, scale=scale), done)

            def exps(u, s, p):
                wait("max_ready")
                i = u % 2
                for q, (lo_, hi_) in enumerate(((0, P), (P, 3 * P))):
                    a(act.activation(p[:, i, lo_:hi_], s[:, i, lo_:hi_], ACT.Exp, scale=-1.0, bias=small[:, 2 + 2 * i + q:3 + 2 * i + q],
                                     accum_out=small[:, 6 + 2 * i + q:7 + 2 * i + q]), "exp_done")

            def take_turned(pt):
                a(act.activation(pt, full(1)[:, 0:3 * P], ACT.Copy), "bank1_free")

            for name, (r, ap, tiles) in pack.items():
                act.dma_start(rows[r:r + tiles, :], ap.rearrange("(r p) -> r p", p=P)).then_inc(sem("params_loaded"), 16)
            act.dma_start(adab[0:NMOD, :], t["ada_b_2"].rearrange("l (r p) -> (l r) p", p=P)).then_inc(sem("params_loaded"), 16)
            act.dma_start(cwr[0:TAPS, :, :], t["dw_conv_w_2"].rearrange("l j o c -> j (l o) c")).then_inc(sem("params_loaded"), 16)

            squares_of_x("x_tiles_ready")
            split(0)
            wait("eps_ready")
            rstd_from(D, 0, 0)
            high_of_norm(lambda k: hng[:, k, :])
            split(1)
            wait("c_loaded")
            a(act.activation(ca[:, 0, :], pcols("c"), ACT.Exp, scale=-1.0), "c_exp_ready")
            wait("lam_dots_ready")
            a(act.activation(lams[0:1, 4:8], lams[0:1, 0:4], ACT.Exp), "lam_exps_ready")
            steps(("in", 0))
            evacuate(("in", 0), qk1[:, 0:4, :])
            steps(("in", 1))
            wait("angles_ready")
            a(act.activation(tabs[:, :, :], tabs[:, :, :], other(ACT.Sin)), "tables_ready")
            evacuate(("in", 1), qk1[:, 4:8, :])
            steps(("in", 2))
            evacuate(("in", 2), v1[:, :, :])
            log_tables()

            wait("gates_biased")
            a(act.activation(gate[:, 2, :], gate[:, 1, :], ACT.Abs))
            a.settle()
            a(act.activation(gate[:, 2, :], gate[:, 2, :], ACT.Exp, scale=-1.0))
            a.settle()
            a(act.activation(gate[:, 2, :], gate[:, 2, :], ACT.Ln, bias=1.0), "softplus_ready")

            exps(0, sA, pA)
            for i in range(UNITS + 1):
                if i < len(todoA):
                    name, j = todoA[i]
                    split(groups[name][1][j] + LEAD)
                if i + 1 < UNITS:
                    exps(i + 1, sA, pA)
                if i < UNITS:
                    take_turned(ptA[:, i % 2, :])
                if i < len(todoA) and j == 1:
                    if name[1] == 3:
                        evacuate(name, mqk[:, :, :])
                    elif name[1] == 4:
                        evacuate(name, mv[:, :, :])
                    else:
                        evacuate(name, mo[:, :, :], other(ACT.Tanh), 0.5)
                if i >= 2 and i % 2 == 0:
                    h = i // 2 - 1
                    high(hf[:, h % 2, :], att_hi[:, h, :], "of_ready", "act_hi_ready")

            def m_exps(h):
                a(act.activation(bcA[:, h % 2, :], full(1)[:], ACT.Copy), "bank1_free")
                wait("mexp_arg_ready")
                a(act.activation(sA[:, h % 2, :], sA[:, h % 2, :], ACT.Exp), "mexp_done")
                if h >= 2:
                    act.wait_ge(sem("hm_ready"), h - 1)
                a(act.activation(emA[:, h % 2, :], bcA[:, h % 2, S:2 * S], ACT.Exp), "mexp_done")

            def m_norm(h):
                wait("hm_ready")
                a(act.activation(sq[:, 0, :], hmA[:, h % 2, :], ACT.Square), "hsq_ready")
                rstd_from(P, 0, h % 2)
                high(hf[:, h % 2, :], act_hi[:, 4 + h, :], "of_ready", "act_hi_ready")

            m_exps(0)
            for h in range(MH + 1):
                if h in fill_at:
                    split(groups[("out", fill_at[h])][1][0] + LEAD)
                if h + 1 < MH:
                    m_exps(h + 1)
                if h:
                    m_norm(h - 1)

            def post_norm(stage):
                log_tables()
                src = complete((stage, 0))
                for b in range(2):
                    a(act.activation(sq[:, 2 * b:2 * b + 2, :], src[:, b, :].rearrange("p (a s) -> p a s", a=2), ACT.Square), "sq_ready")
                wait("half_done")
                src = banks((stage, 1))
                for b in range(2):
                    if b:
                        complete((stage, 1))
                    a(act.activation(sq[:, 4 + 2 * b:6 + 2 * b, :], src[:, b, :].rearrange("p (a s) -> p a s", a=2), ACT.Square), "sq_ready")
                rstd_from(D, 0, 0)

            for c in groups[("out", 0)][1][1:] + groups[("out", 1)][1][1:]:
                split(c + LEAD)
            post_norm("out")
            squares_of_x()
            rstd_from(D, 0, 1)
            high_of_norm(lambda k: hf[:, k % 4, :])
            for g in range(8):
                steps(("up", g))
                if g:
                    act.wait_ge(sem("u_hi_ready"), g)
                a(act.activation(sq[:, 0:4, :], complete(("up", g)), ACT.Relu), *freed(("up", g)))
                high(sq[:, 4:8, :], u_hi[:, 4 * g:4 * g + 4, :], "u_f32_ready", "u_hi_ready")
            steps(("down", 0))
            steps(("down", 1))
            post_norm("down")

            for l in range(LAYERS):
                squares_of_x()
                rstd_from(D, 0, 1)
                high_of_norm(lambda k: hf[:, k % 4, :], shift=modT[:, l * MODS:l * MODS + KD])
                steps((l, "in", 3))
                steps((l, "in", 4))
                evacuate((l, "in", 4), csq[:, :, :], other(ACT.Tanh), 0.5)
                for g in (0, 1):
                    steps((l, "in", g))
                    evacuate((l, "in", g), qk2[:, 4 * g:4 * g + 4, :])
                steps((l, "in", 2))
                evacuate((l, "in", 2), v2[:, :, :])
                exps(0, sB, pB)
                for i in range(UNITS + 2):
                    if i < UNITS:
                        name, j = todoB(l)[i]
                        split(groups[name][1][j] + LEAD)
                    else:
                        split(groups[(l, "conv", i - UNITS)][1][0] + LEAD)
                    if i + 1 < UNITS:
                        exps(i + 1, sB, pB)
                    if i == CONV_END + 1:
                        wait("centred")
                        a(act.activation(csq[:, :, :], cacc[:, :, :], ACT.Square), "csq_ready")
                    if i % 2 == 0 and i >= 2:
                        wait("o_f32_ready")
                        a(act.activation(sq[:, 0, :], oB[:], ACT.Square), "hsq_ready")
                    if i % 2 == 1 and i < UNITS:
                        take_turned(ptB[:])
                    if i == CONV_END + 2:
                        rstd_from(GF, 1, 1)
                        for k in range(GT + 1):
                            if k < GT:
                                wait("ln_ready")
                                a(act.activation(csq[:, k, :], cacc[:, k, :], other(ACT.Tanh), scale=0.5, bias=cols[:, 40 + k:41 + k]), "ln_tanh_ready")
                            if k:
                                high(csq[:, k - 1, :], uc_hi[:, k - 1, :], "uc_f32_ready", "uc_hi_ready", scale=0.5)
                    if i < UNITS and j == 1:
                        g = name[2] - 5
                        evacuate(name, gates[:, 4 * g:4 * g + 4, :], other(ACT.Tanh), 0.5)
                    if i % 2 == 1 and i >= 3:
                        h = (i - 3) // 2
                        rstd_from(P, 1, h % 2)
                        high(hf[:, h % 2, :], o_hi[:, h, :], "on_ready", "o_hi_ready")
                for half in range(2):
                    steps((l, "attn", half))
                    for pair in (2 * half, 2 * half + 1):
                        k = slice(2 * pair, 2 * pair + 2)
                        high(gates[:, k, :], act_hi[:, k, :], "mixed_ready", "mixed_hi_ready", scale=0.5)
                for c in out_chunks(l):
                    split(c + LEAD)
                squares_of_x()
                rstd_from(D, 0, 0)
                high_of_norm(lambda k: hf[:, k % 4, :], shift=modT[:, l * MODS + 3 * KD:l * MODS + 4 * KD])
                for g in range(11):
                    steps((l, "ffn", g))
                    a(act.activation(sq[:, 0:2, :], complete((l, "ffn", g))[:, 0, :], other(ACT.Tanh), scale=0.5), "silu_gate_ready")
                    high(sq[:, 4:6, :], u_hi[:, 2 * g:2 * g + 2, :], "u_f32_ready", "u_hi_ready")
                for half in range(2):
                    steps((l, "down", half))
            squares_of_x()
            rstd_from(D, 0, 1)

        @block.gpsimd
        def _(pool):
            p = Own(pool, sem, "pool_step")

            loads = LAYERS * ADA_GROUPS * KD // ADA_K

            def load(j):
                if j >= loads:
                    return
                i, k = j * ADA_K // KD, j * ADA_K % KD
                src = t["ada_w_2"][i // ADA_GROUPS, k * P:(k + ADA_K) * P, i % ADA_GROUPS * GF:(i % ADA_GROUPS + 1) * GF]
                pool.dma_start(ada_raw[:, j % ADA_RING], src.rearrange("(k p) f -> p k f", p=P)).then_inc(sem(f"ada_loaded{j % ADA_RING}"), 16)

            def ada(i, k):
                acc = ada_acc[:, i % 2, :]
                if k == 0 and i >= 2:
                    pool.wait_ge(sem("ada_reduced"), i - 1)
                j, kk = (i * KD + k) // ADA_K, k % ADA_K
                w = ada_raw[:, j % ADA_RING, kk, :]
                if kk == 0:
                    pool.wait_ge(sem(f"ada_loaded{j % ADA_RING}"), 16 * (j // ADA_RING + 1))
                p(pool.tensor_scalar(w if k else acc, w, ca[:, 1, k:k + 1], 0.0, ALU.mult, ALU.add))
                if k:
                    p.settle()
                    p(pool.tensor_tensor(acc, acc, w, ALU.add), "ada_ready" if k == KD - 1 else None)
                if kk == ADA_K - 1:
                    p.settle()
                    load(j + ADA_RING)

            def split(c):
                if c not in by_pool:
                    return
                pool.wait_ge(sem("hi_done"), c + 1)
                nk = chunks[c][0]
                p(pool.tensor_tensor(lo[:, c % RING, 0:nk, :], raw[:, c % RING, 0:nk, :], hi[:, c % RING, 0:nk, :].bitcast(F32),
                                     ALU.subtract), "lo_done_p")

            for j in range(ADA_RING):
                load(j)
            pairs = lamr[:].rearrange("o (l c) i d -> o l c i d", c=2)
            for i, name in enumerate(("lambda_q1_2", "lambda_k1_2", "lambda_q2_2", "lambda_k2_2")):
                for l in range(LAYERS):
                    pool.dma_start(pairs[0:1, l, i // 2, i % 2, :], t[name][l:l + 1, :]).then_inc(sem("lam_loaded"), 16)
            pool.dma_start(wg[:, :, :], t["w_in"][0, :, 3072:3080].rearrange("(k p) f -> p k f", p=P)).then_inc(sem("gate_weights_loaded"), 16)
            pool.dma_start(gbias[:, 0:1], t["b_igate"].rearrange("o h -> h o")).then_inc(sem("gate_weights_loaded"), 16)
            pool.dma_start(gbias[:, 1:2], t["b_fgate"].rearrange("o h -> h o")).then_inc(sem("gate_weights_loaded"), 16)
            pool.wait_ge(sem("c_ready"), 1)
            for c in range(NCH):
                split(c + LEAD)
                for i, k in ada_work.get(c, ()):
                    ada(i, k)

        @block.vector
        def _(dve):
            v = Own(dve, sem, "dve_step")
            n = Tally()

            def wait(name, by=1):
                dve.wait_ge(sem(name), n(name, by))

            def full(i):
                wait(f"bank{i}_full")
                return pv[i]

            def link(ins, name=None, value=None):
                v(ins, name, value)
                v.settle()

            def split(c):
                if c >= NCH or c in by_pool:
                    return
                dve.wait_ge(sem("hi_done"), c + 1)
                nk = chunks[c][0]
                v(dve.tensor_tensor(lo[:, c % RING, 0:nk, :], raw[:, c % RING, 0:nk, :], hi[:, c % RING, 0:nk, :].bitcast(F32),
                                    ALU.subtract), "lo_done_v")

            def ada_columns(c):
                if c not in ada_at:
                    return
                l, q = ada_at[c]
                b = full(2)
                m = hf[:, 0:2, :].rearrange("p a (b c) -> p (a b) c", b=2)
                link(dve.tensor_tensor(m, b[:].rearrange("p (f j) -> p f j", f=GT), ident.unsqueeze(1).to_broadcast([P, GT, P]), ALU.mult), "bank2_free")
                dve.sem_inc(sem("ada_reduced"), 1)
                link(dve.tensor_reduce(small[:, 10:14], m, AX.X, ALU.add))
                mc = slice(l * MODS + q * GT, l * MODS + q * GT + GT)
                link(dve.tensor_tensor(modT[:, mc], small[:, 10:14], adabT[:, mc], ALU.add))

            def steps(name):
                for c in groups[name][1]:
                    split(c + LEAD)
                    ada_columns(c)

            def complete(name):
                dve.wait_ge(sem("mm_done"), groups[name][1][-1] + 1)
                return banks(name)

            def low(src, d_hi, d_lo, hi_done, done, scale=None, shift=None):
                wait(hi_done)
                h = d_hi.bitcast(F32)
                if scale is not None:
                    ins = dve.scalar_tensor_tensor(out=d_lo, in0=src, scalar=scale, in1=h, op0=ALU.mult, op1=ALU.subtract)
                elif shift is not None:
                    ins = dve.scalar_tensor_tensor(out=d_lo, in0=src, scalar=shift, in1=h, op0=ALU.add, op1=ALU.subtract)
                else:
                    ins = dve.tensor_tensor(d_lo, src, h, ALU.subtract)
                v(ins, done)

            def normalise(gain, slot, dst, shift=None):
                wait("rstd_ready")

                def low_part(k):
                    low(dst(k), act_hi[:, k, :], act_lo[:, k, :], "act_hi_ready", "act_ready",
                        shift=shift[:, k:k + 1] if shift is not None else None)

                for k in range(KD):
                    if k >= 4:
                        v.settle()
                    v(dve.scalar_tensor_tensor(out=dst(k), in0=x[:, k, :], scalar=gain[:, k:k + 1], in1=rstd[:, slot, :],
                                               op0=ALU.mult, op1=ALU.mult), "hf_ready")
                    if k >= 2:
                        low_part(k - 2)
                low_part(KD - 2)
                low_part(KD - 1)
                v.settle()

            def conv_work(l):
                for j in range(TAPS):
                    for k in range(GT):
                        w = convw[:, GT * l + k, j:j + 1]
                        src = cu[:, k, j:j + S]
                        name = "conv_done" if j == TAPS - 1 else f"conv_step{k}"
                        if j == 0:
                            v(dve.tensor_scalar(cacc[:, k, :], src, w, pcols(("convb", l))[:, k:k + 1], ALU.mult, ALU.add), name)
                        else:
                            dve.wait_ge(sem(f"conv_step{k}"), v.n.seen(f"conv_step{k}"))
                            v(dve.scalar_tensor_tensor(out=cacc[:, k, :], in0=src, scalar=w, in1=cacc[:, k, :], op0=ALU.mult, op1=ALU.add), name)
                        yield

            def softmax_max(u, s):
                b = full(0)
                i = u % 2
                for q, (lo_, hi_) in enumerate(((0, P), (P, 3 * P))):
                    v(dve.tensor_tensor_reduce(out=s[:, i, lo_:hi_], in0=b[:, lo_:hi_], in1=cst[:, C_ADD + lo_:C_ADD + hi_], scale=-SCALE,
                                               scalar=FAR, op0=ALU.add, op1=ALU.min, accum_out=small[:, 2 + 2 * i + q:3 + 2 * i + q]),
                      "bank0_free" if q else None)
                v.settle()
                dve.sem_inc(sem("max_ready"), 1)

            def rope(qk, blk):
                for j in range(4):
                    i = 2 * (j % 2)
                    b = full(i)
                    z = hf[:, 0:2, :]
                    k = slice(2 * j, 2 * j + 2)
                    sn = tabs[:, blk, 0:S].unsqueeze(1).to_broadcast([P, 2, S])
                    cs = tabs[:, blk, S:2 * S].unsqueeze(1).to_broadcast([P, 2, S])
                    v(dve.tensor_tensor(z, b[:].rearrange("p (a s) -> p a s", a=2), sn, ALU.mult), f"bank{i}_free")
                    link(dve.tensor_tensor(qk[:, k, :], qk[:, k, :], cs, ALU.mult))
                    link(dve.tensor_tensor(qk[:, k, :], qk[:, k, :], z, ALU.add), "rope_done")

            def reduce_angles(i, ang):
                tmp, r = hf[:, 0, :], hf[:, 1, :]
                link(dve.tensor_scalar(tmp, ang, 1.0 / (2.0 * np.pi), MAGIC, ALU.mult, ALU.add))
                link(dve.tensor_scalar(tmp, tmp, MAGIC, None, ALU.subtract))
                link(dve.scalar_tensor_tensor(out=r, in0=tmp, scalar=-TWO_PI[0], in1=ang, op0=ALU.mult, op1=ALU.add))
                link(dve.scalar_tensor_tensor(out=r, in0=tmp, scalar=-TWO_PI[1], in1=r, op0=ALU.mult, op1=ALU.add))
                link(dve.scalar_tensor_tensor(out=r, in0=tmp, scalar=-TWO_PI[2], in1=r, op0=ALU.mult, op1=ALU.add))
                link(dve.tensor_scalar(tabs[:, i, 0:S], r, BEFORE_PI, -BEFORE_PI, ALU.min, ALU.max))
                link(dve.scalar_tensor_tensor(out=r, in0=tabs[:, i, 0:S], scalar=-1.0, in1=tabs[:, i, 0:S], op0=ALU.mult, op1=ALU.max))
                link(dve.tensor_scalar(tabs[:, i, S:2 * S], r, -1.0, PI / 2, ALU.mult, ALU.add), "angles_ready" if i else None)

            v(dve.memset(small[:, 0:1], EPS))
            v(dve.memset(small[:, 1:2], EPS_SUB), "eps_ready")
            for j in range(4):
                i = 2 * (j % 2)
                b = full(i)
                v(dve.tensor_copy(x[:, 2 * j:2 * j + 2, :], b[:].rearrange("p (a s) -> p a s", a=2)), f"bank{i}_free")
                v.settle()
                dve.sem_inc(sem("x_tiles_ready"), 1)
            wait("pos_loaded", 32)
            v(dve.tensor_copy(posf[0:1, :], posi[0:1, :]), "positions_ready")
            b = full(0)
            v(dve.tensor_copy(parT[:], b[:, 0:NROW]))
            link(dve.tensor_copy(adabT[:], b[:, P:P + NMOD]), "bank0_free")
            dve.sem_inc(sem("c_loaded"), 1)
            v(dve.tensor_scalar(convw[:], full(2)[:, 0:32 * LAYERS * GT].rearrange("p (i j) -> p i j", j=32)[:, :, 0:TAPS], 0.5, None, ALU.mult), "bank2_free")
            split(0)
            normalise(pcols("g_mix_pre"), 0, lambda k: hng[:, k, :])
            split(1)
            wait("c_exp_ready")
            link(dve.tensor_scalar(ca[:, 0, :], ca[:, 0, :], 1.0, None, ALU.add))
            link(dve.reciprocal(ca[:, 0, :], ca[:, 0, :]))
            link(dve.tensor_tensor(ca[:, 1, :], ca[:, 0, :], pcols("c"), ALU.mult), "c_ready")
            wait("lam_loaded", 16 * 4 * LAYERS)
            link(dve.tensor_tensor(lamp[0:1, :, :], lamr[0:1, :, 0, :], lamr[0:1, :, 1, :], ALU.mult))
            v(dve.tensor_reduce(lams[0:1, 0:4], lamp[0:1, :, :], AX.X, ALU.add), "lam_dots_ready")
            v(dve.tensor_scalar(cols[:, 32:36], pcols("g_mlstm"), 0.5, None, ALU.mult))
            for l in range(LAYERS):
                v(dve.tensor_scalar(cols[:, 36 + l:37 + l], pcols(("subln", l)), 1.0 - LAMBDA_INIT[l], None, ALU.mult))
            steps(("in", 0))
            wait("lam_exps_ready")
            e = lams[0:1, 4:8].rearrange("o (l c) -> o l c", c=2)
            link(dve.tensor_tensor(lams[0:1, 8:10], e[:, :, 1], e[:, :, 0], ALU.subtract))
            link(dve.tensor_scalar(lams[0:1, 8:9], lams[0:1, 8:9], -LAMBDA_INIT[0], None, ALU.add))
            v(dve.tensor_scalar(lams[0:1, 9:10], lams[0:1, 9:10], -LAMBDA_INIT[1], None, ALU.add), "lam_ready")
            b = full(0)
            dve.wait_ge(sem("const_loaded"), 16)
            link(dve.tensor_scalar(hf[:, 2:4, :], b[:].rearrange("p (a s) -> p a s", a=2), cst[:, C_FREQ:C_FREQ + 1], None, ALU.mult), "bank0_free")
            reduce_angles(0, hf[:, 2, :])
            reduce_angles(1, hf[:, 3, :])
            steps(("in", 1))
            link(dve.tensor_copy(nlam[:], full(2)[:, 0:LAYERS]), "bank2_free")
            wait("tables_ready")
            for c in groups[("in", 2)][1]:
                split(c + LEAD)
                if c == groups[("in", 2)][1][0]:
                    rope(qk1, 0)
                ada_columns(c)

            b = full(2)
            wait("gate_weights_loaded", 48)
            v(dve.tensor_scalar(gate[:, 0, :], b[0:4, 0:S], gbias[:, 0:1], None, ALU.add))
            v(dve.tensor_scalar(gate[:, 1, :], b[0:4, S:2 * S], gbias[:, 1:2], None, ALU.add), "bank2_free")
            v.settle()
            dve.sem_inc(sem("gates_biased"), 1)
            link(dve.memset(gate[:, 7, :], 0.0))

            def gate_rows():
                wait("softplus_ready")
                link(dve.scalar_tensor_tensor(out=gate[:, 3, :], in0=gate[:, 1, :], scalar=0.0, in1=gate[:, 2, :], op0=ALU.min, op1=ALU.subtract))
                link(dve.tensor_tensor_scan(gate[:, 4, :], gate[:, 3, :], gate[:, 7, :], 0.0, ALU.add, ALU.add))
                link(dve.tensor_tensor(gate[:, 5, :], gate[:, 0, :], gate[:, 4, :], ALU.subtract))
                link(dve.tensor_tensor_scan(gate[:, 6, :], gate[:, 5, :], gate[:, 5, :], 0.0, ALU.max, ALU.max))
                link(dve.tensor_scalar(gate[:, 2, :], gate[:, 6, :], -1.0, None, ALU.mult))
                link(dve.tensor_tensor(gate[:, 3, :], gate[:, 2, :], gate[:, 4, :], ALU.subtract), "gate_rows_ready")

            def probs(u, p):
                i = u % 2
                wait("exp_done", 2)
                r = small[:, 14 + 2 * i:16 + 2 * i]
                link(dve.reciprocal(r, small[:, 6 + 2 * i:8 + 2 * i]))
                v(dve.tensor_scalar(p[:, i, 0:P], p[:, i, 0:P], r[:, 0:1], None, ALU.mult))
                v(dve.tensor_scalar(p[:, i, P:3 * P], p[:, i, P:3 * P], r[:, 1:2], None, ALU.mult), "probs_ready")

            softmax_max(0, sA)
            gate_rows()
            for i in range(UNITS + 1):
                if i < len(todoA):
                    name, j = todoA[i]
                    split(groups[name][1][j] + LEAD)
                if i < UNITS:
                    probs(i, pA)
                if i + 1 < UNITS:
                    softmax_max(i + 1, sA)
                if i >= 2 and i % 2 == 0:
                    h = i // 2 - 1
                    v(dve.tensor_copy(hf[:, h % 2, :], full(2)[:, 0:S]), "bank2_free")
                    v.settle()
                    dve.sem_inc(sem("of_ready"), 1)
                    low(hf[:, h % 2, :], att_hi[:, h, :], att_lo[:, h, :], "act_hi_ready", "act_ready")
            link(dve.tensor_copy(acol[:].rearrange("p t h -> p (t h)"), full(0)[:, 0:8]), "bank0_free")

            def m_args(h):
                dve.wait_ge(sem("bank1_free"), UNITS + h + 1)
                i = h % 2
                v(dve.tensor_scalar(sA[:, i, 0:S], bcA[:, i, 0:S], acol[:, 0, h:h + 1], 0.0, ALU.add, ALU.min))
                v(dve.tensor_scalar(sA[:, i, S:3 * P], bcA[:, i, P:S], acol[:, 1, h:h + 1], 0.0, ALU.add, ALU.min), "mexp_arg_ready")

            def m_weights(h):
                i = h % 2
                wait("mexp_done", 2)
                link(dve.tensor_tensor(sA[:, i, :], sA[:, i, :], cst[:, C_MUL:C_MUL + 3 * P], ALU.mult))
                link(dve.scalar_tensor_tensor(out=pA[:, i, :], in0=full(0)[:, 0:3 * P], scalar=SCALE, in1=sA[:, i, :],
                                              op0=ALU.mult, op1=ALU.mult), "bank0_free")
                dve.sem_inc(sem("mweights_ready"), 1)

            def m_out(h):
                i = h % 2
                b = full(2)
                d = hf[:, 2 + i, :]
                link(dve.tensor_tensor(d, b[:, S:2 * S], emA[:, i, :], ALU.max))
                link(dve.scalar_tensor_tensor(out=d, in0=b[:, S:2 * S], scalar=-1.0, in1=d, op0=ALU.mult, op1=ALU.max))
                link(dve.reciprocal(d, d))
                link(dve.tensor_tensor(hmA[:, i, :], b[:, 0:S], d, ALU.mult), "bank2_free")
                dve.sem_inc(sem("hm_ready"), 1)

            def m_final(h):
                i = h % 2
                wait("rstd_ready")
                link(dve.scalar_tensor_tensor(out=hf[:, 2 + i, :], in0=hmA[:, i, :], scalar=cols[:, 32 + h:33 + h], in1=rstd[:, i, :],
                                              op0=ALU.mult, op1=ALU.mult))
                v(dve.scalar_tensor_tensor(out=hf[:, i, :], in0=mo[:, h, :], scalar=1.0, in1=hf[:, 2 + i, :], op0=ALU.add, op1=ALU.mult), "of_ready", MH + h + 1)
                low(hf[:, i, :], act_hi[:, 4 + h, :], act_lo[:, 4 + h, :], "act_hi_ready", "act_ready")
                v.settle()

            m_args(0)
            m_weights(0)
            for h in range(MH + 1):
                if h in fill_at:
                    split(groups[("out", fill_at[h])][1][0] + LEAD)
                if h + 1 < MH:
                    m_args(h + 1)
                if h < MH:
                    m_out(h)
                if h + 1 < MH:
                    m_weights(h + 1)
                if h:
                    m_final(h - 1)

            def post_norm(stage, gain):
                wait("rstd_ready")
                n("half_done")
                for pair in range(KD // 2):
                    name = (stage, pair // 2)
                    src = complete(name)
                    for a in range(2):
                        k = 2 * pair + a
                        f = k % GT
                        ins = dve.scalar_tensor_tensor(out=hf[:, f, :], in0=tile_of(src, f), scalar=gain[:, k:k + 1], in1=rstd[:, 0, :],
                                                       op0=ALU.mult, op1=ALU.mult)
                        v(ins, *(freed(name) if f == GT - 1 else ()))
                    v.settle()
                    k, f = slice(2 * pair, 2 * pair + 2), slice(2 * (pair % 2), 2 * (pair % 2) + 2)
                    link(dve.tensor_tensor(x[:, k, :], x[:, k, :], hf[:, f, :], ALU.add), "x_ready")

            for c in groups[("out", 0)][1][1:] + groups[("out", 1)][1][1:]:
                split(c + LEAD)
                ada_columns(c)
            post_norm("out", pcols("g_mix_post"))
            normalise(pcols("g_mlp_pre"), 1, lambda k: hf[:, k % 4, :])
            for g in range(8):
                steps(("up", g))
                name, value = freed(("up", g))
                dve.wait_ge(sem(name), value)
                v(dve.tensor_tensor(sq[:, 4:8, :], sq[:, 0:4, :], sq[:, 0:4, :], ALU.mult), "u_f32_ready")
                k = slice(4 * g, 4 * g + 4)
                low(sq[:, 4:8, :], u_hi[:, k, :], u_lo[:, k, :], "u_hi_ready", "u_ready")
                v.settle()
            steps(("down", 0))
            steps(("down", 1))
            post_norm("down", pcols("g_mlp_post"))

            def update(name, half, gain):
                src = banks(name)
                for f in range(GT):
                    if half and f == 0:
                        wait("half_done")
                    elif f == (2 if half else 0):
                        complete(name)
                    k = GT * half + f
                    ins = dve.scalar_tensor_tensor(out=x[:, k, :], in0=tile_of(src, f), scalar=gain[:, k:k + 1], in1=x[:, k, :],
                                                   op0=ALU.mult, op1=ALU.add)
                    v(ins, *(freed(name) if f == GT - 1 else ()))
                    if f % 2:
                        v.settle()
                        dve.sem_inc(sem("x_ready"), 1)

            for l in range(LAYERS):
                mod = [modT[:, l * MODS + i * KD:l * MODS + (i + 1) * KD] for i in range(6)]
                gain1, gate1, gain2, gate2 = (cols[:, 8 * i:8 * i + 8] for i in range(4))
                v(dve.scalar_tensor_tensor(out=gain1, in0=mod[1], scalar=1.0, in1=pcols(("norm1", l)), op0=ALU.add, op1=ALU.mult))
                v(dve.tensor_scalar(gate1, mod[2], 1.0, None, ALU.add))
                v(dve.scalar_tensor_tensor(out=gain2, in0=mod[4], scalar=1.0, in1=pcols(("norm2", l)), op0=ALU.add, op1=ALU.mult))
                link(dve.tensor_scalar(gate2, mod[5], 1.0, None, ALU.add))
                link(dve.tensor_scalar(cols[:, 40:44], pcols(("lnb", l)), 0.5, None, ALU.mult))
                normalise(gain1, 1, lambda k: hf[:, k % 4, :], shift=mod[0])
                steps((l, "in", 3))
                steps((l, "in", 4))
                link(dve.memset(cu[:, :, 0:TAPS - 1], 0.0))
                name, value = freed((l, "in", 4))
                dve.wait_ge(sem(name), value)
                src = complete((l, "in", 3)).rearrange("p b (a s) -> p (b a) s", a=2)
                link(dve.scalar_tensor_tensor(out=cu[:, :, TAPS - 1:], in0=csq[:], scalar=1.0, in1=src, op0=ALU.add, op1=ALU.mult), *freed((l, "in", 3)))
                conv = conv_work(l)

                def taps(count):
                    for _ in range(count):
                        next(conv, None)

                for c in groups[(l, "in", 0)][1] + groups[(l, "in", 1)][1]:
                    split(c + LEAD)
                    taps(13)
                first_v, second_v = groups[(l, "in", 2)][1]
                split(first_v + LEAD)
                taps(6)
                rope(qk2, 1)
                split(second_v + LEAD)
                taps(10)
                softmax_max(0, sB)

                def low_of_head(h):
                    low(hf[:, h % 2, :], o_hi[:, h, :], o_lo[:, h, :], "o_hi_ready", "o_ready")
                    v.settle()

                def gate_branch(branch, half):
                    at = (8 if branch == "conv" else 0) + 4 * half
                    g = gates[:, at:at + 4, :]
                    link(dve.scalar_tensor_tensor(out=g, in0=g, scalar=1.0, in1=complete((l, branch, half)).rearrange("p b (a s) -> p (b a) s", a=2),
                                                  op0=ALU.add, op1=ALU.mult), *freed((l, branch, half)))

                for i in range(UNITS + 2):
                    if i < UNITS:
                        name, j = todoB(l)[i]
                        split(groups[name][1][j] + LEAD)
                        c = i % 2
                        wait("exp_done", 2)
                        r = small[:, 14 + 2 * c:16 + 2 * c]
                        link(dve.reciprocal(r, small[:, 6 + 2 * c:8 + 2 * c]))
                        if c:
                            link(dve.tensor_scalar(r, r, nlam[:, l:l + 1], None, ALU.mult))
                        for q, (lo_, hi_) in enumerate(((0, P), (P, 3 * P))):
                            pc = pB[:, c, lo_:hi_]
                            if c == 0:
                                v(dve.tensor_scalar(pc, pc, r[:, q:q + 1], None, ALU.mult))
                            else:
                                v(dve.scalar_tensor_tensor(out=pc, in0=pc, scalar=r[:, q:q + 1], in1=pB[:, 0, lo_:hi_], op0=ALU.mult, op1=ALU.add),
                                  "probs_ready" if q else None)
                        v.settle()
                    else:
                        c = groups[(l, "conv", i - UNITS)][1][0]
                        split(c + LEAD)
                        ada_columns(c)
                    if i + 1 < UNITS:
                        softmax_max(i + 1, sB)
                    if i == CONV_END + 1:
                        link(dve.tensor_scalar(hf[:, 2, :], full(2)[:, 0:S], 1.0 / GF, None, ALU.mult), "bank2_free")
                        link(dve.tensor_tensor(cacc[:], cacc[:], hf[:, 2:3, :].to_broadcast([P, GT, S]), ALU.subtract), "centred")
                    if i % 2 == 0 and i >= 2:
                        if i >= 4:
                            low_of_head(i // 2 - 2)
                        link(dve.tensor_copy(oB[:], full(2)[:, 0:S]), "bank2_free")
                        dve.sem_inc(sem("o_f32_ready"), 1)
                    if i <= CONV_END:
                        taps(TAPS_PER_UNIT)
                    if i == CONV_END + 2:
                        wait("rstd_ready")
                        for k in range(GT):
                            v(dve.scalar_tensor_tensor(out=cacc[:, k, :], in0=cacc[:, k, :], scalar=pcols(("lng", l))[:, k:k + 1], in1=rstd[:, 1, :],
                                                       op0=ALU.mult, op1=ALU.mult), "ln_ready")
                        for k in range(GT + 1):
                            if k < GT:
                                wait("ln_tanh_ready")
                                link(dve.tensor_scalar(cacc[:, k, :], cacc[:, k, :], pcols(("lnb", l))[:, k:k + 1], None, ALU.add))
                                v(dve.scalar_tensor_tensor(out=csq[:, k, :], in0=csq[:, k, :], scalar=1.0, in1=cacc[:, k, :], op0=ALU.add, op1=ALU.mult),
                                  "uc_f32_ready")
                            if k:
                                low(csq[:, k - 1, :], uc_hi[:, k - 1, :], uc_lo[:, k - 1, :], "uc_hi_ready", "uc_ready", scale=0.5)
                        v.settle()
                    if i % 2 == 1 and i >= 3:
                        h = (i - 3) // 2
                        wait("rstd_ready")
                        v(dve.scalar_tensor_tensor(out=hf[:, h % 2, :], in0=oB[:], scalar=cols[:, 36 + l:37 + l], in1=rstd[:, h % 2, :],
                                                   op0=ALU.mult, op1=ALU.mult), "on_ready")
                    if i >= UNITS:
                        gate_branch("conv", i - UNITS)
                low_of_head(ATTN_HEADS - 1)
                for half in range(2):
                    steps((l, "attn", half))
                    gate_branch("attn", half)
                    pairs = [slice(2 * pair, 2 * pair + 2) for pair in (2 * half, 2 * half + 1)]
                    for k in pairs:
                        v(dve.tensor_tensor(gates[:, k, :], gates[:, k, :], gates[:, 8 + k.start:8 + k.stop, :], ALU.add), "mixed_ready")
                    for k in pairs:
                        low(gates[:, k, :], act_hi[:, k, :], act_lo[:, k, :], "mixed_hi_ready", "mixed_split", scale=0.5)
                for c in out_chunks(l):
                    split(c + LEAD)
                    ada_columns(c)
                for half in range(2):
                    update((l, "out", half), half, gate1)
                normalise(gain2, 0, lambda k: hf[:, k % 4, :], shift=mod[3])
                for g in range(11):
                    steps((l, "ffn", g))
                    src = complete((l, "ffn", g))
                    wait("silu_gate_ready")
                    link(dve.scalar_tensor_tensor(out=sq[:, 2:4, :], in0=sq[:, 0:2, :], scalar=1.0, in1=src[:, 0, :].rearrange("p (a s) -> p a s", a=2),
                                                  op0=ALU.add, op1=ALU.mult))
                    link(dve.scalar_tensor_tensor(out=sq[:, 4:6, :], in0=sq[:, 2:4, :], scalar=0.5, in1=src[:, 1, :].rearrange("p (a s) -> p a s", a=2),
                                                  op0=ALU.mult, op1=ALU.mult), *freed((l, "ffn", g)))
                    dve.sem_inc(sem("u_f32_ready"), 1)
                    k = slice(2 * g, 2 * g + 2)
                    low(sq[:, 4:6, :], u_hi[:, k, :], u_lo[:, k, :], "u_hi_ready", "u_ready")
                    v.settle()
                for half in range(2):
                    steps((l, "down", half))
                    update((l, "down", half), half, gate2)
            wait("rstd_ready")
            gain = pcols("final")
            for k in range(KD):
                v(dve.scalar_tensor_tensor(out=outf[:, k, :], in0=x[:, k, :], scalar=gain[:, k:k + 1], in1=rstd[:, 1, :],
                                           op0=ALU.mult, op1=ALU.mult), "outf_ready")
            for kh in range(2):
                for tt in range(TT):
                    link(dve.tensor_copy(outt[:, tt, kh * GF:kh * GF + GF], full(2 * tt)[:]), f"bank{2 * tt}_free")
                    dve.sem_inc(sem("out_ready"), 1)


_INS = ["x", "positions", "g_mix_pre", "w_in", "b_igate", "b_fgate", "g_mlstm_out", "w_out", "g_mix_post", "g_mlp_pre",
        "w_up", "w_down", "g_mlp_post", "c_2", "positions_2", "ada_w_2", "ada_b_2", "norm1_g_2", "w_in_2",
        "lambda_q1_2", "lambda_k1_2", "lambda_q2_2", "lambda_k2_2", "subln_g_2", "w_attn_o_2", "dw_conv_w_2",
        "dw_conv_b_2", "conv_ln_g_2", "conv_ln_b_2", "w_conv_o_2", "w_out_2", "norm2_g_2", "w_ffn_in_2",
        "w_ffn_out_2", "final_g_2"]


def kernel(**inputs):
    import numpy as _np
    import concourse.bacc as _bacc
    from concourse import mybir as _mybir
    from concourse.bass_utils import run_bass_kernel_spmd as _run

    nc = _bacc.Bacc("TRN2", target_bir_lowering=False, num_devices=1)
    arrays, aps = {}, {}
    for name in _INS:
        a = _np.ascontiguousarray(inputs[name])
        arrays[f"in_{name}_dram"] = a
        aps[name] = nc.dram_tensor(f"in_{name}_dram", a.shape, _mybir.dt.from_np(a.dtype), kind="ExternalInput").ap()
    c = constants()
    arrays["constants_dram"] = c
    consts = nc.dram_tensor("constants_dram", c.shape, _mybir.dt.float32, kind="ExternalInput").ap()
    out = nc.dram_tensor("out_0_dram", (1, S, D), _mybir.dt.float32, kind="ExternalOutput").ap()
    two_blocks(nc, aps, consts, out)
    r = _run(nc, [arrays], core_ids=[0])
    return r.results[0]["out_0_dram"]
```

```python
from contextlib import ExitStack

import numpy as np

import concourse.bass as bass
from concourse import mybir

F32 = mybir.dt.float32
F32R = mybir.dt.float32r
I32 = mybir.dt.int32
ALU = mybir.AluOpType
ACT = mybir.ActivationFunctionType
AX = mybir.AxisListType

P = 128
S = 256
TT = S // P
D = 1024
KD = D // P
GF = 512
GT = GF // P
CK = 4
RING = 3
LEAD = 2
EPS = 1e-6
EPS_SUB = 1e-5
QK = 64
SCALE = QK ** -0.5
ATTN_HEADS = 4
FAR = 3e38
TAPS_BEFORE, ROPE_AT, TAPS_AFTER = (13, 13, 9, 12, 7, 12), ("", "", "q", "", "k", ""), (0, 0, 2, 0, 2, 0)
TAPS_PER_UNIT = 9
CONV_END = 5
UNITS = 8
TAPS = 31
MH = 4
LAYERS = 2
MODS = 48
ADA_GROUPS = MODS // GT
ADA_K = 2
ADA_RING = 4
ADA_P = KD // ADA_K
LAMBDA_INIT = [0.8 - 0.6 * float(np.exp(-0.3 * l)) for l in range(LAYERS)]
MAGIC = 1.5 * 2.0 ** 23
TWO_PI = (6.28125, 0.0019350051879882812, 3.0199157663446332e-07)
PI = float(np.float32(np.pi))
BEFORE_PI = 3.1415925

C_ID, C_ROT, C_ONE = 0, P, 2 * P
C_ADD, C_MUL, C_FREQ = 3 * P, 6 * P, 9 * P
C_ALL = 9 * P + 1


def constants():
    c = np.zeros((P, C_ALL), np.float32)
    i = np.arange(P)
    c[:, C_ID:C_ID + P] = np.eye(P)
    half = QK // 8
    freq = 500000.0 ** (-np.arange(0, 2 * half, 2, dtype=np.float32) / np.float32(2 * half))
    for p in range(P):
        d = p % QK
        if d < half:
            c[p + half, C_ROT + p] = -1.0
        elif d < 2 * half:
            c[p - half, C_ROT + p] = 1.0
        if d < 2 * half:
            c[p, C_FREQ] = freq[d % half]
    c[:, C_ONE:C_ONE + P] = 1.0
    tri = np.where(i[None, :] <= i[:, None], 0.0, -1e30)
    c[:, C_ADD:C_ADD + P] = tri
    c[:, C_ADD + 2 * P:C_ADD + 3 * P] = tri
    up = (i[:, None] <= i[None, :]).astype(np.float32)
    c[:, C_MUL:C_MUL + P] = up
    c[:, C_MUL + P:C_MUL + 2 * P] = 1.0
    c[:, C_MUL + 2 * P:C_MUL + 3 * P] = up
    return c


class Tally:

    def __init__(self):
        self.n = {}

    def __call__(self, name, by=1):
        self.n[name] = self.n.get(name, 0) + by
        return self.n[name]

    def seen(self, name):
        return self.n.get(name, 0)


class Own:

    def __init__(self, eng, sem, steps):
        self.eng, self.sem, self.steps, self.n, self.last = eng, sem, steps, Tally(), None

    def __call__(self, ins, name=None, value=None):
        name = name or self.steps
        ins.then_inc(self.sem(name), 1)
        self.last = name, value or self.n(name)
        return self.last[1]

    def settle(self):
        self.eng.wait_ge(self.sem(self.last[0]), self.last[1])


def plan(t):
    chunks, groups = [], {}

    def group(name, w, cols, tiles, start=0):
        _, ids = groups.setdefault(name, (len(groups), []))
        for k in range(start, tiles, CK):
            nk = min(CK, tiles - k)
            rows = w[k * P:(k + nk) * P, :]
            parts, at = [], 0
            for lo, n in cols:
                parts.append((at, n, rows[:, lo:lo + n].rearrange("(k p) f -> p k f", p=P)))
                at += n
            ids.append(len(chunks))
            chunks.append((nk, parts))

    w = t["w_in"][0]
    for n in range(6):
        group(("in", n), w, [(n * GF, GF)], KD)
    for start in (0, CK):
        for n in range(2):
            group(("out", n), t["w_out"][0], [(n * GF, GF)], start + CK, start)
    for n in range(8):
        group(("up", n), t["w_up"][0], [(n * GF, GF)], KD)
    for n in range(2):
        group(("down", n), t["w_down"][0], [(n * GF, GF)], 32)
    for l in range(LAYERS):
        w = t["w_in_2"][l]
        for n in (3, 4, 0, 1, 2, 5, 6, 7, 8):
            group((l, "in", n), w, [(n * GF, GF)], KD)
        for branch, w_o in (("conv", t["w_conv_o_2"][l]), ("attn", t["w_attn_o_2"][l])):
            for n in range(2):
                group((l, branch, n), w_o, [(n * GF, GF)], GT)
        for start in (0, CK):
            for n in range(2):
                group((l, "out", n), t["w_out_2"][l], [(n * GF, GF)], start + CK, start)
        for n in range(11):
            group((l, "ffn", n), t["w_ffn_in_2"][l], [(n * 256, 256), (2816 + n * 256, 256)], KD)
        for n in range(2):
            group((l, "down", n), t["w_ffn_out_2"][l], [(n * GF, GF)], 22)
    return chunks, groups


def two_blocks(nc, t, consts, out):
    chunks, groups = plan(t)
    NCH = len(chunks)

    first = {name: ids[0] for name, (_, ids) in groups.items()}
    pieces = LAYERS * ADA_GROUPS * ADA_P
    stages = [(range(groups[("out", 0)][1][1], first[(0, "in", 3)]), 9, lambda c: 1.0 if c < first[("down", 0)] else 1.15)]
    for l, after_mix, after_ffn in ((0, 1, 11), (1, 1, 2)):
        stages.append((range(first[(l, "attn", 0)], first[(l, "ffn", 0)]), after_mix, lambda c: 1.0))
        stages.append((range(first[(l, "ffn", 0)], first[(1, "in", 3)] if l == 0 else first[(1, "down", 0)]), after_ffn,
                       lambda c: 1.0 if c < first[(0, "down", 0)] else 0.9))
    ada_pos, ada_at = [], {}
    for window, count, share in stages:
        until = np.cumsum([share(c) for c in window[:-2]])
        for j in range(count * ADA_P):
            ada_pos.append(window[int(np.searchsorted(until, (j + 0.5) / (count * ADA_P) * until[-1]))])
            if j % ADA_P == ADA_P - 1:
                ada_at[ada_pos[-1] + 1] = divmod(len(ada_pos) // ADA_P - 1, ADA_GROUPS)

    by_pool = set(range(first[("out", 0)] + 1, first[("up", 0)] + 1))
    for l in range(LAYERS):
        by_pool |= set(range(first[(l, "in", 1)], first[(l, "ffn", 0)]))
    by_pool |= set(range(first[(0, "ffn", 0)] + 1, first[(1, "in", 3)], 3))
    low_done, made = [], {"lo_done_v": 0, "lo_done_p": 0}
    for c in range(NCH):
        name = "lo_done_p" if c in by_pool else "lo_done_v"
        made[name] += 1
        low_done.append((name, made[name]))

    pack, srcs = {}, [
        ("g_mix_pre", t["g_mix_pre"][0], KD), ("g_mlstm", t["g_mlstm_out"][0], MH), ("g_mix_post", t["g_mix_post"][0], KD),
        ("g_mlp_pre", t["g_mlp_pre"][0], KD), ("g_mlp_post", t["g_mlp_post"][0], KD), ("c", t["c_2"][0], KD),
        ("final", t["final_g_2"], KD)]
    for l in range(LAYERS):
        srcs += [(("norm1", l), t["norm1_g_2"][l], KD), (("norm2", l), t["norm2_g_2"][l], KD), (("subln", l), t["subln_g_2"][l], 1),
                 (("convb", l), t["dw_conv_b_2"][l], GT), (("lng", l), t["conv_ln_g_2"][l], GT), (("lnb", l), t["conv_ln_b_2"][l], GT)]
    NROW = 0
    for name, ap, tiles in srcs:
        pack[name] = (NROW, ap, tiles)
        NROW += tiles
    NMOD = LAYERS * MODS

    landed, count = [], [0] * RING
    for c, (nk, parts) in enumerate(chunks):
        count[c % RING] += 16 * len(parts)
        landed.append(count[c % RING])

    with ExitStack() as ctx:
        def sb(name, shape, dt=F32, on=ctx):
            return on.enter_context(nc.sbuf_tensor(name, shape, dt))

        def ps(name, shape):
            return ctx.enter_context(nc.psum_tensor(name, shape, F32))

        sems = {}

        def sem(name):
            if name not in sems:
                sems[name] = nc.alloc_semaphore(name)
            return sems[name]

        mm = ps("mm", [P, 4, GF])
        pa = ps("pa", [P, GF])
        pv = [ps(f"pv{i}", [P, GF]) for i in range(3)]

        raw = sb("raw", [P, RING, CK, GF])
        hi = sb("hi", [P, RING, CK, GF], F32R)
        lo = sb("lo", [P, RING, CK, GF], F32R)
        ada_raw = sb("ada_raw", [P, ADA_RING, ADA_K, GF])
        ada_acc = sb("ada_acc", [P, 2, GF])
        cst = sb("cst", [P, C_ALL])
        x = sb("x", [P, KD, S])
        act_hi = sb("act_hi", [P, KD, S], F32R)
        act_lo = sb("act_lo", [P, KD, S], F32R)
        hf = sb("hf", [P, 4, S])
        sq = sb("sq", [P, KD, S])
        rstd = sb("rstd", [P, 2, S])
        tabs = sb("tabs", [P, 2, 2 * S])
        parT = sb("parT", [P, NROW])
        adabT = sb("adabT", [P, NMOD])
        modT = sb("modT", [P, NMOD])
        convw = sb("convw", [P, LAYERS * GT, TAPS])
        ca = sb("ca", [P, 2, KD])
        cols = sb("cols", [P, 40])
        small = sb("small", [P, 24])
        nlam = sb("nlam", [P, LAYERS])

        mixA = ExitStack()
        qk1 = sb("qk1", [P, KD, S], on=mixA)
        v1 = sb("v1", [P, TT, GF], on=mixA)
        early = ExitStack()
        xin = sb("xin", [P, TT, D], on=early)
        early.close()
        mqk = sb("mqk", [P, 4, S], on=mixA)
        mv = sb("mv", [P, TT, GF], on=mixA)
        mo = sb("mo", [P, 4, S], on=mixA)
        wg = sb("wg", [P, KD, 8], on=mixA)
        att = ExitStack()
        att_hi = sb("att_hi", [P, 4, S], F32R, on=att)
        att_lo = sb("att_lo", [P, 4, S], F32R, on=att)
        att.close()
        hng = sb("hng", [P, KD, S], on=mixA)
        gbias = sb("gbias", [4, 2], on=mixA)
        gate = sb("gate", [4, 8, S], on=mixA)
        acol = sb("acol", [P, TT, 4], on=mixA)
        start = ExitStack()
        rows = sb("rows", [P, P], on=start)
        adab = sb("adab", [P, P], on=start)
        cwr = sb("cwr", [P, LAYERS, GF], on=start)
        posi = sb("posi", [1, 2 * S], I32, on=start)
        posf = sb("posf", [1, 2 * S], on=start)
        start.close()
        sA = sb("sA", [P, 2, 3 * P], on=mixA)
        pA = sb("pA", [P, 2, 3 * P], on=mixA)
        ptA = sb("ptA", [P, 2, 3 * P], on=mixA)
        bcA = sb("bcA", [P, 2, 2 * S], on=mixA)
        emA = sb("emA", [P, 2, S], on=mixA)
        hmA = sb("hmA", [P, 2, S], on=mixA)
        lamr = sb("lamr", [1, LAYERS * 2, 2, QK], on=mixA)
        lamp = sb("lamp", [1, LAYERS * 2, QK], on=mixA)
        lams = sb("lams", [1, 16], on=mixA)
        mixA.close()
        mixB = ExitStack()
        qk2 = sb("qk2", [P, KD, S], on=mixB)
        v2 = sb("v2", [P, TT, GF], on=mixB)
        gates = sb("gates", [P, 16, S], on=mixB)
        cu = sb("cu", [P, GT, S + TAPS - 1], on=mixB)
        cacc = sb("cacc", [P, GT, S], on=mixB)
        csq = sb("csq", [P, GT, S], on=mixB)
        o_hi = sb("o_hi", [P, GT, S], F32R, on=mixB)
        o_lo = sb("o_lo", [P, GT, S], F32R, on=mixB)
        uc_hi = sb("uc_hi", [P, GT, S], F32R, on=mixB)
        uc_lo = sb("uc_lo", [P, GT, S], F32R, on=mixB)
        sB = sb("sB", [P, 2, 3 * P], on=mixB)
        pB = sb("pB", [P, 2, 3 * P], on=mixB)
        ptB = sb("ptB", [P, 3 * P], on=mixB)
        oB = sb("oB", [P, S], on=mixB)
        mixB.close()
        last = ExitStack()
        outf = sb("outf", [P, KD, S], on=last)
        outt = sb("outt", [P, TT, D], on=last)
        last.close()
        u_hi = sb("u_hi", [P, 32, S], F32R)
        u_lo = sb("u_lo", [P, 32, S], F32R)

        ident = cst[:, C_ID:C_ID + P]
        rot = cst[:, C_ROT:C_ROT + P]
        ones = cst[:, C_ONE:C_ONE + P]

        def pcols(name):
            at, _, tiles = pack[name]
            return parT[:, at:at + tiles]

        def banks(name):
            g = groups[name][0]
            return mm[:, 2 * (g % 2):2 * (g % 2) + 2, :]

        def tile_of(src, f):
            return src[:, f // 2, (f % 2) * S:(f % 2) * S + S]

        def freed(name):
            g = groups[name][0]
            return f"group_free{g % 2}", g // 2 + 1

        fill_at = {0: 0, 2: 1}
        ahead_of_norm = [("out", 1), ("down", 1)] + [(l, stage, 1) for l in range(LAYERS) for stage in ("out", "down")]

        todoA = [(("in", 2), 1)] + [(("in", g), j) for g in (3, 4, 5) for j in range(2)]

        def todoB(l):
            return [((l, "in", g), j) for g in (5, 6, 7, 8) for j in range(2)]

        def out_chunks(l):
            return sorted(groups[(l, "out", 0)][1] + groups[(l, "out", 1)][1])

        block = ctx.enter_context(nc.Block())

        @block.sync
        def _(sp):
            sp.dma_start(cst[:, C_ID:C_ID + P], consts[:, C_ID:C_ID + P]).then_inc(sem("identity_loaded"), 16)
            for half in range(2):
                f = slice(half * D // 2, (half + 1) * D // 2)
                for tt in range(TT):
                    sp.dma_start(xin[:, tt, f], t["x"][0, tt * P:tt * P + P, f]).then_inc(sem(f"x_loaded{half}"), 16)
            sp.dma_start(cst[:, P:], consts[:, P:]).then_inc(sem("const_loaded"), 16)
            sp.dma_start(posi[0:1, 0:S], t["positions"]).then_inc(sem("pos_loaded"), 16)
            sp.dma_start(posi[0:1, S:2 * S], t["positions_2"]).then_inc(sem("pos_loaded"), 16)
            j = 0
            for c, (nk, parts) in enumerate(chunks):
                while j < pieces and ada_pos[j] + 3 == c:
                    i, k = j // ADA_P, j % ADA_P * ADA_K
                    if j >= ADA_RING:
                        sp.wait_ge(sem("ada_used"), j - ADA_RING + 1)
                    src = t["ada_w_2"][i // ADA_GROUPS, k * P:(k + ADA_K) * P, i % ADA_GROUPS * GF:(i % ADA_GROUPS + 1) * GF]
                    sp.dma_start(ada_raw[:, j % ADA_RING], src.rearrange("(k p) f -> p k f", p=P)).then_inc(sem(f"ada_loaded{j % ADA_RING}"), 16)
                    j += 1
                if c >= RING:
                    name, value = low_done[c - RING]
                    sp.wait_ge(sem(name), value)
                for at, w, src in parts:
                    sp.dma_start(raw[:, c % RING, 0:nk, at:at + w], src).then_inc(sem(f"raw_loaded{c % RING}"), 16)
            for i in range(4):
                sp.wait_ge(sem("out_ready"), i + 1)
                kh, tt = i // TT, i % TT
                f = slice(kh * GF, kh * GF + GF)
                sp.dma_start(out[0, tt * P:tt * P + P, f], outt[:, tt, f]).then_inc(sem("stored"), 16)
            sp.wait_ge(sem("stored"), 64)

        @block.tensor
        def _(pe):
            n = Tally()

            def bank(i):
                used = n.seen(f"bank{i}")
                n(f"bank{i}")
                if used:
                    pe.wait_ge(sem(f"bank{i}_free"), used)
                return pa if i == "a" else pv[i]

            def full(ins, i):
                ins.then_inc(sem(f"bank{i}_full"), 1)

            def wait(name, by=1):
                pe.wait_ge(sem(name), n(name, by))

            def tile_products(b0, slot, kk, k, tiles, a_hi, a_lo, ends):
                w_hi, w_lo = hi[:, slot], lo[:, slot]
                for f in tiles:
                    o = mm[:, b0 + f // 2, (f % 2) * S:(f % 2) * S + S]
                    fs = slice(f * P, f * P + P)
                    for i, (w, a) in enumerate(((w_hi, a_hi), (w_hi, a_lo), (w_lo, a_hi))):
                        ins = pe.matmul(o, w[:, kk, fs], a[:, k, :], start=(k == 0 and i == 0 and f % 2 == 0),
                                        stop=(ends and i == 2), skip_group_check=True)
                return ins

            def chunk(name, j, a_hi, a_lo, token_major=False, ready=None, per=1):
                g, ids = groups[name]
                c = ids[j]
                nk = chunks[c][0]
                if j == 0 and g >= 2:
                    pe.wait_ge(sem(f"group_free{g % 2}"), g // 2)
                pe.wait_ge(sem(low_done[c][0]), low_done[c][1])
                w_hi, w_lo = hi[:, c % RING], lo[:, c % RING]
                b0 = 2 * (g % 2)
                for kk in range(nk):
                    k = CK * j + kk
                    if ready and k % per == 0:
                        wait(ready)
                    ends = j == len(ids) - 1 and kk == nk - 1
                    if token_major:
                        for tt in range(TT):
                            tok = slice(tt * P, tt * P + P)
                            for i, (a, w) in enumerate(((a_hi, w_hi), (a_lo, w_hi), (a_hi, w_lo))):
                                ins = pe.matmul(mm[:, b0 + tt, :], a[:, k, tok], w[:, kk, :], start=(k == 0 and i == 0),
                                                stop=(ends and i == 2), skip_group_check=True)
                    elif not (name in ahead_of_norm and j == len(ids) - 1):
                        ins = tile_products(b0, c % RING, kk, k, range(GT), a_hi, a_lo, ends)
                if name in ahead_of_norm and j == len(ids) - 1:
                    for pair in range(2):
                        for kk in range(nk):
                            ins = tile_products(b0, c % RING, kk, CK * j + kk, (2 * pair, 2 * pair + 1), a_hi, a_lo, kk == nk - 1)
                        if pair == 0:
                            ins.then_inc(sem("half_done"), 1)
                ins.then_inc(sem("mm_done"), 1)
                if c in ada_at:
                    l, q = ada_at[c]
                    i = l * ADA_GROUPS + q
                    pe.wait_ge(sem("ada_used"), (i + 1) * ADA_P)
                    full(pe.matmul(bank(2)[:], ones, ada_acc[:, i % 2, :], start=True, stop=True), 2)

            def product(name, a_hi, a_lo, **kw):
                for j in range(len(groups[name][1])):
                    chunk(name, j, a_hi, a_lo, **kw)

            def sum_squares():
                bank("a")
                for pair in range(KD // 2):
                    wait("sq_ready")
                    for k in (2 * pair, 2 * pair + 1):
                        ins = pe.matmul(pa[:, 0:S], ones, sq[:, k, :], start=(k == 0), stop=(k == KD - 1))
                full(ins, "a")

            def rope(qk, names="qk"):
                for name in names:
                    for j in range(2):
                        i = 2 * j
                        k = (0 if name == "q" else 4) + 2 * j
                        full(pe.matmul(bank(i)[:], rot, qk[:, k:k + 2, :], start=True, stop=True), i)

            def scores(qk, u):
                b = bank(0)
                r = slice(QK * (u % 2), QK * (u % 2) + QK)
                q, k = qk[r, u // 2, :], qk[r, 4 + u // 2, :]
                pe.matmul(b[:, 0:P], q[:, 0:P], k[:, 0:P], start=True, stop=True)
                full(pe.matmul(b[:, P:3 * P], q[:, P:S], k, start=True, stop=True), 0)

            turned = []

            def turn(p):
                wait("probs_ready")
                b = bank(1)
                turned.append(n.seen("bank1"))
                for i in range(3):
                    ins = pe.transpose(b[:, i * P:(i + 1) * P], p[:, i * P:(i + 1) * P], ident)
                full(ins, 1)

            def apply_v(pt, v, f0, width, r0, last):
                pe.wait_ge(sem("bank1_free"), turned.pop(0))
                b = bank(2) if r0 == 0 else pv[2]
                o = b[r0:r0 + width, :]
                pe.matmul(o[:, 0:S], v[:, 0, f0:f0 + width], pt[:, 0:S], start=True, stop=False, skip_group_check=True)
                ins = pe.matmul(o[:, P:S], v[:, 1, f0:f0 + width], pt[:, S:3 * P], start=False, stop=True, skip_group_check=True)
                if last:
                    full(ins, 2)

            def head_squares():
                wait("hsq_ready")
                full(pe.matmul(bank("a")[:, 0:S], ones, sq[:, 0, :], start=True, stop=True), "a")

            pe.wait_ge(sem("identity_loaded"), 16)
            for j in range(4):
                if j % 2 == 0:
                    pe.wait_ge(sem(f"x_loaded{j // 2}"), 16 * TT)
                i = 2 * (j % 2)
                b = bank(i)
                for a, k in enumerate((2 * j, 2 * j + 1)):
                    for tt in range(TT):
                        ins = pe.transpose(b[:, a * S + tt * P:a * S + tt * P + P], xin[:, tt, k * P:(k + 1) * P], ident)
                full(ins, i)
            pe.wait_ge(sem("const_loaded"), 16)
            sum_squares()
            pe.wait_ge(sem("params_loaded"), 16 * (2 + len(srcs[::2])))
            pe.wait_ge(sem("more_params_loaded"), 16 * len(srcs[1::2]))
            b = bank(0)
            pe.transpose(b[:, 0:NROW], rows[0:NROW, :], ident[0:NROW, 0:NROW])
            full(pe.transpose(b[:, P:P + NMOD], adab[0:NMOD, :], ident[0:NMOD, 0:NMOD]), 0)
            b = bank(2)
            for i in range(LAYERS * GT):
                ins = pe.transpose(b[:, 32 * i:32 * i + TAPS], cwr[0:TAPS, i // GT, (i % GT) * P:(i % GT + 1) * P], ident[0:TAPS, 0:TAPS])
            full(ins, 2)
            wait("positions_ready")
            full(pe.matmul(bank(0)[:], ones[0:1, :], posf[0:1, :], start=True, stop=True), 0)

            product(("in", 0), act_hi, act_lo, ready="act_ready")
            chunk(("in", 1), 0, act_hi, act_lo)
            pe.wait_ge(sem(freed(("in", 0))[0]), freed(("in", 0))[1])
            rope(qk1, "q")
            chunk(("in", 1), 1, act_hi, act_lo)
            pe.wait_ge(sem("gate_weights_loaded"), 48)
            b = bank(2)
            for half in range(2):
                for k in range(KD):
                    ins = pe.matmul(b[0:4, half * S:half * S + S], wg[:, k, 4 * half:4 * half + 4], hng[:, k, :],
                                    start=(k == 0 and half == 0), stop=(k == KD - 1), skip_group_check=True)
            full(ins, 2)
            pe.wait_ge(sem(freed(("in", 1))[0]), freed(("in", 1))[1])
            rope(qk1, "k")
            chunk(("in", 2), 0, act_hi, act_lo, token_major=True)
            wait("lam_ready")
            full(pe.matmul(bank(2)[:, 0:LAYERS], ones[0:1, :], lams[0:1, 8:8 + LAYERS], start=True, stop=True), 2)
            wait("rope_done", 4)
            scores(qk1, 0)
            for i in range(UNITS + 1):
                if i < len(todoA):
                    name, j = todoA[i]
                    chunk(name, j, act_hi, act_lo, token_major=name in (("in", 2), ("in", 4)))
                if i + 1 < UNITS:
                    scores(qk1, i + 1)
                if i < UNITS:
                    turn(pA[:, i % 2, :])
                u = i - 1
                if u == 0:
                    pe.wait_ge(sem(freed(("in", 2))[0]), freed(("in", 2))[1])
                if u >= 0:
                    apply_v(ptA[:, u % 2, :], v1, u * QK, QK, QK * (u % 2), u % 2 == 1)

            wait("gate_rows_ready")
            b = bank(0)
            for tt in range(TT):
                ins = pe.transpose(b[:, 4 * tt:4 * tt + 4], gate[:, 5, tt * P:tt * P + P], ident[0:4, 0:4])
            full(ins, 0)
            for g in (3, 4):
                pe.wait_ge(sem(freed(("in", g))[0]), freed(("in", g))[1])

            def m_scores(h):
                full(pe.matmul(bank(1)[:], ident[0:4, h:h + 1].to_broadcast([4, P]), gate[:, 2:4, :], start=True, stop=True), 1)
                b = bank(0)
                r = slice(QK * (h % 2), QK * (h % 2) + QK)
                q, k = mqk[r, h // 2, :], mqk[r, 2 + h // 2, :]
                pe.matmul(b[:, 0:S], k[:, 0:P], q, start=True, stop=True)
                full(pe.matmul(b[:, S:3 * P], k[:, P:S], q[:, P:S], start=True, stop=True), 0)

            def m_sums(h):
                wait("mweights_ready")
                b = bank(2)
                w = pA[:, h % 2, :]
                f = slice(h * P, (h + 1) * P)
                pe.matmul(b[:, 0:S], mv[:, 0, f], w[:, 0:S], start=True, stop=False, skip_group_check=True)
                pe.matmul(b[:, P:S], mv[:, 1, f], w[:, S:3 * P], start=False, stop=True, skip_group_check=True)
                pe.matmul(b[:, S:2 * S], ones, w[:, 0:S], start=False, stop=False, skip_group_check=True)
                full(pe.matmul(b[:, S + P:2 * S], ones, w[:, S:3 * P], start=False, stop=True, skip_group_check=True), 2)

            m_scores(0)
            for h in range(MH + 1):
                if h + 1 < MH:
                    m_scores(h + 1)
                if h < MH:
                    m_sums(h)
                if h in fill_at:
                    chunk(("out", fill_at[h]), 0, att_hi, att_lo, ready=None if h else "act_ready")
                if h:
                    head_squares()

            for half in range(2):
                chunk(("out", half), 1, act_hi, act_lo, ready=None if half else "act_ready")
            for _ in range(2):
                sum_squares()
            for g in range(8):
                product(("up", g), act_hi, act_lo, ready="act_ready" if g == 0 else None)
            product(("down", 0), u_hi, u_lo, ready="u_ready", per=4)
            product(("down", 1), u_hi, u_lo)
            for _ in range(2):
                sum_squares()

            for l in range(LAYERS):
                product((l, "in", 3), act_hi, act_lo, ready="act_ready")
                for g in (4, 0):
                    product((l, "in", g), act_hi, act_lo)
                chunk((l, "in", 1), 0, act_hi, act_lo)
                pe.wait_ge(sem(freed((l, "in", 0))[0]), freed((l, "in", 0))[1])
                rope(qk2, "q")
                chunk((l, "in", 1), 1, act_hi, act_lo)
                chunk((l, "in", 2), 0, act_hi, act_lo, token_major=True)
                pe.wait_ge(sem(freed((l, "in", 1))[0]), freed((l, "in", 1))[1])
                rope(qk2, "k")
                chunk((l, "in", 2), 1, act_hi, act_lo, token_major=True)
                wait("rope_done", 4)
                scores(qk2, 0)
                for i in range(UNITS + 2):
                    if i == CONV_END + 2:
                        wait("csq_ready")
                        b = bank("a")
                        for k in range(GT):
                            ins = pe.matmul(b[:, 0:S], ones, csq[:, k, :], start=(k == 0), stop=(k == GT - 1))
                        full(ins, "a")
                    if i < UNITS:
                        chunk(*todoB(l)[i], act_hi, act_lo)
                    else:
                        chunk((l, "conv", i - UNITS), 0, uc_hi, uc_lo, ready="uc_ready" if i == UNITS else None)
                    if i + 1 < UNITS:
                        scores(qk2, i + 1)
                    if i == CONV_END + 1:
                        wait("conv_done", GT)
                        b = bank(2)
                        for k in range(GT):
                            ins = pe.matmul(b[:, 0:S], ones, cacc[:, k, :], start=(k == 0), stop=(k == GT - 1))
                        full(ins, 2)
                    if i % 2 == 0 and i >= 2:
                        if i == 2:
                            pe.wait_ge(sem(freed((l, "in", 2))[0]), freed((l, "in", 2))[1])
                        apply_v(ptB, v2, (i // 2 - 1) * P, P, 0, True)
                    if i % 2 == 1 and i < UNITS:
                        turn(pB[:, 1, :])
                    if i % 2 == 1 and i >= 3:
                        head_squares()
                product((l, "attn", 0), o_hi, o_lo, ready="o_ready")
                product((l, "attn", 1), o_hi, o_lo)
                for j in range(2):
                    for half in range(2):
                        chunk((l, "out", half), j, act_hi, act_lo, ready=None if half else "mixed_split", per=2)
                sum_squares()
                for g in range(11):
                    product((l, "ffn", g), act_hi, act_lo, ready="act_ready" if g == 0 else None)
                product((l, "down", 0), u_hi, u_lo, ready="u_ready", per=2)
                product((l, "down", 1), u_hi, u_lo)
                sum_squares()

            for kh in range(2):
                wait("outf_ready", 4)
                for tt in range(TT):
                    i = 2 * tt
                    b = bank(i)
                    for k in range(4):
                        ins = pe.transpose(b[:, k * P:(k + 1) * P], outf[:, 4 * kh + k, tt * P:tt * P + P], ident)
                    full(ins, i)

        @block.scalar
        def _(act):
            a = Own(act, sem, "act_step")
            n = Tally()

            def wait(name, by=1):
                act.wait_ge(sem(name), n(name, by))

            def full(i):
                wait(f"bank{i}_full")
                return pa if i == "a" else pv[i]

            def split(c):
                if c >= NCH:
                    return
                act.wait_ge(sem(f"raw_loaded{c % RING}"), landed[c])
                if c >= RING:
                    act.wait_ge(sem("mm_done"), c - RING + 1)
                nk = chunks[c][0]
                a(act.activation(hi[:, c % RING, 0:nk, :], raw[:, c % RING, 0:nk, :], ACT.Copy), "hi_done")

            def steps(name):
                for c in groups[name][1]:
                    split(c + LEAD)

            def complete(name):
                act.wait_ge(sem("mm_done"), groups[name][1][-1] + 1)
                return banks(name)

            def evacuate(name, dst, func=ACT.Copy, scale=1.0):
                a(act.activation(dst, complete(name), func, scale=scale), *freed(name))

            loaded = [None]

            def log_tables():
                if loaded[0] != "log":
                    act.preload_act_table_set("natural_log_exp_and_others")
                loaded[0] = "log"

            def other(func):
                loaded[0] = None
                return func

            def rstd_from(width, eps, slot):
                log_tables()
                b = full("a")
                a(act.activation(rstd[:, slot, :], b[:, 0:S], ACT.Ln, scale=1.0 / width, bias=small[:, eps:eps + 1]), "banka_free")
                a.settle()
                a(act.activation(rstd[:, slot, :], rstd[:, slot, :], ACT.Exp, scale=-0.5), "rstd_ready")

            def squares_of_x(ready="x_ready"):
                log_tables()
                for pair in range(KD // 2):
                    wait(ready)
                    k = slice(2 * pair, 2 * pair + 2)
                    a(act.activation(sq[:, k, :], x[:, k, :], ACT.Square), "sq_ready")

            def high_of_norm(src, shift=None):
                for k in range(KD):
                    wait("hf_ready")
                    bias = shift[:, k:k + 1] if shift is not None else 0.0
                    a(act.activation(act_hi[:, k, :], src(k), ACT.Identity, bias=bias), "act_hi_ready")

            def high(src, dst, ready, done, scale=1.0):
                wait(ready)
                a(act.activation(dst, src, ACT.Copy, scale=scale), done)

            def exps(u, s, p):
                wait("max_ready")
                i = u % 2
                for q, (lo_, hi_) in enumerate(((0, P), (P, 3 * P))):
                    a(act.activation(p[:, i, lo_:hi_], s[:, i, lo_:hi_], ACT.Exp, scale=-1.0, bias=small[:, 2 + 2 * i + q:3 + 2 * i + q],
                                     accum_out=small[:, 6 + 2 * i + q:7 + 2 * i + q]), "exp_done")

            def take_turned(pt):
                a(act.activation(pt, full(1)[:, 0:3 * P], ACT.Copy), "bank1_free")

            for r, ap, tiles in list(pack.values())[::2]:
                act.dma_start(rows[r:r + tiles, :], ap.rearrange("(r p) -> r p", p=P)).then_inc(sem("params_loaded"), 16)
            act.dma_start(adab[0:NMOD, :], t["ada_b_2"].rearrange("l (r p) -> (l r) p", p=P)).then_inc(sem("params_loaded"), 16)
            act.dma_start(cwr[0:TAPS, :, :], t["dw_conv_w_2"].rearrange("l j o c -> j (l o) c")).then_inc(sem("params_loaded"), 16)

            squares_of_x("x_tiles_ready")
            split(0)
            wait("eps_ready")
            rstd_from(D, 0, 0)
            high_of_norm(lambda k: hng[:, k, :])
            split(1)
            wait("c_loaded")
            a(act.activation(ca[:, 0, :], pcols("c"), ACT.Exp, scale=-1.0), "c_exp_ready")
            wait("lam_dots_ready")
            a(act.activation(lams[0:1, 4:8], lams[0:1, 0:4], ACT.Exp), "lam_exps_ready")
            steps(("in", 0))
            evacuate(("in", 0), qk1[:, 0:4, :])
            split(groups[("in", 1)][1][0] + LEAD)
            wait("angles_ready")
            a(act.activation(tabs[:, :, :], tabs[:, :, :], other(ACT.Sin)), "tables_ready")
            split(groups[("in", 1)][1][1] + LEAD)
            evacuate(("in", 1), qk1[:, 4:8, :])
            log_tables()

            wait("gates_biased")
            a(act.activation(gate[:, 2, :], gate[:, 1, :], ACT.Abs))
            a.settle()
            a(act.activation(gate[:, 2, :], gate[:, 2, :], ACT.Exp, scale=-1.0))
            a.settle()
            a(act.activation(gate[:, 2, :], gate[:, 2, :], ACT.Ln, bias=1.0), "softplus_ready")

            split(groups[("in", 2)][1][0] + LEAD)
            exps(0, sA, pA)
            for i in range(UNITS + 1):
                if i < len(todoA):
                    name, j = todoA[i]
                    split(groups[name][1][j] + LEAD)
                if i + 1 < UNITS:
                    exps(i + 1, sA, pA)
                if i < UNITS:
                    take_turned(ptA[:, i % 2, :])
                if i < len(todoA) and j == 1:
                    if name[1] == 2:
                        evacuate(name, v1[:, :, :])
                    elif name[1] == 3:
                        evacuate(name, mqk[:, :, :])
                    elif name[1] == 4:
                        evacuate(name, mv[:, :, :])
                if i >= 2 and i % 2 == 0:
                    h = i // 2 - 1
                    high(hf[:, h % 2, :], att_hi[:, h, :], "of_ready", "act_hi_ready")

            def m_exps(h):
                a(act.activation(bcA[:, h % 2, :], full(1)[:], ACT.Copy), "bank1_free")
                wait("mexp_arg_ready")
                a(act.activation(sA[:, h % 2, :], sA[:, h % 2, :], ACT.Exp), "mexp_done")
                if h >= 2:
                    act.wait_ge(sem("hm_ready"), h - 1)
                a(act.activation(emA[:, h % 2, :], bcA[:, h % 2, S:2 * S], ACT.Exp), "mexp_done")

            def m_norm(h):
                wait("hm_ready")
                a(act.activation(sq[:, 0, :], hmA[:, h % 2, :], ACT.Square), "hsq_ready")
                rstd_from(P, 0, h % 2)
                high(hf[:, h % 2, :], act_hi[:, 4 + h, :], "of_ready", "act_hi_ready")

            m_exps(0)
            evacuate(("in", 5), mo[:, :, :], other(ACT.Tanh), 0.5)
            for h in range(MH + 1):
                if h in fill_at:
                    split(groups[("out", fill_at[h])][1][0] + LEAD)
                if h + 1 < MH:
                    m_exps(h + 1)
                if h:
                    m_norm(h - 1)

            def post_norm(stage):
                log_tables()
                src = complete((stage, 0))
                for b in range(2):
                    a(act.activation(sq[:, 2 * b:2 * b + 2, :], src[:, b, :].rearrange("p (a s) -> p a s", a=2), ACT.Square), "sq_ready")
                wait("half_done")
                src = banks((stage, 1))
                for b in range(2):
                    if b:
                        complete((stage, 1))
                    a(act.activation(sq[:, 4 + 2 * b:6 + 2 * b, :], src[:, b, :].rearrange("p (a s) -> p a s", a=2), ACT.Square), "sq_ready")
                rstd_from(D, 0, 0)

            for c in groups[("out", 0)][1][1:] + groups[("out", 1)][1][1:]:
                split(c + LEAD)
            post_norm("out")
            squares_of_x()
            rstd_from(D, 0, 1)
            high_of_norm(lambda k: hf[:, k % 4, :])
            for g in range(8):
                steps(("up", g))
                if g:
                    act.wait_ge(sem("u_ready"), g)
                a(act.activation(sq[:, 0:4, :], complete(("up", g)), ACT.Relu), *freed(("up", g)))
                a.settle()
                a(act.activation(sq[:, 4:8, :], sq[:, 0:4, :], ACT.Square))
                a.settle()
                a(act.activation(u_hi[:, 4 * g:4 * g + 4, :], sq[:, 4:8, :], ACT.Copy), "u_hi_ready")
            steps(("down", 0))
            steps(("down", 1))
            post_norm("down")

            for l in range(LAYERS):
                squares_of_x()
                rstd_from(D, 0, 1)
                high_of_norm(lambda k: hf[:, k % 4, :], shift=modT[:, l * MODS:l * MODS + KD])
                steps((l, "in", 3))
                evacuate((l, "in", 3), cu[:, :, TAPS - 1:])
                steps((l, "in", 4))
                evacuate((l, "in", 4), csq[:, :, :], other(ACT.Tanh), 0.5)
                for g in (0, 1):
                    steps((l, "in", g))
                    evacuate((l, "in", g), qk2[:, 4 * g:4 * g + 4, :])
                steps((l, "in", 2))
                evacuate((l, "in", 2), v2[:, :, :])
                exps(0, sB, pB)
                for i in range(UNITS + 2):
                    if i < UNITS:
                        name, j = todoB(l)[i]
                        split(groups[name][1][j] + LEAD)
                    else:
                        split(groups[(l, "conv", i - UNITS)][1][0] + LEAD)
                    if i + 1 < UNITS:
                        exps(i + 1, sB, pB)
                    if i == CONV_END + 1:
                        wait("centred")
                        a(act.activation(csq[:, :, :], cacc[:, :, :], ACT.Square), "csq_ready")
                    if i % 2 == 0 and i >= 2:
                        wait("o_f32_ready")
                        a(act.activation(sq[:, 0, :], oB[:], ACT.Square), "hsq_ready")
                    if i == CONV_END + 2:
                        rstd_from(GF, 1, 1)
                        for k in range(GT + 1):
                            if k < GT:
                                wait("ln_ready")
                                silu_at = a(act.activation(csq[:, k, :], cacc[:, k, :], other(ACT.Silu), bias=pcols(("lnb", l))[:, k:k + 1]), "uc_f32_ready")
                            if k:
                                act.wait_ge(sem("uc_f32_ready"), silu_at - (k < GT))
                                a(act.activation(uc_hi[:, k - 1, :], csq[:, k - 1, :], ACT.Copy), "uc_hi_ready")
                    if i % 2 == 1 and i < UNITS:
                        take_turned(ptB[:])
                    if i % 2 == 1 and i >= 3:
                        h = (i - 3) // 2
                        rstd_from(P, 1, h % 2)
                    if i < UNITS and j == 1:
                        g = name[2] - 5
                        evacuate(name, gates[:, 4 * g:4 * g + 4, :], other(ACT.Tanh), 0.5)
                        log_tables()
                    if i % 2 == 1 and i >= 3:
                        high(hf[:, h % 2, :], o_hi[:, h, :], "on_ready", "o_hi_ready")
                for half in range(2):
                    steps((l, "attn", half))
                    for pair in (2 * half, 2 * half + 1):
                        k = slice(2 * pair, 2 * pair + 2)
                        high(gates[:, k, :], act_hi[:, k, :], "mixed_ready", "mixed_hi_ready", scale=0.5)
                for c in out_chunks(l):
                    split(c + LEAD)
                squares_of_x()
                rstd_from(D, 0, 0)
                high_of_norm(lambda k: hf[:, k % 4, :], shift=modT[:, l * MODS + 3 * KD:l * MODS + 4 * KD])
                for g in range(11):
                    steps((l, "ffn", g))
                    a(act.activation(sq[:, 0:2, :], complete((l, "ffn", g))[:, 0, :], other(ACT.Silu)), "silu_gate_ready")
                    high(sq[:, 4:6, :], u_hi[:, 2 * g:2 * g + 2, :], "u_f32_ready", "u_hi_ready")
                for half in range(2):
                    steps((l, "down", half))
            squares_of_x()
            rstd_from(D, 0, 1)

        @block.gpsimd
        def _(pool):
            p = Own(pool, sem, "pool_step")

            def split(c):
                if c not in by_pool:
                    return
                pool.wait_ge(sem("hi_done"), c + 1)
                nk = chunks[c][0]
                p(pool.tensor_tensor(lo[:, c % RING, 0:nk, :], raw[:, c % RING, 0:nk, :], hi[:, c % RING, 0:nk, :].bitcast(F32),
                                     ALU.subtract), "lo_done_p")

            for r, ap, tiles in list(pack.values())[1::2]:
                pool.dma_start(rows[r:r + tiles, :], ap.rearrange("(r p) -> r p", p=P)).then_inc(sem("more_params_loaded"), 16)
            pairs = lamr[:].rearrange("o (l c) i d -> o l c i d", c=2)
            for i, name in enumerate(("lambda_q1_2", "lambda_k1_2", "lambda_q2_2", "lambda_k2_2")):
                for l in range(LAYERS):
                    pool.dma_start(pairs[0:1, l, i // 2, i % 2, :], t[name][l:l + 1, :]).then_inc(sem("lam_loaded"), 16)
            pool.dma_start(wg[:, :, :], t["w_in"][0, :, 3072:3080].rearrange("(k p) f -> p k f", p=P)).then_inc(sem("gate_weights_loaded"), 16)
            pool.dma_start(gbias[:, 0:1], t["b_igate"].rearrange("o h -> h o")).then_inc(sem("gate_weights_loaded"), 16)
            pool.dma_start(gbias[:, 1:2], t["b_fgate"].rearrange("o h -> h o")).then_inc(sem("gate_weights_loaded"), 16)
            for c in range(NCH):
                split(c)

        @block.vector
        def _(dve):
            v = Own(dve, sem, "dve_step")
            n = Tally()

            def wait(name, by=1):
                dve.wait_ge(sem(name), n(name, by))

            def full(i):
                wait(f"bank{i}_full")
                return pv[i]

            def link(ins, name=None, value=None):
                v(ins, name, value)
                v.settle()

            def split(c):
                if c >= NCH or c in by_pool:
                    return
                dve.wait_ge(sem("hi_done"), c + 1)
                nk = chunks[c][0]
                v(dve.tensor_tensor(lo[:, c % RING, 0:nk, :], raw[:, c % RING, 0:nk, :], hi[:, c % RING, 0:nk, :].bitcast(F32),
                                    ALU.subtract), "lo_done_v")

            def ada_columns(c):
                if c not in ada_at:
                    return
                l, q = ada_at[c]
                b = full(2)
                m = hf[:, 0:2, :].rearrange("p a (b c) -> p (a b) c", b=2)
                link(dve.tensor_tensor(m, b[:].rearrange("p (f j) -> p f j", f=GT), ident.unsqueeze(1).to_broadcast([P, GT, P]), ALU.mult), "bank2_free")
                link(dve.tensor_reduce(small[:, 10:14], m, AX.X, ALU.add))
                mc = slice(l * MODS + q * GT, l * MODS + q * GT + GT)
                link(dve.tensor_tensor(modT[:, mc], small[:, 10:14], adabT[:, mc], ALU.add))

            def ada_piece(j):
                i = j // ADA_P
                acc = ada_acc[:, i % 2, :]
                dve.wait_ge(sem(f"ada_loaded{j % ADA_RING}"), 16 * (j // ADA_RING + 1))
                for kk in range(ADA_K):
                    k = j % ADA_P * ADA_K + kk
                    w = ada_raw[:, j % ADA_RING, kk, :]
                    name = "ada_used" if kk == ADA_K - 1 else None
                    if k == 0:
                        link(dve.tensor_scalar(acc, w, ca[:, 1, 0:1], None, ALU.mult), name)
                    else:
                        link(dve.scalar_tensor_tensor(out=acc, in0=w, scalar=ca[:, 1, k:k + 1], in1=acc, op0=ALU.mult, op1=ALU.add), name)

            def advance(c):
                split(c + LEAD)
                ada_columns(c - 1)
                for j in range(pieces):
                    if ada_pos[j] == c:
                        ada_piece(j)

            def steps(name):
                for c in groups[name][1]:
                    advance(c)

            def complete(name):
                dve.wait_ge(sem("mm_done"), groups[name][1][-1] + 1)
                return banks(name)

            def low(src, d_hi, d_lo, hi_done, done, scale=None, shift=None):
                wait(hi_done)
                h = d_hi.bitcast(F32)
                if scale is not None:
                    ins = dve.scalar_tensor_tensor(out=d_lo, in0=src, scalar=scale, in1=h, op0=ALU.mult, op1=ALU.subtract)
                elif shift is not None:
                    ins = dve.scalar_tensor_tensor(out=d_lo, in0=src, scalar=shift, in1=h, op0=ALU.add, op1=ALU.subtract)
                else:
                    ins = dve.tensor_tensor(d_lo, src, h, ALU.subtract)
                v(ins, done)

            def normalise(gain, slot, dst, shift=None):
                wait("rstd_ready")

                def low_part(k):
                    low(dst(k), act_hi[:, k, :], act_lo[:, k, :], "act_hi_ready", "act_ready",
                        shift=shift[:, k:k + 1] if shift is not None else None)

                for k in range(KD):
                    if k >= 4:
                        v.settle()
                    v(dve.scalar_tensor_tensor(out=dst(k), in0=x[:, k, :], scalar=gain[:, k:k + 1], in1=rstd[:, slot, :],
                                               op0=ALU.mult, op1=ALU.mult), "hf_ready")
                    if k >= 2:
                        low_part(k - 2)
                low_part(KD - 2)
                low_part(KD - 1)
                v.settle()

            def conv_work(l):
                for j in range(TAPS):
                    for k in range(GT):
                        w = convw[:, GT * l + k, j:j + 1]
                        src = cu[:, k, j:j + S]
                        name = "conv_done" if j == TAPS - 1 else f"conv_step{k}"
                        if j == 0:
                            v(dve.tensor_scalar(cacc[:, k, :], src, w, pcols(("convb", l))[:, k:k + 1], ALU.mult, ALU.add), name)
                        else:
                            dve.wait_ge(sem(f"conv_step{k}"), v.n.seen(f"conv_step{k}"))
                            v(dve.scalar_tensor_tensor(out=cacc[:, k, :], in0=src, scalar=w, in1=cacc[:, k, :], op0=ALU.mult, op1=ALU.add), name)
                        yield

            def softmax_max(u, s):
                b = full(0)
                i = u % 2
                for q, (lo_, hi_) in enumerate(((0, P), (P, 3 * P))):
                    v(dve.tensor_tensor_reduce(out=s[:, i, lo_:hi_], in0=b[:, lo_:hi_], in1=cst[:, C_ADD + lo_:C_ADD + hi_], scale=-SCALE,
                                               scalar=FAR, op0=ALU.add, op1=ALU.min, accum_out=small[:, 2 + 2 * i + q:3 + 2 * i + q]),
                      "bank0_free" if q else None)
                v.settle()
                dve.sem_inc(sem("max_ready"), 1)

            def rope(qk, blk, names="qk"):
                for j in [j for j in range(4) if "qqkk"[j] in names]:
                    i = 2 * (j % 2)
                    b = full(i)
                    z = hf[:, 0:2, :]
                    k = slice(2 * j, 2 * j + 2)
                    sn = tabs[:, blk, 0:S].unsqueeze(1).to_broadcast([P, 2, S])
                    cs = tabs[:, blk, S:2 * S].unsqueeze(1).to_broadcast([P, 2, S])
                    v(dve.tensor_tensor(z, b[:].rearrange("p (a s) -> p a s", a=2), sn, ALU.mult), f"bank{i}_free")
                    link(dve.tensor_tensor(qk[:, k, :], qk[:, k, :], cs, ALU.mult))
                    link(dve.tensor_tensor(qk[:, k, :], qk[:, k, :], z, ALU.add), "rope_done")

            def reduce_angles(i, ang):
                tmp, r = hf[:, 0, :], hf[:, 1, :]
                link(dve.tensor_scalar(tmp, ang, 1.0 / (2.0 * np.pi), MAGIC, ALU.mult, ALU.add))
                link(dve.tensor_scalar(tmp, tmp, MAGIC, None, ALU.subtract))
                link(dve.scalar_tensor_tensor(out=r, in0=tmp, scalar=-TWO_PI[0], in1=ang, op0=ALU.mult, op1=ALU.add))
                link(dve.scalar_tensor_tensor(out=r, in0=tmp, scalar=-TWO_PI[1], in1=r, op0=ALU.mult, op1=ALU.add))
                link(dve.scalar_tensor_tensor(out=r, in0=tmp, scalar=-TWO_PI[2], in1=r, op0=ALU.mult, op1=ALU.add))
                link(dve.tensor_scalar(tabs[:, i, 0:S], r, BEFORE_PI, -BEFORE_PI, ALU.min, ALU.max))
                link(dve.scalar_tensor_tensor(out=r, in0=tabs[:, i, 0:S], scalar=-1.0, in1=tabs[:, i, 0:S], op0=ALU.mult, op1=ALU.max))
                link(dve.tensor_scalar(tabs[:, i, S:2 * S], r, -1.0, PI / 2, ALU.mult, ALU.add), "angles_ready" if i else None)

            v(dve.memset(small[:, 0:1], EPS))
            v(dve.memset(small[:, 1:2], EPS_SUB), "eps_ready")
            for j in range(4):
                i = 2 * (j % 2)
                b = full(i)
                v(dve.tensor_copy(x[:, 2 * j:2 * j + 2, :], b[:].rearrange("p (a s) -> p a s", a=2)), f"bank{i}_free")
                v.settle()
                dve.sem_inc(sem("x_tiles_ready"), 1)
            wait("pos_loaded", 32)
            v(dve.tensor_copy(posf[0:1, :], posi[0:1, :]), "positions_ready")
            b = full(0)
            v(dve.tensor_copy(parT[:], b[:, 0:NROW]))
            link(dve.tensor_copy(adabT[:], b[:, P:P + NMOD]), "bank0_free")
            dve.sem_inc(sem("c_loaded"), 1)
            v(dve.tensor_scalar(convw[:], full(2)[:, 0:32 * LAYERS * GT].rearrange("p (i j) -> p i j", j=32)[:, :, 0:TAPS], 0.5, None, ALU.mult), "bank2_free")
            split(0)
            normalise(pcols("g_mix_pre"), 0, lambda k: hng[:, k, :])
            split(1)
            wait("c_exp_ready")
            link(dve.tensor_scalar(ca[:, 0, :], ca[:, 0, :], 1.0, None, ALU.add))
            link(dve.reciprocal(ca[:, 0, :], ca[:, 0, :]))
            link(dve.tensor_tensor(ca[:, 1, :], ca[:, 0, :], pcols("c"), ALU.mult), "c_ready")
            wait("lam_loaded", 16 * 4 * LAYERS)
            link(dve.tensor_tensor(lamp[0:1, :, :], lamr[0:1, :, 0, :], lamr[0:1, :, 1, :], ALU.mult))
            v(dve.tensor_reduce(lams[0:1, 0:4], lamp[0:1, :, :], AX.X, ALU.add), "lam_dots_ready")
            v(dve.tensor_scalar(cols[:, 32:36], pcols("g_mlstm"), 0.5, None, ALU.mult))
            for l in range(LAYERS):
                v(dve.tensor_scalar(cols[:, 36 + l:37 + l], pcols(("subln", l)), 1.0 - LAMBDA_INIT[l], None, ALU.mult))
            steps(("in", 0))
            wait("lam_exps_ready")
            e = lams[0:1, 4:8].rearrange("o (l c) -> o l c", c=2)
            link(dve.tensor_tensor(lams[0:1, 8:10], e[:, :, 1], e[:, :, 0], ALU.subtract))
            link(dve.tensor_scalar(lams[0:1, 8:9], lams[0:1, 8:9], -LAMBDA_INIT[0], None, ALU.add))
            v(dve.tensor_scalar(lams[0:1, 9:10], lams[0:1, 9:10], -LAMBDA_INIT[1], None, ALU.add), "lam_ready")
            b = full(0)
            dve.wait_ge(sem("const_loaded"), 16)
            link(dve.tensor_scalar(hf[:, 2:4, :], b[:].rearrange("p (a s) -> p a s", a=2), cst[:, C_FREQ:C_FREQ + 1], None, ALU.mult), "bank0_free")
            reduce_angles(0, hf[:, 2, :])
            reduce_angles(1, hf[:, 3, :])
            advance(groups[("in", 1)][1][0])
            wait("tables_ready")
            rope(qk1, 0, "q")
            advance(groups[("in", 1)][1][1])

            b = full(2)
            wait("gate_weights_loaded", 48)
            v(dve.tensor_scalar(gate[:, 0, :], b[0:4, 0:S], gbias[:, 0:1], None, ALU.add))
            v(dve.tensor_scalar(gate[:, 1, :], b[0:4, S:2 * S], gbias[:, 1:2], None, ALU.add), "bank2_free")
            v.settle()
            dve.sem_inc(sem("gates_biased"), 1)
            link(dve.memset(gate[:, 7, :], 0.0))
            rope(qk1, 0, "k")
            advance(groups[("in", 2)][1][0])
            link(dve.tensor_copy(nlam[:], full(2)[:, 0:LAYERS]), "bank2_free")

            def gate_rows():
                wait("softplus_ready")
                link(dve.scalar_tensor_tensor(out=gate[:, 3, :], in0=gate[:, 1, :], scalar=0.0, in1=gate[:, 2, :], op0=ALU.min, op1=ALU.subtract))
                link(dve.tensor_tensor_scan(gate[:, 4, :], gate[:, 3, :], gate[:, 7, :], 0.0, ALU.add, ALU.add))
                link(dve.tensor_tensor(gate[:, 5, :], gate[:, 0, :], gate[:, 4, :], ALU.subtract))
                link(dve.tensor_tensor_scan(gate[:, 6, :], gate[:, 5, :], gate[:, 5, :], 0.0, ALU.max, ALU.max))
                link(dve.tensor_scalar(gate[:, 2, :], gate[:, 6, :], -1.0, None, ALU.mult))
                link(dve.tensor_tensor(gate[:, 3, :], gate[:, 2, :], gate[:, 4, :], ALU.subtract), "gate_rows_ready")

            def probs(u, p):
                i = u % 2
                wait("exp_done", 2)
                r = small[:, 14 + 2 * i:16 + 2 * i]
                link(dve.reciprocal(r, small[:, 6 + 2 * i:8 + 2 * i]))
                v(dve.tensor_scalar(p[:, i, 0:P], p[:, i, 0:P], r[:, 0:1], None, ALU.mult))
                v(dve.tensor_scalar(p[:, i, P:3 * P], p[:, i, P:3 * P], r[:, 1:2], None, ALU.mult), "probs_ready")

            def low_of_heads(h):
                low(hf[:, h % 2, :], att_hi[:, h, :], att_lo[:, h, :], "act_hi_ready", "act_ready")
                v.settle()

            softmax_max(0, sA)
            gate_rows()
            for i in range(UNITS + 1):
                if i < UNITS:
                    probs(i, pA)
                if i < len(todoA):
                    name, j = todoA[i]
                    advance(groups[name][1][j])
                if i + 1 < UNITS:
                    softmax_max(i + 1, sA)
                if i % 2 == 1 and i >= 3:
                    low_of_heads(i // 2 - 1)
                if i >= 2 and i % 2 == 0:
                    h = i // 2 - 1
                    v(dve.tensor_copy(hf[:, h % 2, :], full(2)[:, 0:S]), "bank2_free")
                    v.settle()
                    dve.sem_inc(sem("of_ready"), 1)
            low_of_heads(UNITS // 2 - 1)
            link(dve.tensor_copy(acol[:].rearrange("p t h -> p (t h)"), full(0)[:, 0:8]), "bank0_free")

            def m_args(h):
                dve.wait_ge(sem("bank1_free"), UNITS + h + 1)
                i = h % 2
                v(dve.tensor_scalar(sA[:, i, 0:S], bcA[:, i, 0:S], acol[:, 0, h:h + 1], 0.0, ALU.add, ALU.min))
                v(dve.tensor_scalar(sA[:, i, S:3 * P], bcA[:, i, P:S], acol[:, 1, h:h + 1], 0.0, ALU.add, ALU.min), "mexp_arg_ready")

            def m_weights(h):
                i = h % 2
                wait("mexp_done", 2)
                link(dve.tensor_tensor(sA[:, i, :], sA[:, i, :], cst[:, C_MUL:C_MUL + 3 * P], ALU.mult))
                link(dve.scalar_tensor_tensor(out=pA[:, i, :], in0=full(0)[:, 0:3 * P], scalar=SCALE, in1=sA[:, i, :],
                                              op0=ALU.mult, op1=ALU.mult), "bank0_free")
                dve.sem_inc(sem("mweights_ready"), 1)

            def m_out(h):
                i = h % 2
                b = full(2)
                d = hf[:, 2 + i, :]
                link(dve.tensor_tensor(d, b[:, S:2 * S], emA[:, i, :], ALU.max))
                link(dve.scalar_tensor_tensor(out=d, in0=b[:, S:2 * S], scalar=-1.0, in1=d, op0=ALU.mult, op1=ALU.max))
                link(dve.reciprocal(d, d))
                link(dve.tensor_tensor(hmA[:, i, :], b[:, 0:S], d, ALU.mult), "bank2_free")
                dve.sem_inc(sem("hm_ready"), 1)

            def m_final(h):
                i = h % 2
                wait("rstd_ready")
                link(dve.scalar_tensor_tensor(out=hf[:, 2 + i, :], in0=hmA[:, i, :], scalar=cols[:, 32 + h:33 + h], in1=rstd[:, i, :],
                                              op0=ALU.mult, op1=ALU.mult))
                dve.wait_ge(sem(freed(("in", 5))[0]), freed(("in", 5))[1])
                v(dve.scalar_tensor_tensor(out=hf[:, i, :], in0=mo[:, h, :], scalar=1.0, in1=hf[:, 2 + i, :], op0=ALU.add, op1=ALU.mult), "of_ready", MH + h + 1)
                low(hf[:, i, :], act_hi[:, 4 + h, :], act_lo[:, 4 + h, :], "act_hi_ready", "act_ready")
                v.settle()

            m_args(0)
            m_weights(0)
            for h in range(MH + 1):
                if h in fill_at:
                    split(groups[("out", fill_at[h])][1][0] + LEAD)
                if h + 1 < MH:
                    m_args(h + 1)
                    m_weights(h + 1)
                if h < MH:
                    m_out(h)
                if h:
                    m_final(h - 1)

            def post_norm(stage, gain):
                wait("rstd_ready")
                n("half_done")
                for pair in range(KD // 2):
                    name = (stage, pair // 2)
                    src = complete(name)
                    for a in range(2):
                        k = 2 * pair + a
                        f = k % GT
                        ins = dve.scalar_tensor_tensor(out=hf[:, f, :], in0=tile_of(src, f), scalar=gain[:, k:k + 1], in1=rstd[:, 0, :],
                                                       op0=ALU.mult, op1=ALU.mult)
                        v(ins, *(freed(name) if f == GT - 1 else ()))
                    v.settle()
                    k, f = slice(2 * pair, 2 * pair + 2), slice(2 * (pair % 2), 2 * (pair % 2) + 2)
                    link(dve.tensor_tensor(x[:, k, :], x[:, k, :], hf[:, f, :], ALU.add), "x_ready")

            for c in groups[("out", 0)][1][1:] + groups[("out", 1)][1][1:]:
                advance(c)
            post_norm("out", pcols("g_mix_post"))
            normalise(pcols("g_mlp_pre"), 1, lambda k: hf[:, k % 4, :])
            for g in range(8):
                steps(("up", g))
                k = slice(4 * g, 4 * g + 4)
                low(sq[:, 4:8, :], u_hi[:, k, :], u_lo[:, k, :], "u_hi_ready", "u_ready")
                v.settle()
            steps(("down", 0))
            steps(("down", 1))
            post_norm("down", pcols("g_mlp_post"))

            def update(name, half, gain):
                src = banks(name)
                for f in range(GT):
                    if half and f == 0:
                        wait("half_done")
                    elif f == (2 if half else 0):
                        complete(name)
                    k = GT * half + f
                    ins = dve.scalar_tensor_tensor(out=x[:, k, :], in0=tile_of(src, f), scalar=gain[:, k:k + 1], in1=x[:, k, :],
                                                   op0=ALU.mult, op1=ALU.add)
                    v(ins, *(freed(name) if f == GT - 1 else ()))
                    if f % 2:
                        v.settle()
                        dve.sem_inc(sem("x_ready"), 1)

            for l in range(LAYERS):
                mod = [modT[:, l * MODS + i * KD:l * MODS + (i + 1) * KD] for i in range(6)]
                gain1, gate1, gain2, gate2 = (cols[:, 8 * i:8 * i + 8] for i in range(4))
                v(dve.scalar_tensor_tensor(out=gain1, in0=mod[1], scalar=1.0, in1=pcols(("norm1", l)), op0=ALU.add, op1=ALU.mult))
                link(dve.tensor_scalar(gate1, mod[2], 1.0, None, ALU.add))
                normalise(gain1, 1, lambda k: hf[:, k % 4, :], shift=mod[0])
                steps((l, "in", 3))
                steps((l, "in", 4))
                link(dve.memset(cu[:, :, 0:TAPS - 1], 0.0))
                name, value = freed((l, "in", 4))
                dve.wait_ge(sem(name), value)
                u = cu[:, :, TAPS - 1:]
                link(dve.scalar_tensor_tensor(out=u, in0=csq[:], scalar=1.0, in1=u, op0=ALU.add, op1=ALU.mult))
                conv = conv_work(l)

                def taps(count):
                    for _ in range(count):
                        next(conv, None)

                for c, before, name, after in zip(sum((groups[(l, "in", g)][1] for g in range(3)), []), TAPS_BEFORE, ROPE_AT, TAPS_AFTER):
                    split(c + LEAD)
                    taps(before)
                    if name:
                        rope(qk2, 1, name)
                    taps(after)
                softmax_max(0, sB)

                def low_of_head(h):
                    low(hf[:, h % 2, :], o_hi[:, h, :], o_lo[:, h, :], "o_hi_ready", "o_ready")
                    v.settle()

                def gate_branch(branch, half):
                    at = (8 if branch == "conv" else 0) + 4 * half
                    g = gates[:, at:at + 4, :]
                    link(dve.scalar_tensor_tensor(out=g, in0=g, scalar=1.0, in1=complete((l, branch, half)).rearrange("p b (a s) -> p (b a) s", a=2),
                                                  op0=ALU.add, op1=ALU.mult), *freed((l, branch, half)))

                for i in range(UNITS + 2):
                    if i < UNITS:
                        c = i % 2
                        wait("exp_done", 2)
                        r = small[:, 14 + 2 * c:16 + 2 * c]
                        link(dve.reciprocal(r, small[:, 6 + 2 * c:8 + 2 * c]))
                        if c:
                            link(dve.tensor_scalar(r, r, nlam[:, l:l + 1], None, ALU.mult))
                        for q, (lo_, hi_) in enumerate(((0, P), (P, 3 * P))):
                            pc = pB[:, c, lo_:hi_]
                            if c == 0:
                                v(dve.tensor_scalar(pc, pc, r[:, q:q + 1], None, ALU.mult))
                            else:
                                v(dve.scalar_tensor_tensor(out=pc, in0=pc, scalar=r[:, q:q + 1], in1=pB[:, 0, lo_:hi_], op0=ALU.mult, op1=ALU.add),
                                  "probs_ready" if q else None)
                        v.settle()
                        c = groups[todoB(l)[i][0]][1][todoB(l)[i][1]]
                    else:
                        c = groups[(l, "conv", i - UNITS)][1][0]
                        advance(c)
                    if i + 1 < UNITS:
                        softmax_max(i + 1, sB)
                    if i == CONV_END + 1:
                        link(dve.tensor_scalar(hf[:, 2, :], full(2)[:, 0:S], 1.0 / GF, None, ALU.mult), "bank2_free")
                        link(dve.tensor_tensor(cacc[:], cacc[:], hf[:, 2:3, :].to_broadcast([P, GT, S]), ALU.subtract), "centred")
                    if i % 2 == 0 and i >= 2:
                        if i >= 4:
                            low_of_head(i // 2 - 2)
                        link(dve.tensor_copy(oB[:], full(2)[:, 0:S]), "bank2_free")
                        dve.sem_inc(sem("o_f32_ready"), 1)
                    if i < UNITS - 1:
                        split(c + LEAD)
                    if i <= CONV_END:
                        taps(TAPS_PER_UNIT)
                    if i == CONV_END + 2:
                        wait("rstd_ready")
                        for k in range(GT):
                            v(dve.scalar_tensor_tensor(out=cacc[:, k, :], in0=cacc[:, k, :], scalar=pcols(("lng", l))[:, k:k + 1], in1=rstd[:, 1, :],
                                                       op0=ALU.mult, op1=ALU.mult), "ln_ready")
                        for k in range(GT):
                            low(csq[:, k, :], uc_hi[:, k, :], uc_lo[:, k, :], "uc_hi_ready", "uc_ready")
                        v.settle()
                    if i == UNITS - 1:
                        split(c + LEAD)
                    if i % 2 == 1 and i >= 3:
                        h = (i - 3) // 2
                        wait("rstd_ready")
                        v(dve.scalar_tensor_tensor(out=hf[:, h % 2, :], in0=oB[:], scalar=cols[:, 36 + l:37 + l], in1=rstd[:, h % 2, :],
                                                   op0=ALU.mult, op1=ALU.mult), "on_ready")
                    if i >= UNITS:
                        gate_branch("conv", i - UNITS)
                low_of_head(ATTN_HEADS - 1)
                for half in range(2):
                    steps((l, "attn", half))
                    gate_branch("attn", half)
                    pairs = [slice(2 * pair, 2 * pair + 2) for pair in (2 * half, 2 * half + 1)]
                    for k in pairs:
                        v(dve.tensor_tensor(gates[:, k, :], gates[:, k, :], gates[:, 8 + k.start:8 + k.stop, :], ALU.add), "mixed_ready")
                    for k in pairs:
                        low(gates[:, k, :], act_hi[:, k, :], act_lo[:, k, :], "mixed_hi_ready", "mixed_split", scale=0.5)
                for c in out_chunks(l):
                    advance(c)
                for half in range(2):
                    update((l, "out", half), half, gate1)
                link(dve.scalar_tensor_tensor(out=gain2, in0=mod[4], scalar=1.0, in1=pcols(("norm2", l)), op0=ALU.add, op1=ALU.mult))
                normalise(gain2, 0, lambda k: hf[:, k % 4, :], shift=mod[3])
                for g in range(11):
                    steps((l, "ffn", g))
                    src = complete((l, "ffn", g))
                    wait("silu_gate_ready")
                    link(dve.tensor_tensor(sq[:, 4:6, :], sq[:, 0:2, :], src[:, 1, :].rearrange("p (a s) -> p a s", a=2), ALU.mult), *freed((l, "ffn", g)))
                    dve.sem_inc(sem("u_f32_ready"), 1)
                    k = slice(2 * g, 2 * g + 2)
                    low(sq[:, 4:6, :], u_hi[:, k, :], u_lo[:, k, :], "u_hi_ready", "u_ready")
                    v.settle()
                link(dve.tensor_scalar(gate2, mod[5], 1.0, None, ALU.add))
                for half in range(2):
                    steps((l, "down", half))
                    update((l, "down", half), half, gate2)
            wait("rstd_ready")
            gain = pcols("final")
            for k in range(KD):
                v(dve.scalar_tensor_tensor(out=outf[:, k, :], in0=x[:, k, :], scalar=gain[:, k:k + 1], in1=rstd[:, 1, :],
                                           op0=ALU.mult, op1=ALU.mult), "outf_ready")
            for kh in range(2):
                for tt in range(TT):
                    link(dve.tensor_copy(outt[:, tt, kh * GF:kh * GF + GF], full(2 * tt)[:]), f"bank{2 * tt}_free")
                    dve.sem_inc(sem("out_ready"), 1)


_INS = ["x", "positions", "g_mix_pre", "w_in", "b_igate", "b_fgate", "g_mlstm_out", "w_out", "g_mix_post", "g_mlp_pre",
        "w_up", "w_down", "g_mlp_post", "c_2", "positions_2", "ada_w_2", "ada_b_2", "norm1_g_2", "w_in_2",
        "lambda_q1_2", "lambda_k1_2", "lambda_q2_2", "lambda_k2_2", "subln_g_2", "w_attn_o_2", "dw_conv_w_2",
        "dw_conv_b_2", "conv_ln_g_2", "conv_ln_b_2", "w_conv_o_2", "w_out_2", "norm2_g_2", "w_ffn_in_2",
        "w_ffn_out_2", "final_g_2"]


def kernel(**inputs):
    import numpy as _np
    import concourse.bacc as _bacc
    from concourse import mybir as _mybir
    from concourse.bass_utils import run_bass_kernel_spmd as _run

    nc = _bacc.Bacc("TRN2", target_bir_lowering=False, num_devices=1)
    arrays, aps = {}, {}
    for name in _INS:
        a = _np.ascontiguousarray(inputs[name])
        arrays[f"in_{name}_dram"] = a
        aps[name] = nc.dram_tensor(f"in_{name}_dram", a.shape, _mybir.dt.from_np(a.dtype), kind="ExternalInput").ap()
    c = constants()
    arrays["constants_dram"] = c
    consts = nc.dram_tensor("constants_dram", c.shape, _mybir.dt.float32, kind="ExternalInput").ap()
    out = nc.dram_tensor("out_0_dram", (1, S, D), _mybir.dt.float32, kind="ExternalOutput").ap()
    two_blocks(nc, aps, consts, out)
    r = _run(nc, [arrays], core_ids=[0])
    return r.results[0]["out_0_dram"]
```
